# Optimizing a Trainium2 kernel written in Bass

```python
import math
import jax, jax.numpy as jnp
from jax import lax
import numpy as np

D_MODEL = 1024
BATCH = 1
SEQ = 256
DEPTH = 2
DEC_BATCH = 8
DEC_SEQ = 8
PAST_LEN = 1024
PAGE_SIZE = 128

F32 = jnp.float32
RMS_EPS = 1e-6
CONV_WIDTH = 4
SSD_HEADS = 8
SSD_HEAD_DIM = 64
SSD_INNER = SSD_HEADS * SSD_HEAD_DIM
SSD_GROUPS = 2
SSD_STATE = 64
SSD_CONV_DIM = SSD_INNER + 2 * SSD_GROUPS * SSD_STATE
SSD_CHUNK = 64
HG_HEADS = 4
HG_KEY = 128
HG_VAL = 128
HG_INNER = HG_HEADS * HG_VAL
HG_CHUNK = 16
MLA_HEADS = 8
MLA_Q_LORA = 256
MLA_KV_LORA = 256
MLA_NOPE = 64
MLA_ROPE = 32
MLA_V = 64
MLA_INNER = MLA_HEADS * MLA_V
ROPE_THETA = 10000.0
Q_BLOCK = 128
LRU_WIDTH = 512
LRU_BLOCKS = 8
LRU_BLOCK_DIM = LRU_WIDTH // LRU_BLOCKS
LRU_C = 8.0
N_BRANCH = 4
BRANCH_WIDTH = 512
IN_SIZES = (SSD_INNER, SSD_CONV_DIM, SSD_HEADS,
            HG_HEADS * HG_KEY, HG_HEADS * HG_KEY, HG_INNER, HG_INNER,
            MLA_Q_LORA, MLA_KV_LORA, MLA_ROPE,
            LRU_WIDTH, LRU_WIDTH,
            N_BRANCH * D_MODEL)
D_IN = sum(IN_SIZES)
MOE_GROUPS = 4
MOE_EXPERTS_PER_GROUP = 8
MOE_EXPERTS = MOE_GROUPS * MOE_EXPERTS_PER_GROUP
MOE_TOPK = 2
MOE_HIDDEN = 256

kernel_name = 'hybrid_ssd_hgrn2_mla_rglru_hmoe_step'

def rmsnorm(x, g):
    xf = x.astype(F32)
    y = xf * lax.rsqrt(jnp.mean(xf * xf, axis=-1, keepdims=True) + RMS_EPS)
    return (y * g.astype(F32)).astype(x.dtype)

def causal_dwconv(x, buf, w, b):
    xx = jnp.concatenate([buf.astype(x.dtype), x], axis=1)
    y = lax.conv_general_dilated(xx, w[:, None, :].astype(x.dtype), window_strides=(1,), padding='VALID',
                                 dimension_numbers=('NWC', 'WIO', 'NWC'), feature_group_count=x.shape[-1])
    return y + b.astype(x.dtype), xx[:, -(CONV_WIDTH - 1):]

def rope_angles(pos):
    half = MLA_ROPE // 2
    inv = ROPE_THETA ** (-jnp.arange(half, dtype=F32) * 2.0 / MLA_ROPE)
    ang = pos.astype(F32)[:, None] * inv[None, :]
    return jnp.cos(ang), jnp.sin(ang)

def apply_rope(x, cos, sin):
    x1, x2 = jnp.split(x.astype(F32), 2, axis=-1)
    return jnp.concatenate([x1 * cos - x2 * sin, x2 * cos + x1 * sin], axis=-1).astype(x.dtype)

def ssd_chunked(x, dt, a, bm, cm, h0):
    b, L = x.shape[:2]
    cl = SSD_CHUNK if L % SSD_CHUNK == 0 else L
    nc = L // cl
    G, R, P, N = SSD_GROUPS, SSD_HEADS // SSD_GROUPS, SSD_HEAD_DIM, SSD_STATE
    xs = x.astype(F32).reshape(b, nc, cl, G, R, P)
    dts = dt.astype(F32).reshape(b, nc, cl, G, R)
    bs = bm.astype(F32).reshape(b, nc, cl, G, N)
    cs = cm.astype(F32).reshape(b, nc, cl, G, N)
    acs = jnp.cumsum(dts * a.reshape(G, R), axis=2)
    tri = jnp.tril(jnp.ones((cl, cl), bool))[:, :, None, None]
    seg = acs[:, :, :, None] - acs[:, :, None]
    decay = jnp.exp(jnp.where(tri, seg, -jnp.inf))
    cb = jnp.einsum('bctgn,bcsgn->bctsg', cs, bs)
    y_intra = jnp.einsum('bctsg,bctsgr,bcsgr,bcsgrp->bctgrp', cb, decay, dts, xs)
    decay_end = jnp.exp(acs[:, :, -1:] - acs)
    chunk_states = jnp.einsum('bclgn,bclgr,bclgrp->bcgrpn', bs, decay_end * dts, xs)
    chunk_decay = jnp.exp(acs[:, :, -1])

    def step(h, inp):
        st, dc = inp
        return dc[..., None, None] * h + st, h

    h_last, h_prev = lax.scan(step, h0.astype(F32).reshape(b, G, R, P, N),
                              (jnp.moveaxis(chunk_states, 1, 0), jnp.moveaxis(chunk_decay, 1, 0)))
    h_prev = jnp.moveaxis(h_prev, 0, 1)
    y_inter = jnp.einsum('bctgn,bcgrpn,bctgr->bctgrp', cs, h_prev, jnp.exp(acs))
    y = (y_intra + y_inter).reshape(b, L, SSD_HEADS, P)
    return y, h_last.reshape(b, SSD_HEADS, P, N)

def hgrn2_chunked(q, k, v, logf, s0):
    b, L = q.shape[:2]
    cl = HG_CHUNK if L % HG_CHUNK == 0 else L
    nc = L // cl
    tri = jnp.tril(jnp.ones((cl, cl), bool))[:, :, None, None]

    def to_chunks(t):
        return jnp.moveaxis(t.astype(F32).reshape(b, nc, cl, *t.shape[2:]), 1, 0)

    def step(s, inp):
        qc, kc, vc, lc = inp
        bc = jnp.cumsum(lc, axis=1)
        decay = jnp.exp(jnp.where(tri, bc[:, :, None] - bc[:, None], -jnp.inf))
        att = jnp.einsum('bthk,bshk,btshk->bhts', qc, kc, decay)
        o = jnp.einsum('bhts,bshv->bthv', att, vc) + jnp.einsum('bthk,bhkv->bthv', qc * jnp.exp(bc), s)
        s = jnp.exp(bc[:, -1])[..., None] * s + jnp.einsum('bshk,bshv->bhkv', kc * jnp.exp(bc[:, -1:] - bc), vc)
        return s, o

    s_last, o = lax.scan(step, s0.astype(F32), tuple(to_chunks(t) for t in (q, k, v, logf)))
    o = jnp.moveaxis(o, 0, 1).reshape(b, L, HG_HEADS, HG_VAL)
    return o, s_last

def rglru(x, r, i, a_param, pos, h0):
    log_a = -LRU_C * r * jax.nn.softplus(-a_param.astype(F32))
    a = jnp.exp(log_a)
    mult = jnp.sqrt(-jnp.expm1(2.0 * log_a))
    mult = jnp.where((pos == 0)[None, :, None], 1.0, mult)
    u = mult * (i * x.astype(F32))
    u = u.at[:, 0].add(a[:, 0] * h0.astype(F32))
    _, h = lax.associative_scan(lambda c1, c2: (c1[0] * c2[0], c2[0] * c1[1] + c2[1]), (a, u), axis=1)
    return h, h[:, -1]

def latent_attention(q_abs, q_rope, c_kv, k_rope, q_pos, k_pos):
    b, T, H, R = q_abs.shape
    qb = Q_BLOCK if T % Q_BLOCK == 0 else T
    nb = T // qb
    scale = (MLA_NOPE + MLA_ROPE) ** -0.5
    c_kv = c_kv.astype(q_abs.dtype)
    k_rope = k_rope.astype(q_abs.dtype)

    def blocks(t):
        return jnp.moveaxis(t.reshape(b, nb, qb, *t.shape[2:]), 1, 0)

    def one(inp):
        qa, qr, qp = inp
        s = (jnp.einsum('bqhr,bkr->bhqk', qa, c_kv, preferred_element_type=F32)
             + jnp.einsum('bqhd,bkd->bhqk', qr, k_rope, preferred_element_type=F32)) * scale
        s = jnp.where(k_pos[None, :] <= qp[:, None], s, -jnp.inf)
        p = jax.nn.softmax(s, axis=-1)
        return jnp.einsum('bhqk,bkr->bqhr', p.astype(c_kv.dtype), c_kv)

    o = lax.map(one, (blocks(q_abs), blocks(q_rope), q_pos.reshape(nb, qb)))
    return jnp.moveaxis(o, 0, 1).reshape(b, T, H, R)

def token_mixers(h, pos, lp, lb, st):
    past_c, past_kr, ssm0, ssm_conv0, hg0, lru0, lru_conv0 = st
    bsz, T, _ = h.shape
    dtp = h.dtype
    splits = np.cumsum(IN_SIZES)[:-1].tolist()
    (z, xbc, dt_raw, hq, hf, hi, hg, qd, kvd, krr, lx, ly, gl) = jnp.split(h @ lp['w_in'], splits, axis=-1)

    xbc, ssm_conv1 = causal_dwconv(xbc, ssm_conv0, lp['ssd_conv_w'], lp['ssd_conv_b'])
    xbc = jax.nn.silu(xbc)
    xs, bm, cm = jnp.split(xbc, [SSD_INNER, SSD_INNER + SSD_GROUPS * SSD_STATE], axis=-1)
    xs = xs.reshape(bsz, T, SSD_HEADS, SSD_HEAD_DIM)
    dt = jax.nn.softplus(dt_raw.astype(F32) + lp['ssd_dt_bias'].astype(F32))
    a = -jnp.exp(lp['ssd_a_log'].astype(F32))
    y, ssm1 = ssd_chunked(xs, dt, a, bm.reshape(bsz, T, SSD_GROUPS, SSD_STATE),
                          cm.reshape(bsz, T, SSD_GROUPS, SSD_STATE), ssm0)
    y = y + lp['ssd_d'].astype(F32)[:, None] * xs.astype(F32)
    y_a = rmsnorm(y.reshape(bsz, T, SSD_INNER) * jax.nn.silu(z.astype(F32)), lp['ssd_norm_g']).astype(dtp)

    hf32 = hf.astype(F32)
    logf = jnp.logaddexp(jnp.log(lb), jnp.log1p(-lb) + jax.nn.log_sigmoid(hf32))
    k_in = (1.0 - lb) * jax.nn.sigmoid(-hf32)
    shp = (bsz, T, HG_HEADS, HG_KEY)
    o, hg1 = hgrn2_chunked(hq.reshape(shp), k_in.reshape(shp), hi.reshape(bsz, T, HG_HEADS, HG_VAL),
                           logf.reshape(shp), hg0)
    y_b = (rmsnorm(o, lp['hg_norm_g']) * jax.nn.silu(hg.astype(F32).reshape(bsz, T, HG_HEADS, HG_VAL)))
    y_b = y_b.reshape(bsz, T, HG_INNER).astype(dtp)

    cos, sin = rope_angles(pos)
    q = (rmsnorm(qd, lp['mla_q_norm_g']) @ lp['mla_w_uq']).reshape(bsz, T, MLA_HEADS, MLA_NOPE + MLA_ROPE)
    q_nope = q[..., :MLA_NOPE]
    q_rope = apply_rope(q[..., MLA_NOPE:], cos[:, None], sin[:, None])
    c_kv = rmsnorm(kvd, lp['mla_kv_norm_g'])
    k_rope = apply_rope(krr, cos, sin)
    w_ukv = lp['mla_w_ukv'].reshape(MLA_KV_LORA, MLA_HEADS, MLA_NOPE + MLA_V)
    q_abs = jnp.einsum('bthn,rhn->bthr', q_nope, w_ukv[..., :MLA_NOPE])
    if past_c is None:
        keys_c, keys_r = c_kv, k_rope
    else:
        keys_c = jnp.concatenate([past_c.astype(dtp), c_kv], axis=1)
        keys_r = jnp.concatenate([past_kr.astype(dtp), k_rope], axis=1)
    k_pos = jnp.arange(keys_c.shape[1])
    o_lat = latent_attention(q_abs, q_rope, keys_c, keys_r, pos, k_pos)
    y_c = jnp.einsum('bthr,rhv->bthv', o_lat, w_ukv[..., MLA_NOPE:]).reshape(bsz, T, MLA_INNER).astype(dtp)

    xl, lru_conv1 = causal_dwconv(lx, lru_conv0, lp['lru_conv_w'], lp['lru_conv_b'])
    xb = xl.reshape(bsz, T, LRU_BLOCKS, LRU_BLOCK_DIM)
    r = jax.nn.sigmoid(jnp.einsum('btnd,nde->btne', xb, lp['lru_w_r']).reshape(bsz, T, LRU_WIDTH).astype(F32)
                       + lp['lru_b_r'].astype(F32))
    ig = jax.nn.sigmoid(jnp.einsum('btnd,nde->btne', xb, lp['lru_w_i']).reshape(bsz, T, LRU_WIDTH).astype(F32)
                        + lp['lru_b_i'].astype(F32))
    hseq, lru1 = rglru(xl, r, ig, lp['lru_a'], pos, lru0)
    y_d = (hseq * jax.nn.gelu(ly.astype(F32))).astype(dtp)

    branches = jnp.stack([y_a, y_b, y_c, y_d])
    br = jnp.einsum('nbtw,nwd->nbtd', branches, lp['w_branch'])
    gates = jax.nn.sigmoid(gl.reshape(bsz, T, N_BRANCH, D_MODEL))
    merged = jnp.einsum('btnd,nbtd->btd', gates, br)
    out = merged @ lp['w_out']
    new = (c_kv, k_rope, ssm1.astype(dtp), ssm_conv1, hg1.astype(dtp), lru1.astype(dtp), lru_conv1)
    return out, new

def hier_moe(h, lp):
    bsz, T, D = h.shape
    xf = h.reshape(bsz * T, D)
    g_prob = jax.nn.softmax((xf @ lp['moe_w_grp']).astype(F32) + lp['moe_b_grp'].astype(F32), axis=-1)
    g_top, g_idx = lax.top_k(g_prob, 1)
    e_logits = ((xf @ lp['moe_w_rt']).astype(F32) + lp['moe_b_rt'].astype(F32)).reshape(
        -1, MOE_GROUPS, MOE_EXPERTS_PER_GROUP)
    e_prob = jax.nn.softmax(jnp.take_along_axis(e_logits, g_idx[:, :, None], axis=1)[:, 0], axis=-1)
    e_top, e_idx = lax.top_k(e_prob, MOE_TOPK)
    weights = g_top * e_top / jnp.sum(e_top, axis=-1, keepdims=True)
    expert_id = g_idx * MOE_EXPERTS_PER_GROUP + e_idx
    combine = jnp.einsum('nk,nke->ne', weights, jax.nn.one_hot(expert_id, MOE_EXPERTS, dtype=F32)).astype(h.dtype)
    hid = jax.nn.silu(jnp.einsum('nd,edf->nef', xf, lp['moe_w_gate'])) * jnp.einsum('nd,edf->nef', xf, lp['moe_w_up'])
    out = jnp.einsum('nef,ne,efd->nd', hid, combine, lp['moe_w_down'])
    return out.reshape(bsz, T, D)

def decoder_layer(x, c, pos, lp, lb, st):
    bsz = x.shape[0]
    mod = (jax.nn.silu(c) @ lp['w_mod'] + lp['b_mod']).reshape(bsz, 6, D_MODEL)
    sh1, sc1, g1, sh2, sc2, g2 = [mod[:, j, None] for j in range(6)]
    h = rmsnorm(x, lp['norm1_g']) * (1.0 + sc1) + sh1
    y, new = token_mixers(h, pos, lp, lb, st)
    x = x + g1 * y
    h = rmsnorm(x, lp['norm2_g']) * (1.0 + sc2) + sh2
    x = x + g2 * hier_moe(h, lp)
    return x, new

def setup_inputs(seed: int = 0) -> dict:
    key = jax.random.key(seed)
    ks = iter(jax.random.split(key, 64))
    L, D = DEPTH, D_MODEL

    def nrm(shape, scale=1.0):
        return jax.random.normal(next(ks), shape, F32) * scale

    def gain(shape):
        return 1.0 + 0.05 * jax.random.normal(next(ks), shape, F32)

    n_pages = PAST_LEN // PAGE_SIZE
    n_used = DEC_BATCH * n_pages
    n_pool = n_used + max(1, n_used // 4)
    dt0 = jnp.exp(jax.random.uniform(next(ks), (L, SSD_HEADS), F32, math.log(1e-3), math.log(1e-1)))
    ssd_dt_bias = dt0 + jnp.log(-jnp.expm1(-dt0))
    ssd_a_log = jnp.log(jax.random.uniform(next(ks), (L, SSD_HEADS), F32, 1.0, 16.0))
    u = jax.random.uniform(next(ks), (L, LRU_WIDTH), F32, 0.9, 0.999) ** (1.0 / LRU_C)
    lru_a = jnp.log(u) - jnp.log1p(-u)
    page_table = jax.random.permutation(next(ks), n_pool)[:n_used].reshape(DEC_BATCH, n_pages).astype(jnp.int32)
    return {
        'x_prompt': nrm((BATCH, SEQ, D)),
        'x_sample': nrm((DEC_BATCH, DEC_SEQ, D)),
        'c_prompt': nrm((BATCH, D)),
        'c_sample': nrm((DEC_BATCH, D)),
        'cache_kv_latent': nrm((L, n_pool, PAGE_SIZE, MLA_KV_LORA)),
        'cache_k_rope': nrm((L, n_pool, PAGE_SIZE, MLA_ROPE)),
        'state_ssm': nrm((L, DEC_BATCH, SSD_HEADS, SSD_HEAD_DIM, SSD_STATE), 0.1),
        'state_ssm_conv': nrm((L, DEC_BATCH, CONV_WIDTH - 1, SSD_CONV_DIM)),
        'state_hgrn': nrm((L, DEC_BATCH, HG_HEADS, HG_KEY, HG_VAL), 0.1),
        'state_lru': nrm((L, DEC_BATCH, LRU_WIDTH), 0.5),
        'state_lru_conv': nrm((L, DEC_BATCH, CONV_WIDTH - 1, LRU_WIDTH)),
        'page_table': page_table,
        'norm1_g': gain((L, D)),
        'norm2_g': gain((L, D)),
        'w_mod': nrm((L, D, 6 * D), 0.5 * D ** -0.5),
        'b_mod': nrm((L, 6 * D), 0.02),
        'w_in': nrm((L, D, D_IN), D ** -0.5),
        'ssd_conv_w': nrm((L, CONV_WIDTH, SSD_CONV_DIM), CONV_WIDTH ** -0.5),
        'ssd_conv_b': nrm((L, SSD_CONV_DIM), 0.02),
        'ssd_dt_bias': ssd_dt_bias,
        'ssd_a_log': ssd_a_log,
        'ssd_d': gain((L, SSD_HEADS)),
        'ssd_norm_g': gain((L, SSD_INNER)),
        'hg_lb_raw': nrm((L, HG_HEADS * HG_KEY)),
        'hg_norm_g': gain((L, HG_VAL)),
        'mla_q_norm_g': gain((L, MLA_Q_LORA)),
        'mla_w_uq': nrm((L, MLA_Q_LORA, MLA_HEADS * (MLA_NOPE + MLA_ROPE)), MLA_Q_LORA ** -0.5),
        'mla_kv_norm_g': gain((L, MLA_KV_LORA)),
        'mla_w_ukv': nrm((L, MLA_KV_LORA, MLA_HEADS * (MLA_NOPE + MLA_V)), MLA_KV_LORA ** -0.5),
        'lru_conv_w': nrm((L, CONV_WIDTH, LRU_WIDTH), CONV_WIDTH ** -0.5),
        'lru_conv_b': nrm((L, LRU_WIDTH), 0.02),
        'lru_w_r': nrm((L, LRU_BLOCKS, LRU_BLOCK_DIM, LRU_BLOCK_DIM), LRU_BLOCK_DIM ** -0.5),
        'lru_b_r': nrm((L, LRU_WIDTH), 0.02),
        'lru_w_i': nrm((L, LRU_BLOCKS, LRU_BLOCK_DIM, LRU_BLOCK_DIM), LRU_BLOCK_DIM ** -0.5),
        'lru_b_i': nrm((L, LRU_WIDTH), 0.02),
        'lru_a': lru_a,
        'w_branch': nrm((L, N_BRANCH, BRANCH_WIDTH, D), BRANCH_WIDTH ** -0.5),
        'w_out': nrm((L, D, D), D ** -0.5),
        'moe_w_grp': nrm((L, D, MOE_GROUPS), D ** -0.5),
        'moe_b_grp': nrm((L, MOE_GROUPS), 0.01),
        'moe_w_rt': nrm((L, D, MOE_EXPERTS), D ** -0.5),
        'moe_b_rt': nrm((L, MOE_EXPERTS), 0.01),
        'moe_w_gate': nrm((L, MOE_EXPERTS, D, MOE_HIDDEN), D ** -0.5),
        'moe_w_up': nrm((L, MOE_EXPERTS, D, MOE_HIDDEN), D ** -0.5),
        'moe_w_down': nrm((L, MOE_EXPERTS, MOE_HIDDEN, D), MOE_HIDDEN ** -0.5),
        'final_norm_g': gain((D,)),
    }

def reference(x_prompt, x_sample, c_prompt, c_sample,
              cache_kv_latent, cache_k_rope, state_ssm, state_ssm_conv, state_hgrn, state_lru, state_lru_conv,
              page_table,
              norm1_g, norm2_g, w_mod, b_mod, w_in,
              ssd_conv_w, ssd_conv_b, ssd_dt_bias, ssd_a_log, ssd_d, ssd_norm_g,
              hg_lb_raw, hg_norm_g,
              mla_q_norm_g, mla_w_uq, mla_kv_norm_g, mla_w_ukv,
              lru_conv_w, lru_conv_b, lru_w_r, lru_b_r, lru_w_i, lru_b_i, lru_a,
              w_branch, w_out,
              moe_w_grp, moe_b_grp, moe_w_rt, moe_b_rt, moe_w_gate, moe_w_up, moe_w_down,
              final_norm_g):
    bp, tp = x_prompt.shape[:2]
    bs, ts = x_sample.shape[:2]
    n_past = page_table.shape[1] * cache_kv_latent.shape[2]
    pos_p = jnp.arange(tp)
    pos_s = n_past + jnp.arange(ts)
    lb_all = jnp.cumsum(jax.nn.softmax(hg_lb_raw.astype(F32), axis=0), axis=0)
    lb_all = lb_all - lb_all[:1]
    dtp = x_prompt.dtype
    yp, ys = x_prompt, x_sample
    p_new, s_new = [], []
    for l in range(DEPTH):
        lp = {
            'norm1_g': norm1_g[l], 'norm2_g': norm2_g[l], 'w_mod': w_mod[l], 'b_mod': b_mod[l], 'w_in': w_in[l],
            'ssd_conv_w': ssd_conv_w[l], 'ssd_conv_b': ssd_conv_b[l], 'ssd_dt_bias': ssd_dt_bias[l],
            'ssd_a_log': ssd_a_log[l], 'ssd_d': ssd_d[l], 'ssd_norm_g': ssd_norm_g[l],
            'hg_norm_g': hg_norm_g[l],
            'mla_q_norm_g': mla_q_norm_g[l], 'mla_w_uq': mla_w_uq[l],
            'mla_kv_norm_g': mla_kv_norm_g[l], 'mla_w_ukv': mla_w_ukv[l],
            'lru_conv_w': lru_conv_w[l], 'lru_conv_b': lru_conv_b[l], 'lru_w_r': lru_w_r[l], 'lru_b_r': lru_b_r[l],
            'lru_w_i': lru_w_i[l], 'lru_b_i': lru_b_i[l], 'lru_a': lru_a[l],
            'w_branch': w_branch[l], 'w_out': w_out[l],
            'moe_w_grp': moe_w_grp[l], 'moe_b_grp': moe_b_grp[l], 'moe_w_rt': moe_w_rt[l], 'moe_b_rt': moe_b_rt[l],
            'moe_w_gate': moe_w_gate[l], 'moe_w_up': moe_w_up[l], 'moe_w_down': moe_w_down[l],
        }
        p_st = (None, None,
                jnp.zeros((bp, SSD_HEADS, SSD_HEAD_DIM, SSD_STATE), dtp),
                jnp.zeros((bp, CONV_WIDTH - 1, SSD_CONV_DIM), dtp),
                jnp.zeros((bp, HG_HEADS, HG_KEY, HG_VAL), dtp),
                jnp.zeros((bp, LRU_WIDTH), dtp),
                jnp.zeros((bp, CONV_WIDTH - 1, LRU_WIDTH), dtp))
        s_st = (cache_kv_latent[l, page_table].reshape(bs, n_past, MLA_KV_LORA),
                cache_k_rope[l, page_table].reshape(bs, n_past, MLA_ROPE),
                state_ssm[l], state_ssm_conv[l], state_hgrn[l], state_lru[l], state_lru_conv[l])
        yp, pn = decoder_layer(yp, c_prompt, pos_p, lp, lb_all[l], p_st)
        ys, sn = decoder_layer(ys, c_sample, pos_s, lp, lb_all[l], s_st)
        p_new.append(pn)
        s_new.append(sn)
    yp = rmsnorm(yp, final_norm_g)
    ys = rmsnorm(ys, final_norm_g)

    def stk(news, j):
        return jnp.stack([n[j] for n in news])

    return (yp, ys,
            stk(p_new, 0), stk(p_new, 1), stk(p_new, 2), stk(p_new, 3), stk(p_new, 4), stk(p_new, 5), stk(p_new, 6),
            stk(s_new, 0), stk(s_new, 1), stk(s_new, 2), stk(s_new, 3), stk(s_new, 4), stk(s_new, 5), stk(s_new, 6))


_drawn_inputs = setup_inputs


def setup_inputs(seed=0):
    import zlib

    import numpy as np

    out = dict(_drawn_inputs(seed))
    spreads = {}
    factors = {'cache_kv_latent': 3.265,
     'cache_k_rope': 4.201,
     'ssd_d': 3.583,
     'ssd_norm_g': 3.399,
     'hg_norm_g': 4.652,
     'mla_q_norm_g': 8.0,
     'lru_b_r': 8.0,
     'lru_b_i': 7.557,
     'moe_b_grp': 29.161,
     'moe_b_rt': 24.284}
    for name, (base, spread) in spreads.items():
        noise = np.random.default_rng([zlib.crc32(name.encode()), seed]).standard_normal(out[name].shape)
        drawn = base * np.exp(spread * noise) if base else spread * noise
        out[name] = __import__('jax').numpy.asarray(drawn.astype(out[name].dtype))
    for name, factor in factors.items():
        out[name] = (out[name] * factor).astype(out[name].dtype)
    return out
```

```python
from contextlib import ExitStack

import concourse.bass as bass
import numpy as np
from concourse import mybir

ALU = mybir.AluOpType
ACT = mybir.ActivationFunctionType
AX = mybir.AxisListType
F32 = mybir.dt.float32
I32 = mybir.dt.int32

P = 128
DEPTH, D, SEQ, NB, TS = 2, 1024, 256, 8, 8
NSAMP = NB * TS
T = SEQ + NSAMP
KD = D // P
NREQ = 1 + NB
PAST, PAGE = 1024, 128
NPAGE = PAST // PAGE
EPS = 1e-6
NH, HD, NST = 8, 64, 64
HG_LEVELS = (2, 4, 8, 16, 32, 64, 128, 256)
MH, NOPE, ROPE = 8, 64, 32
ATT_SCALE = float((NOPE + ROPE) ** -0.5)
NEXP, HID = 32, 256
BIG = 1e30

Z0, XBC0, HQ0, HF0, HI0, HG0, QD0, KVD0, LX0, LY0, GL0 = 0, 4, 10, 14, 18, 22, 26, 28, 30, 34, 38
NPROJ = 70
C_N1, C_N2, C_BMOD, C_CW, C_CB, C_SSDN, C_HG0, C_HG1, C_SEL, C_HGN, C_QN, C_KVN, C_BR, C_BI, C_LA, C_DSK, C_DTB, C_ALOG = (
    0, 8, 16, 64, 104, 114, 118, 122, 126, 127, 128, 130, 132, 136, 140, 144, 148, 149)
NCOLS = 150


class Chain:

    def __init__(self, sem):
        self.sem, self.n = sem, 0

    def link(self, eng, ins):
        self.n += 1
        ins.then_inc(self.sem, 1)
        eng.wait_ge(self.sem, self.n)


class Core:
    pass


def prompt(ap):
    return ap[:, :, 0:SEQ]


def sample(ap):
    return ap[:, :, SEQ:T].rearrange("p k (b t) -> p k b t", t=TS)


def modulation_stage(K, l):
    nc, s = K.nc, K.sem
    with nc.sbuf_tensor("u_wmod", [P, 3, KD, 512], F32) as wmod, nc.Block(no_gpsimd_drain=True) as block:
        @block.sync
        def _(sp):
            for i0, i1 in ((0, 1), (1, 4)):
                with sp.Fori(i0, i1) as i:
                    for j in range(3):
                        if i0:
                            sp.wait_ge(s("mod_panel_done"), (i - 1) * 3 + j + 1)
                        sp.dma_start(wmod[:, j], K.d["w_mod"][l, bass.ds(i * 3 + j, 1)].rearrange("o p k n -> p (o k) n")
                                     ).then_inc(s(f"mod_loaded{j}"), 16)

        @block.scalar
        def _(act):
            act.dma_start(K.cols[:, :], K.d["cols"][l]).then_inc(s("cols_loaded"), 16)

        @block.tensor
        def _(pe):
            for i0, i1 in ((0, 1), (1, 4)):
                with pe.Fori(i0, i1) as i:
                    for j in range(3):
                        pe.wait_ge(s(f"mod_loaded{j}"), i * 16 + 16)
                        for m in range(4):
                            for k in range(KD):
                                mm = pe.matmul(K.ps[:, 0, bass.ds((i * 12 + j * 4 + m) * NREQ, NREQ)],
                                               wmod[:, j, k, m * P:(m + 1) * P], K.silu_c[:, k, :],
                                               start=(k == 0), stop=(k == KD - 1))
                        mm.then_inc(s("mod_panel_done"), 1)

        @block.vector
        def _(dve):
            v, link = nc.vector, lambda ins: K.vc.link(dve, ins)
            dve.wait_ge(s("cols_loaded"), 16)
            dve.wait_ge(s("mod_panel_done"), 12)
            link(v.tensor_tensor(K.mod[:, :, :], K.ps[:, 0, 0:48 * NREQ].rearrange("p (m r) -> p m r", r=NREQ),
                                 K.cols[:, C_BMOD:C_BMOD + 48].unsqueeze(2).to_broadcast([P, 48, NREQ]), ALU.add))
            for n, c in ((0, C_N1), (1, C_N2)):
                v.scalar_tensor_tensor(out=K.gain[:, n], in0=K.mod[:, 24 * n + 8:24 * n + 16, :], scalar=1.0,
                                       in1=K.cols[:, c:c + 8].unsqueeze(2).to_broadcast([P, 8, NREQ]),
                                       op0=ALU.add, op1=ALU.mult)


def sum_over_partitions(K, pe, out, tiles, start=True):
    for n, tile in enumerate(tiles):
        mm = pe.matmul(out, K.ones[:, :], tile, start=(n == 0), stop=(n == len(tiles) - 1))
    return mm


def norm_stage(K, n, tag):
    nc, s = K.nc, K.sem
    with nc.sbuf_tensor(tag + "_rstd_row", [P, T], F32) as rstd, nc.Block(no_gpsimd_drain=True) as block:
        @block.vector
        def _(dve):
            v, link = nc.vector, lambda ins: K.vc.link(dve, ins)
            v.tensor_tensor(K.h[:, :, :], K.x[:, :, :], K.x[:, :, :], ALU.mult).then_inc(s(tag + "_squares"), 1)
            dve.wait_ge(s(tag + "_sum"), 1)
            link(v.tensor_scalar(rstd[:, :], K.ps[:, 0, 0:T], 1.0 / D, EPS, ALU.mult, ALU.add))
            v.reciprocal(rstd[:, :], rstd[:, :]).then_inc(s(tag + "_inv"), 1)
            dve.wait_ge(s(tag + "_rstd"), 1)
            link(v.tensor_tensor(K.h[:, :, :], K.x[:, :, :], rstd[:, :].unsqueeze(1).to_broadcast([P, KD, T]), ALU.mult))
            if n == 2:
                v.tensor_tensor(K.h[:, :, :], K.h[:, :, :], K.fin[:, :].unsqueeze(2).to_broadcast([P, KD, T]), ALU.mult)
                return
            g, sh = K.gain[:, n], K.mod[:, 24 * n:24 * n + 8, :]
            for op, a in ((ALU.mult, g), (ALU.add, sh)):
                v.tensor_tensor(prompt(K.h), prompt(K.h), a[:, :, 0:1].to_broadcast([P, KD, SEQ]), op)
                link(v.tensor_tensor(sample(K.h), sample(K.h),
                                     a[:, :, 1:NREQ].unsqueeze(3).to_broadcast([P, KD, NB, TS]), op))

        @block.tensor
        def _(pe):
            pe.wait_ge(s(tag + "_squares"), 1)
            sum_over_partitions(K, pe, K.ps[:, 0, 0:T], [K.h[:, k, :] for k in range(KD)]).then_inc(s(tag + "_sum"), 1)

        @block.scalar
        def _(act):
            act.wait_ge(s(tag + "_inv"), 1)
            nc.scalar.activation(rstd[:, :], rstd[:, :], ACT.Sqrt).then_inc(s(tag + "_rstd"), 1)


def projection_stage(K, l):
    nc, s = K.nc, K.sem
    SL, PB = 5, 5
    with (nc.sbuf_tensor("u_win", [P, SL, KD, 256], F32) as win, nc.sbuf_tensor("u_wsmall", [P, KD, 40], F32) as wsm,
          nc.Block(no_gpsimd_drain=True) as block):
        @block.sync
        def _(sp):
            for i0, i1 in ((0, 1), (1, 7)):
                with sp.Fori(i0, i1) as i:
                    for j in range(SL):
                        if i0:
                            sp.wait_ge(s("in_evacuated"), (i - 1) * 2 * SL + 2 * j + 2)
                        sp.dma_start(win[:, j], K.d["w_in"][l, bass.ds(i * SL + j, 1)].rearrange("o p k n -> p (o k) n")
                                     ).then_inc(s(f"in_loaded{j}"), 16)

        @block.scalar
        def _(act):
            act.dma_start(wsm[:, :, :], K.d["w_small"][l]).then_inc(s("small_loaded"), 16)

        @block.tensor
        def _(pe):
            for i0, i1 in ((0, 1), (1, 7)):
                with pe.Fori(i0, i1) as i:
                    for t in range(2 * SL):
                        j, m = t // 2, t % 2
                        if m == 0:
                            pe.wait_ge(s(f"in_loaded{j}"), i * 16 + 16)
                        if i0 or t >= PB:
                            pe.wait_ge(s("in_evacuated"), i * 2 * SL + t - PB + 1)
                        for k in range(KD):
                            mm = pe.matmul(K.ps[:, t % PB, 0:T], win[:, j, k, m * P:(m + 1) * P], K.h[:, k, :],
                                           start=(k == 0), stop=(k == KD - 1))
                        mm.then_inc(s("in_tile_done"), 1)
            pe.wait_ge(s("small_loaded"), 16)
            for bank, a, b in ((5, 0, 8), (6, 8, 40)):
                for k in range(KD):
                    mm = pe.matmul(K.ps[0:b - a, bank, 0:T], wsm[:, k, a:b], K.h[:, k, :],
                                   start=(k == 0), stop=(k == KD - 1))
            mm.then_inc(s("small_done"), 1)

        @block.vector
        def _(dve):
            with dve.Fori(0, 7) as i:
                for t in range(2 * SL):
                    dve.wait_ge(s("in_tile_done"), i * 2 * SL + t + 1)
                    nc.vector.tensor_copy(K.proj[:, bass.ds(i * 2 * SL + t, 1), :], K.ps[:, t % PB:t % PB + 1, 0:T]
                                          ).then_inc(s("in_evacuated"), 1)
            dve.wait_ge(s("small_done"), 1)
            nc.vector.tensor_copy(K.dt[:, :], K.ps[0:NH, 5, 0:T])
            nc.vector.tensor_copy(K.krope[:, :], K.ps[0:ROPE, 6, 0:T])


def conv_stage(K, l):
    nc, s = K.nc, K.sem
    W3, SEG = 3, TS + 3
    XL = W3 + SEQ + NB * SEG
    YL = XL - W3
    S0 = W3 + SEQ
    with (nc.sbuf_tensor("u_xx", [P, 10, XL], F32) as xx, nc.sbuf_tensor("conv_y", [P, 10, YL + 3], F32) as y,
          nc.sbuf_tensor("u_conv_in", [P, 10, NB, W3], F32) as cin, nc.sbuf_tensor("conv_out", [P, 10, NREQ, W3], F32) as cout,
          nc.sbuf_tensor("u_dt_tmp", [NH, 4, T], F32) as dtt,
          nc.Block(no_gpsimd_drain=True) as block):
        seg = xx[:, :, S0:XL].rearrange("p c (b t) -> p c b t", t=SEG)
        segy = y[:, :, S0:YL + 3].rearrange("p c (b t) -> p c b t", t=SEG)

        @block.sync
        def _(sp):
            sp.dma_start(cin[:, :, :, :], K.d["conv_state"][l]).then_inc(s("conv_in_loaded"), 16)
            sp.wait_ge(s("conv_out_ready"), 1)
            sp.dma_start(K.d["o_conv"][l], cout[:, :, :, :]).then_inc(s("conv_stored"), 16)
            sp.wait_ge(s("conv_stored"), 16)

        @block.vector
        def _(dve):
            v, link = nc.vector, lambda ins: K.vc.link(dve, ins)
            v.memset(xx[:, :, 0:W3], 0.0)
            for c0, n, p0 in ((0, 6, XBC0), (6, 4, LX0)):
                v.tensor_copy(xx[:, c0:c0 + n, W3:S0], prompt(K.proj)[:, p0:p0 + n, :])
                for b in range(NB):
                    v.tensor_copy(xx[:, c0:c0 + n, S0 + b * SEG + W3:S0 + (b + 1) * SEG],
                                  K.proj[:, p0:p0 + n, SEQ + b * TS:SEQ + (b + 1) * TS])
            dve.wait_ge(s("conv_in_loaded"), 16)
            link(v.tensor_copy(seg[:, :, :, 0:W3], cin[:, :, :, :]))
            v.tensor_copy(cout[:, :, 0, :], xx[:, :, SEQ:S0])
            v.tensor_copy(cout[:, :, 1:NREQ, :], seg[:, :, :, TS:SEG]).then_inc(s("conv_out_ready"), 1)
            for w in range(4):
                for c in range(10):
                    tap = K.cols[:, C_CW + 4 * c + w:C_CW + 4 * c + w + 1]
                    if w == 0:
                        ins = v.tensor_scalar(y[:, c, 0:YL], xx[:, c, 0:YL], tap, K.cols[:, C_CB + c:C_CB + c + 1],
                                              ALU.mult, ALU.add)
                    else:
                        ins = v.scalar_tensor_tensor(out=y[:, c, 0:YL], in0=xx[:, c, w:w + YL], scalar=tap,
                                                     in1=y[:, c, 0:YL], op0=ALU.mult, op1=ALU.add)
                link(ins)
            v.tensor_copy(prompt(K.proj)[:, LX0:LX0 + 4, :], y[:, 6:10, 0:SEQ])
            v.tensor_copy(sample(K.proj)[:, LX0:LX0 + 4], segy[:, 6:10, :, 0:TS]).then_inc(s("conv_done"), 1)
            dve.wait_ge(s("dt_ready"), 1)
            link(v.scalar_tensor_tensor(out=K.dt[:, :], in0=dtt[:, 0, :], scalar=0.0, in1=dtt[:, 2, :],
                                        op0=ALU.max, op1=ALU.add))
            link(v.tensor_scalar(dtt[:, 3, :], K.dt[:, :], K.acol[:, 0:1], -1.0, ALU.mult, ALU.mult))
            link(v.tensor_tensor_scan(K.acs[:, :], K.keep[0:NH, :], dtt[:, 3, :], 0.0, ALU.mult, ALU.add))
            v.tensor_tensor(dtt[:, 0, 0:SEQ], K.acs[:, SEQ - 1:SEQ].to_broadcast([NH, SEQ]), K.acs[:, 0:SEQ], ALU.subtract)
            ac = K.acs[:, SEQ:T].rearrange("p (b t) -> p b t", t=TS)
            v.tensor_tensor(dtt[:, 0, SEQ:T].rearrange("p (b t) -> p b t", t=TS),
                            ac[:, :, TS - 1:TS].to_broadcast([NH, NB, TS]), ac, ALU.subtract).then_inc(s("wend_arg"), 1)
            dve.wait_ge(s("wend_exp"), 1)
            v.tensor_tensor(K.wend[:, :], dtt[:, 1, :], K.dt[:, :], ALU.mult)

        @block.scalar
        def _(act):
            a, link = nc.scalar, lambda ins: K.ac.link(act, ins)
            link(a.activation(dtt[:, 0, :], K.dt[:, :], ACT.Identity, bias=K.cols[0:NH, C_DTB:C_DTB + 1]))
            link(a.activation(dtt[:, 1, :], dtt[:, 0, :], ACT.Abs))
            link(a.activation(K.acol[:, :], K.cols[0:NH, C_ALOG:C_ALOG + 1], ACT.Exp))
            link(a.activation(dtt[:, 1, :], dtt[:, 1, :], ACT.Exp, scale=-1.0))
            a.activation(dtt[:, 2, :], dtt[:, 1, :], ACT.Ln, bias=1.0).then_inc(s("dt_ready"), 1)
            act.wait_ge(s("wend_arg"), 1)
            a.activation(dtt[:, 1, :], dtt[:, 0, :], ACT.Exp).then_inc(s("wend_exp"), 1)
            act.wait_ge(s("conv_done"), 1)
            a.activation(prompt(K.proj)[:, XBC0:XBC0 + 6, :], y[:, 0:6, 0:SEQ], ACT.Silu)
            a.activation(sample(K.proj)[:, XBC0:XBC0 + 6], segy[:, 0:6, :, 0:TS], ACT.Silu)


def ssd_stage(K, l):
    nc, s = K.nc, K.sem
    REG = ((0, P, 0, SEQ, 0), (P, P, P, P, SEQ), (SEQ, NSAMP, SEQ, NSAMP, SEQ + P))
    SC = SEQ + P + NSAMP
    with ExitStack() as e:
        sb = lambda n, sh: e.enter_context(nc.sbuf_tensor("t_" + n, sh, F32))
        xT, bT, rT = sb("ssd_xT", [P, 3, 512]), sb("ssd_bT", [P, 3, P]), sb("ssd_rT", [P, 3, 3, NH])
        xdt, xw = sb("ssd_xdt", [P, 3, 512]), sb("ssd_xw", [P, 3, 512])
        bmask = sb("ssd_bmask", [NSAMP, 2, NB, NST])
        cbm = sb("ssd_cbm", [P, 2, SC])
        E, M = sb("ssd_E", [P, 2, SC]), sb("ssd_M", [P, 2, SC])
        h0T = sb("ssd_h0T", [P, NB, 256])
        h0 = sb("ssd_h0", [P, 4, NB, NST])
        hout = sb("ssd_hout", [P, 4, NREQ, NST])
        ep = sb("ssd_ep", [P, 4, NSAMP])
        zs, yi = sb("ssd_zs", [P, 4, T]), sb("ssd_yi", [P, 4, NSAMP])
        rstd = sb("ssd_rstd", [P, T])
        block = e.enter_context(nc.Block(no_gpsimd_drain=True))
        XB, BB, CB = K.proj[:, XBC0:XBC0 + 4], K.proj[:, XBC0 + 4], K.proj[:, XBC0 + 5]

        @block.sync
        def _(sp):
            sp.dma_start(h0T[:, :, :], K.d["ssm_T"][l]).then_inc(s("h0T_loaded"), 16)
            sp.dma_start(h0[:, :, :, :], K.d["ssm_P"][l]).then_inc(s("h0_loaded"), 16)
            sp.wait_ge(s("ssm_out_ready"), 1)
            sp.dma_start(K.d["o_ssm"][l], hout[:, :, :, :]).then_inc(s("ssm_stored"), 16)
            sp.wait_ge(s("ssm_stored"), 16)

        @block.tensor
        def _(pe):
            for r, (s0, n, _, _, _) in enumerate(REG):
                for c in range(4):
                    mm = pe.transpose(K.ps[0:n, r, c * P:(c + 1) * P], XB[:, c, s0:s0 + n], K.ident[:, :])
                mm = pe.transpose(K.ps[0:n, 3, r * P:(r + 1) * P], BB[:, s0:s0 + n], K.ident[:, :])
                for q, row in enumerate((K.acs, K.dt, K.wend)):
                    mm = pe.transpose(K.ps[0:n, 4, (r * 3 + q) * NH:(r * 3 + q + 1) * NH], row[:, s0:s0 + n],
                                      K.ident[0:NH, 0:NH])
            mm.then_inc(s("ssd_tm"), 1)
            for g in range(2):
                for s0, n, t0, m, c0 in REG:
                    mm = pe.matmul(K.ps[0:n, 5 + g, c0:c0 + m], BB[64 * g:64 * g + 64, s0:s0 + n],
                                   CB[64 * g:64 * g + 64, t0:t0 + m], start=True, stop=True)
            mm.then_inc(s("ssd_cb"), 1)
            for q in range(4):
                mm = pe.matmul(K.ps[:, 7, q * NSAMP:(q + 1) * NSAMP], K.selpair[:, q, :], K.acs[:, SEQ:T],
                               start=True, stop=True)
            mm.then_inc(s("ssd_acspair"), 1)
            pe.wait_ge(s("h0T_loaded"), 16)
            pe.wait_ge(s("ssd_ep"), 1)
            pe.wait_ge(s("ssd_tm_copied"), 1)
            for q in range(4):
                g = q // 2
                for b in range(NB):
                    mm = pe.matmul(K.ps[:, 7 - 3 * g, q * NSAMP + b * TS:q * NSAMP + (b + 1) * TS],
                                   h0T[64 * g:64 * g + 64, b, (q % 2) * P:(q % 2 + 1) * P],
                                   CB[64 * g:64 * g + 64, SEQ + b * TS:SEQ + (b + 1) * TS], start=True, stop=True)
            mm.then_inc(s("ssd_inter"), 1)
            for h in range(NH):
                if h >= 2:
                    pe.wait_ge(s("ssd_seg"), h - 1)
                pe.matmul(K.ps[:, h % 2, 0:T], K.selhead[:, h, :], K.acs[:, :], start=True, stop=True
                          ).then_inc(s("ssd_acsb"), 1)
                if h >= 1:
                    ssd_y(K, pe, h - 1, REG, xdt, M)
            ssd_y(K, pe, NH - 1, REG, xdt, M)
            pe.wait_ge(s("ssd_xw"), 1)
            for q in range(4):
                g = q // 2
                for r in range(2):
                    mm = pe.matmul(K.ps[:, 4, q * NST:(q + 1) * NST], xw[:, r, q * P:(q + 1) * P],
                                   bT[:, r, 64 * g:64 * g + 64], start=(r == 0), stop=(r == 1))
            mm.then_inc(s("ssd_state_p"), 1)
            for q in range(4):
                g = q // 2
                if q >= 2:
                    pe.wait_ge(s("ssd_state_used"), q - 1)
                pe.matmul(K.ps[:, 5 + q % 2, :], xw[0:NSAMP, 2, q * P:(q + 1) * P],
                          bmask[:, g].rearrange("p b n -> p (b n)"), start=True, stop=True).then_inc(s("ssd_state"), 1)
            pe.wait_ge(s("ssd_sq"), 1)
            sum_over_partitions(K, pe, K.ps[:, 7, 0:T], [zs[:, q, :] for q in range(4)]).then_inc(s("ssd_ss"), 1)

        @block.vector
        def _(dve):
            v, link = nc.vector, lambda ins: K.vc.link(dve, ins)
            v.memset(cbm[:, :, :], 0.0)
            v.memset(E[:, :, :], 0.0)
            v.memset(xT[:, 2, :], 0.0)
            link(v.memset(rT[:, 2], 0.0))
            dve.wait_ge(s("ssd_tm"), 1)
            v.tensor_copy(xT[:, 0:2, :], K.ps[:, 0:2, :])
            v.tensor_copy(xT[0:NSAMP, 2, :], K.ps[0:NSAMP, 2, :])
            v.tensor_copy(bT[:, 0:2, :].rearrange("p r n -> p (r n)"), K.ps[:, 3, 0:2 * P])
            v.tensor_copy(bT[0:NSAMP, 2, :], K.ps[0:NSAMP, 3, 2 * P:3 * P])
            v.tensor_copy(rT[:, 0:2].rearrange("p r q h -> p (r q h)"), K.ps[:, 4, 0:6 * NH])
            link(v.tensor_copy(rT[0:NSAMP, 2].rearrange("p q h -> p (q h)"), K.ps[0:NSAMP, 4, 6 * NH:9 * NH]))
            for out, q in ((xdt, 1), (xw, 2)):
                for r in range(3):
                    ins = v.tensor_tensor(out[:, r].rearrange("p (h d) -> p h d", h=NH),
                                          xT[:, r].rearrange("p (h d) -> p h d", h=NH),
                                          rT[:, r, q, :].unsqueeze(2).to_broadcast([P, NH, HD]), ALU.mult)
                if q == 1:
                    ins.then_inc(s("ssd_tm_copied"), 1)
            for g in range(2):
                ins = v.tensor_tensor(bmask[:, g], bT[0:NSAMP, 2, 64 * g:64 * g + 64].unsqueeze(1).to_broadcast([NSAMP, NB, NST]),
                                      K.ownb[:, :].unsqueeze(2).to_broadcast([NSAMP, NB, NST]), ALU.mult)
            ins.then_inc(s("ssd_xw"), 1)
            dve.wait_ge(s("ssd_cb"), 1)
            for g in range(2):
                v.tensor_tensor(cbm[:, g, 0:SEQ + P], K.ps[:, 5 + g, 0:SEQ + P], K.causal[:, 0:SEQ + P], ALU.mult)
                link(v.tensor_tensor(cbm[0:NSAMP, g, SEQ + P:SC], K.ps[0:NSAMP, 5 + g, SEQ + P:SC],
                                     K.causal[0:NSAMP, SEQ + P:SC], ALU.mult))
            dve.wait_ge(s("ssd_inter"), 1)
            for g in range(2):
                link(v.tensor_tensor(yi[:, 2 * g:2 * g + 2, :],
                                     K.ps[:, 7 - 3 * g, 2 * g * NSAMP:2 * (g + 1) * NSAMP].rearrange("p (q t) -> p q t", q=2),
                                     ep[:, 2 * g:2 * g + 2, :], ALU.mult))

            def decayed(h):
                dve.wait_ge(s("ssd_E"), h + 1)
                if h >= 2:
                    dve.wait_ge(s("ssd_y"), h - 1)
                v.tensor_tensor(M[:, h % 2, :], E[:, h % 2, :], cbm[:, h // 4, :], ALU.mult).then_inc(s("ssd_M"), 1)

            def pair_y(q):
                dve.wait_ge(s("ssd_y"), 2 * q + 2)
                link(v.scalar_tensor_tensor(out=K.proj[:, Z0 + q, :], in0=XB[:, q, :],
                                            scalar=K.cols[:, C_DSK + q:C_DSK + q + 1], in1=K.ps[:, 2 + q % 2, 0:T],
                                            op0=ALU.mult, op1=ALU.add))
                link(v.tensor_tensor(K.proj[:, Z0 + q, SEQ:T], K.proj[:, Z0 + q, SEQ:T], yi[:, q, :], ALU.add))
                v.tensor_tensor(K.proj[:, Z0 + q, :], K.proj[:, Z0 + q, :], zs[:, q, :], ALU.mult).then_inc(s("ssd_pair"), 1)

            dve.wait_ge(s("ssd_zs"), 1)
            for h in range(NH):
                dve.wait_ge(s("ssd_acsb"), h + 1)
                if h >= 2:
                    dve.wait_ge(s("ssd_M"), h - 1)
                for r, (s0, n, t0, m, c0) in enumerate(REG):
                    ins = v.tensor_scalar(E[0:n, h % 2, c0:c0 + m], K.ps[0:n, h % 2, t0:t0 + m], rT[0:n, r, 0, h:h + 1],
                                          0.0, ALU.subtract, ALU.min)
                ins.then_inc(s("ssd_seg"), 1)
                if h >= 1:
                    decayed(h - 1)
                if h >= 3 and h % 2:
                    pair_y(h // 2 - 1)
            decayed(NH - 1)
            pair_y(3)
            dve.wait_ge(s("ssd_pair"), 4)
            v.tensor_tensor(zs[:, :, :], K.proj[:, Z0:Z0 + 4, :], K.proj[:, Z0:Z0 + 4, :], ALU.mult).then_inc(s("ssd_sq"), 1)
            dve.wait_ge(s("h0_loaded"), 16)
            dve.wait_ge(s("ssd_state_p"), 1)
            link(v.tensor_copy(hout[:, :, 0, :], K.ps[:, 4, 0:4 * NST].rearrange("p (q n) -> p q n", q=4)))
            for q in range(4):
                end = ep[:, q, :].rearrange("p (b t) -> p b t", t=TS)[:, :, TS - 1:TS].to_broadcast([P, NB, NST])
                link(v.tensor_tensor(hout[:, q, 1:NREQ, :], h0[:, q], end, ALU.mult))
                dve.wait_ge(s("ssd_state"), q + 1)
                v.tensor_tensor(hout[:, q, 1:NREQ, :], hout[:, q, 1:NREQ, :],
                                K.ps[:, 5 + q % 2, :].rearrange("p (b n) -> p b n", b=NB), ALU.add
                                ).then_inc(s("ssd_state_used"), 1)
            dve.wait_ge(s("ssd_ss"), 1)
            link(v.tensor_scalar(rstd[:, :], K.ps[:, 7, 0:T], 1.0 / 512, EPS, ALU.mult, ALU.add))
            v.reciprocal(rstd[:, :], rstd[:, :]).then_inc(s("ssd_inv"), 1)
            dve.wait_ge(s("ssd_rstd"), 1)
            for q in range(4):
                v.scalar_tensor_tensor(out=K.proj[:, Z0 + q, :], in0=K.proj[:, Z0 + q, :],
                                       scalar=K.cols[:, C_SSDN + q:C_SSDN + q + 1], in1=rstd[:, :],
                                       op0=ALU.mult, op1=ALU.mult)
            dve.wait_ge(s("ssd_state_used"), 4)
            dve.sem_inc(s("ssm_out_ready"), 1)

        @block.scalar
        def _(act):
            a = nc.scalar
            a.activation(zs[:, :, :], K.proj[:, Z0:Z0 + 4, :], ACT.Silu).then_inc(s("ssd_zs"), 1)
            act.wait_ge(s("ssd_acspair"), 1)
            a.activation(ep[:, :, :].rearrange("p q t -> p (q t)"), K.ps[:, 7, 0:4 * NSAMP], ACT.Exp).then_inc(s("ssd_ep"), 1)
            for h in range(NH):
                act.wait_ge(s("ssd_seg"), h + 1)
                a.activation(E[:, h % 2, :], E[:, h % 2, :], ACT.Exp).then_inc(s("ssd_E"), 1)
            act.wait_ge(s("ssd_inv"), 1)
            a.activation(rstd[:, :], rstd[:, :], ACT.Sqrt).then_inc(s("ssd_rstd"), 1)


def ssd_y(K, pe, h, REG, xdt, M):
    q, s = h // 2, K.sem
    if h % 2 == 0 and q >= 2:
        pe.wait_ge(s("ssd_pair"), q - 1)
    pe.wait_ge(s("ssd_M"), h + 1)
    for r, (s0, n, t0, m, c0) in enumerate(REG):
        mm = pe.matmul(K.ps[64 * (h % 2):64 * (h % 2) + 64, 2 + q % 2, t0:t0 + m], xdt[0:n, r, h * HD:(h + 1) * HD],
                       M[0:n, h % 2, c0:c0 + m], start=(r != 1), stop=(r != 0))
    mm.then_inc(s("ssd_y"), 1)


def hgrn_gates_stage(K, l, G):
    nc, s = K.nc, K.sem
    with (nc.sbuf_tensor("u_hg_t", [P, 3, 4, T], F32) as t, nc.sbuf_tensor("hg_lb", [P, 4, 4], F32) as lb,
          nc.Block(no_gpsimd_drain=True) as block):
        x = K.proj[:, HF0:HF0 + 4, :]
        @block.scalar
        def _(act):
            a, link = nc.scalar, lambda ins: K.ac.link(act, ins)
            act.wait_ge(s("lb_diff"), 1)
            a.activation(lb[:, 3, :], lb[:, 3, :], ACT.Sigmoid).then_inc(s("lb_sig"), 1)
            a.activation(G.k[:, :, :], x, ACT.Sigmoid, scale=-1.0).then_inc(s("hg_sig"), 1)
            link(a.activation(t[:, 0], x, ACT.Abs))
            a.activation(t[:, 0], t[:, 0], ACT.Exp, scale=-1.0).then_inc(s("hg_eabs"), 1)
            act.wait_ge(s("hg_arg"), 1)
            a.activation(t[:, 1], t[:, 1], ACT.Exp)
            a.activation(t[:, 2], t[:, 2], ACT.Exp).then_inc(s("hg_e"), 1)
            act.wait_ge(s("hg_numer"), 1)
            a.activation(t[:, 1], t[:, 1], ACT.Ln).then_inc(s("hg_ln"), 1)
            act.wait_ge(s("hg_eabs"), 1)
            a.activation(t[:, 0], t[:, 0], ACT.Ln, bias=1.0).then_inc(s("hg_ln"), 1)

        @block.vector
        def _(dve):
            v, link = nc.vector, lambda ins: K.vc.link(dve, ins)
            bc = lambda c: c.unsqueeze(2).to_broadcast([P, 4, T])
            v.tensor_tensor(lb[:, 3, :], K.cols[:, C_HG1:C_HG1 + 4], K.cols[:, C_HG0:C_HG0 + 4], ALU.subtract
                            ).then_inc(s("lb_diff"), 1)
            v.tensor_scalar(t[:, 1], x, 0.0, None, ALU.min)
            v.tensor_scalar(t[:, 2], x, 0.0, -1.0, ALU.max, ALU.mult).then_inc(s("hg_arg"), 1)
            dve.wait_ge(s("lb_sig"), 1)
            link(v.tensor_scalar(lb[:, 0, :], lb[:, 3, :], K.cols[:, C_SEL:C_SEL + 1], None, ALU.mult))
            v.tensor_scalar(lb[:, 1, :], lb[:, 0, :], -1.0, 1.0, ALU.mult, ALU.add)
            link(v.tensor_scalar(lb[:, 2, :], lb[:, 0, :], 0.0, None, ALU.is_equal))
            dve.wait_ge(s("hg_sig"), 1)
            v.tensor_tensor(G.k[:, :, :], G.k[:, :, :], bc(lb[:, 1, :]), ALU.mult)
            dve.wait_ge(s("hg_e"), 1)
            link(v.tensor_tensor(t[:, 2], t[:, 2], bc(lb[:, 0, :]), ALU.mult))
            link(v.tensor_tensor(t[:, 1], t[:, 1], t[:, 2], ALU.add))
            v.tensor_scalar(t[:, 1], t[:, 1], LN_FLOOR, None, ALU.max).then_inc(s("hg_numer"), 1)
            dve.wait_ge(s("hg_numer"), 1)
            link(v.tensor_scalar(t[:, 2], x, -LOG_LN_FLOOR, 0.0, ALU.add, ALU.min))
            link(v.tensor_tensor(t[:, 2], t[:, 2], bc(lb[:, 2, :]), ALU.mult))
            dve.wait_ge(s("hg_ln"), 2)
            link(v.tensor_tensor(t[:, 1], t[:, 1], t[:, 0], ALU.subtract))
            link(v.tensor_tensor(t[:, 1], t[:, 1], t[:, 2], ALU.add))
            for h in range(4):
                v.tensor_tensor_scan(G.b[:, h, :], K.keep[:, :], t[:, 1, h, :], 0.0, ALU.mult, ALU.add)


def hgrn_scores_stage(K, l, G):
    nc, s = K.nc, K.sem
    TILES = ((0, P), (P, P), (SEQ, NSAMP))
    with (nc.sbuf_tensor("u_hg_D", [P, 2, 4, T], F32) as Dk, nc.sbuf_tensor("hg_mask", [P, len(HG_LEVELS) - 1, T], I32) as mask,
          nc.Block(no_gpsimd_drain=True) as block):
        q = K.proj[:, HQ0:HQ0 + 4, :]
        NL = len(HG_LEVELS)

        @block.sync
        def _(sp):
            sp.dma_start(mask[:, :, :], K.d["k_mask"]).then_inc(s("hg_mask_loaded"), 16)

        def halves(ap, L):
            if L <= TS:
                w = ap.rearrange("p h (n c) -> p (h n) c", c=L)
            else:
                w = ap[:, :, 0:SEQ].rearrange("p h (n c) -> p h n c", c=L)
            if L <= TS:
                return w[:, :, 0:L // 2], w[:, :, L // 2:L], w[:, :, L // 2 - 1:L // 2].to_broadcast([P, 4 * T // L, L // 2])
            return (w[:, :, :, 0:L // 2], w[:, :, :, L // 2:L],
                    w[:, :, :, L // 2 - 1:L // 2].to_broadcast([P, 4, SEQ // L, L // 2]))

        def width(L):
            return T if L <= TS else SEQ

        @block.vector
        def _(dve):
            v, link = nc.vector, lambda ins: K.vc.link(dve, ins)
            link(v.memset(G.A[:, :, SEQ:T], 0.0))

            def decays(n):
                L = HG_LEVELS[n]
                if n >= 2:
                    dve.wait_ge(s("hg_gram"), n)
                b1, b2, ref = halves(G.b, L)
                d1, d2, _ = halves(Dk[:, n % 2], L)
                v.tensor_tensor(d1, ref, b1, ALU.subtract)
                v.tensor_tensor(d2, b2, ref, ALU.subtract).then_inc(s("hg_seg"), 1)

            decays(0)
            dve.wait_ge(s("hg_mask_loaded"), 16)
            dve.wait_ge(s("hg_gram"), 1)
            v.tensor_tensor(G.A[:, :, 0:SEQ], K.ps[:, 4:8, 0:SEQ], G.eye[:, 0:SEQ].unsqueeze(1).to_broadcast([P, 4, SEQ]), ALU.mult)
            link(v.tensor_tensor(G.A[0:NSAMP, :, SEQ:T], K.ps[0:NSAMP, 4:8, SEQ:T],
                                 G.eye[0:NSAMP, SEQ:T].unsqueeze(1).to_broadcast([NSAMP, 4, NSAMP]), ALU.mult))
            dve.sem_inc(s("hg_bank_free"), 1)
            for n, L in enumerate(HG_LEVELS):
                dve.wait_ge(s("hg_D"), n + 1)
                d1, d2, _ = halves(Dk[:, n % 2], L)
                k1, _, _ = halves(G.k, L)
                _, q2, _ = halves(q, L)
                v.tensor_tensor(d1, d1, k1, ALU.mult)
                v.tensor_tensor(d2, d2, q2, ALU.mult).then_inc(s("hg_W"), 1)
                if n + 1 < NL:
                    decays(n + 1)
                dve.wait_ge(s("hg_gram"), n + 2)
                B0 = 4 * (n % 2)
                if L == 256:
                    v.tensor_copy(G.A01[:, :, :], K.ps[:, B0:B0 + 4, 0:P])
                    continue
                m = mask[:, n, 0:SEQ].unsqueeze(1).to_broadcast([P, 4, SEQ])
                ins = v.copy_predicated(G.A[:, :, 0:SEQ], m, K.ps[:, B0:B0 + 4, 0:SEQ])
                if L <= TS:
                    m = mask[0:NSAMP, n, SEQ:T].unsqueeze(1).to_broadcast([NSAMP, 4, NSAMP])
                    ins = v.copy_predicated(G.A[0:NSAMP, :, SEQ:T], m, K.ps[0:NSAMP, B0:B0 + 4, SEQ:T])
                ins.then_inc(s("hg_bank_free"), 1)
                dve.wait_ge(s("hg_bank_free"), n + 2)

        @block.scalar
        def _(act):
            for n, L in enumerate(HG_LEVELS):
                act.wait_ge(s("hg_seg"), n + 1)
                w = Dk[:, n % 2, :, 0:width(L)]
                nc.scalar.activation(w, w, ACT.Exp).then_inc(s("hg_D"), 1)

        @block.tensor
        def _(pe):
            for h in range(4):
                for t0, n in TILES:
                    mm = pe.matmul(K.ps[0:n, 4 + h, t0:t0 + n], G.k[:, h, t0:t0 + n], q[:, h, t0:t0 + n], start=True, stop=True)
            mm.then_inc(s("hg_gram"), 1)
            for n, L in enumerate(HG_LEVELS):
                pe.wait_ge(s("hg_W"), n + 1)
                if n >= 1:
                    pe.wait_ge(s("hg_bank_free"), n)
                W = Dk[:, n % 2]
                for h in range(4):
                    if L == 256:
                        mm = pe.matmul(K.ps[:, 4 * (n % 2) + h, 0:P], W[:, h, 0:P], W[:, h, P:SEQ], start=True, stop=True)
                        continue
                    for t0, w in TILES[:3 if L <= TS else 2]:
                        mm = pe.matmul(K.ps[0:w, 4 * (n % 2) + h, t0:t0 + w], W[:, h, t0:t0 + w], W[:, h, t0:t0 + w],
                                       start=True, stop=True)
                mm.then_inc(s("hg_gram"), 1)


def hgrn_output_stage(K, l, G):
    nc, s = K.nc, K.sem
    REG = ((0, P), (P, P), (SEQ, NSAMP))
    with ExitStack() as e:
        sb = lambda n, sh: e.enter_context(nc.sbuf_tensor("t_" + n, sh, F32))
        vT, kwT = sb("hg_vT", [P, 3, 4, P]), sb("hg_kwT", [P, 3, 4, P])
        kw, qe = sb("hg_kw", [P, 4, T]), sb("hg_qe", [P, 4, NSAMP])
        vm, s0 = sb("hg_vm", [NSAMP, 2, NB, P]), sb("hg_s0", [P, 2, NB, P])
        sout = sb("hg_sout", [P, 2, NREQ, P])
        be, rstd = sb("hg_be", [P, 4, NB]), sb("hg_rstd", [P, 4, T])
        block = e.enter_context(nc.Block(no_gpsimd_drain=True))
        O = K.proj[:, HQ0:HQ0 + 4, :]

        @block.sync
        def _(sp):
            for h in range(4):
                if h >= 2:
                    sp.wait_ge(s("hg_state_ready"), h - 1)
                sp.dma_start(s0[:, h % 2], K.d["hgrn"][l, h]).then_inc(s(f"hg_s0_loaded{h % 2}"), 16)
            for h in range(4):
                sp.wait_ge(s("hg_state_ready"), h + 1)
                sp.dma_start(K.d["o_hgrn"][l, h], sout[:, h % 2]).then_inc(s(f"hg_stored{h % 2}"), 16)
            for j in range(2):
                sp.wait_ge(s(f"hg_stored{j}"), 32)

        @block.vector
        def _(dve):
            v, link = nc.vector, lambda ins: K.vc.link(dve, ins)
            bS = sample(G.b)
            v.tensor_copy(be[:, :, :], bS[:, :, :, TS - 1])
            v.tensor_tensor(prompt(kw), G.b[:, :, SEQ - 1:SEQ].to_broadcast([P, 4, SEQ]), prompt(G.b), ALU.subtract)
            v.tensor_tensor(sample(kw), bS[:, :, :, TS - 1:TS].to_broadcast([P, 4, NB, TS]), bS, ALU.subtract
                            ).then_inc(s("hg_kw_arg"), 1)
            dve.wait_ge(s("hg_kw_exp"), 1)
            v.tensor_tensor(qe[:, :, :], qe[:, :, :], O[:, :, SEQ:T], ALU.mult)
            v.tensor_tensor(kw[:, :, :], kw[:, :, :], G.k[:, :, :], ALU.mult).then_inc(s("hg_kw"), 1)
            for n, (dst, sig) in enumerate(((vT, "hg_vT"), (kwT, "hg_kwT"))):
                dve.wait_ge(s("hg_tm"), n + 1)
                v.tensor_copy(dst[:, 0:2].rearrange("p r h c -> p r (h c)"), K.ps[:, 0 + 3 * n:2 + 3 * n, :])
                v.tensor_copy(dst[0:NSAMP, 2].rearrange("p h c -> p (h c)"), K.ps[0:NSAMP, 2 + 3 * n, :]).then_inc(s(sig), 1)
            dve.wait_ge(s("hg_vT"), 1)
            for h in range(4):
                if h >= 2:
                    dve.wait_ge(s("hg_state"), h - 1)
                v.tensor_tensor(vm[:, h % 2], vT[0:NSAMP, 2, h].unsqueeze(1).to_broadcast([NSAMP, NB, P]),
                                K.ownb[:, :].unsqueeze(2).to_broadcast([NSAMP, NB, P]), ALU.mult).then_inc(s("hg_vm"), 1)
                dve.wait_ge(s(f"hg_s0_loaded{h % 2}"), 16 * (h // 2 + 1))
                if h >= 2:
                    dve.wait_ge(s(f"hg_stored{h % 2}"), 16 * (h // 2))
                link(v.tensor_tensor(sout[:, h % 2, 1:NREQ], s0[:, h % 2], be[:, h].unsqueeze(2).to_broadcast([P, NB, P]), ALU.mult))
                dve.wait_ge(s("hg_o"), h + 1)
                v.tensor_copy(O[:, h, :], K.ps[:, 0, 0:T]).then_inc(s("hg_o_copied"), 1)
                dve.wait_ge(s("hg_state"), h + 1)
                v.tensor_copy(sout[:, h % 2, 0], K.ps[:, 1, 0:P])
                so = sout[:, h % 2, 1:NREQ].rearrange("p (a b) n -> p a (b n)", a=2)
                v.tensor_tensor(so, so, K.ps[:, 2:4, :], ALU.add).then_inc(s("hg_state_ready"), 1)
            dve.wait_ge(s("hg_o_copied"), 4)
            v.tensor_tensor(kw[:, :, :], O, O, ALU.mult).then_inc(s("hg_sq"), 1)
            dve.wait_ge(s("hg_ss"), 1)
            link(v.tensor_scalar(rstd[:, :, :], K.ps[:, 4:8, 0:T], 1.0 / P, EPS, ALU.mult, ALU.add))
            v.reciprocal(rstd[:, :, :], rstd[:, :, :]).then_inc(s("hg_inv"), 1)
            dve.wait_ge(s("hg_rstd"), 1)
            link(v.scalar_tensor_tensor(out=O, in0=O, scalar=K.cols[:, C_HGN:C_HGN + 1], in1=rstd[:, :, :],
                                        op0=ALU.mult, op1=ALU.mult))
            v.tensor_tensor(O, O, K.proj[:, HG0:HG0 + 4, :], ALU.mult)

        @block.scalar
        def _(act):
            a = nc.scalar
            act.wait_ge(s("hg_kw_arg"), 1)
            a.activation(kw[:, :, :], kw[:, :, :], ACT.Exp)
            a.activation(qe[:, :, :], G.b[:, :, SEQ:T], ACT.Exp)
            a.activation(be[:, :, :], be[:, :, :], ACT.Exp).then_inc(s("hg_kw_exp"), 1)
            a.activation(K.proj[:, HG0:HG0 + 4, :], K.proj[:, HG0:HG0 + 4, :], ACT.Silu)
            act.wait_ge(s("hg_inv"), 1)
            a.activation(rstd[:, :, :], rstd[:, :, :], ACT.Sqrt).then_inc(s("hg_rstd"), 1)

        @block.tensor
        def _(pe):
            for h in range(4):
                for r, (t0, n) in enumerate(REG):
                    mm = pe.transpose(K.ps[0:n, r, h * P:(h + 1) * P], K.proj[:, HI0 + h, t0:t0 + n], K.ident[:, :])
            mm.then_inc(s("hg_tm"), 1)
            pe.wait_ge(s("hg_kw"), 1)
            for h in range(4):
                for r, (t0, n) in enumerate(REG):
                    mm = pe.transpose(K.ps[0:n, 3 + r, h * P:(h + 1) * P], kw[:, h, t0:t0 + n], K.ident[:, :])
            mm.then_inc(s("hg_tm"), 1)
            pe.wait_ge(s("hg_kwT"), 1)
            for h in range(4):
                if h >= 1:
                    pe.wait_ge(s("hg_o_copied"), h)
                    pe.wait_ge(s("hg_state_ready"), h)
                o = K.ps[:, 0, :]
                pe.matmul(o[:, 0:P], vT[:, 0, h], G.A[:, h, 0:P], start=True, stop=True)
                pe.matmul(o[:, P:SEQ], vT[:, 0, h], G.A01[:, h], start=True, stop=False)
                pe.matmul(o[:, P:SEQ], vT[:, 1, h], G.A[:, h, P:SEQ], start=False, stop=True)
                pe.wait_ge(s(f"hg_s0_loaded{h % 2}"), 16 * (h // 2 + 1))
                pe.matmul(o[:, SEQ:T], vT[0:NSAMP, 2, h], G.A[0:NSAMP, h, SEQ:T], start=True, stop=False)
                for b in range(NB):
                    mm = pe.matmul(o[:, SEQ + b * TS:SEQ + (b + 1) * TS], s0[:, h % 2, b], qe[:, h, b * TS:(b + 1) * TS],
                                   start=False, stop=(b == NB - 1))
                mm.then_inc(s("hg_o"), 1)
                pe.matmul(K.ps[:, 1, 0:P], kwT[:, 0, h], vT[:, 0, h], start=True, stop=False)
                pe.matmul(K.ps[:, 1, 0:P], kwT[:, 1, h], vT[:, 1, h], start=False, stop=True)
                pe.wait_ge(s("hg_vm"), h + 1)
                for j in range(2):
                    mm = pe.matmul(K.ps[:, 2 + j, :], kwT[0:NSAMP, 2, h],
                                   vm[:, h % 2, 4 * j:4 * j + 4].rearrange("p b n -> p (b n)"), start=True, stop=True)
                mm.then_inc(s("hg_state"), 1)
            pe.wait_ge(s("hg_sq"), 1)
            for h in range(4):
                mm = pe.matmul(K.ps[:, 4 + h, 0:T], K.ones[:, :], kw[:, h, :], start=True, stop=True)
            mm.then_inc(s("hg_ss"), 1)


LN_FLOOR = 1e-18
LOG_LN_FLOOR = -41.44653167389282


def mla_project_stage(K, l, A):
    nc, s = K.nc, K.sem
    with ExitStack() as e:
        sb = lambda n, sh: e.enter_context(nc.sbuf_tensor("t_" + n, sh, F32))
        wuq, wuk = sb("w_uq", [P, 2, 768]), sb("w_uk", [NOPE, MH, 256])
        sq, rstd = sb("mla_sq", [P, 4, T]), sb("mla_rstd", [P, 2, T])
        qn, rot = sb("mla_qn", [NOPE, 2, T]), sb("mla_rot", [ROPE, 2, T])
        block = e.enter_context(nc.Block(no_gpsimd_drain=True))
        C = K.proj[:, QD0:QD0 + 4, :]

        @block.sync
        def _(sp):
            sp.dma_start(wuq[:, :, :], K.d["w_uq"][l]).then_inc(s("uq_loaded"), 16)
            sp.dma_start(wuk[:, :, :], K.d["w_uk"][l]).then_inc(s("uk_loaded"), 16)
            sp.wait_ge(s("mla_normed"), 1)
            sp.dma_start(K.d["o_ckv"][l], K.proj[:, KVD0:KVD0 + 2, :]).then_inc(s("ckv_stored"), 16)
            sp.wait_ge(s("krope_ready"), 1)
            sp.dma_start(K.d["o_krope"][l], K.krope[:, :]).then_inc(s("krope_stored"), 16)
            sp.wait_ge(s("ckv_stored"), 16)
            sp.wait_ge(s("krope_stored"), 16)

        @block.vector
        def _(dve):
            v, link = nc.vector, lambda ins: K.vc.link(dve, ins)
            v.tensor_tensor(sq[:, :, :], C, C, ALU.mult).then_inc(s("mla_sq"), 1)
            dve.wait_ge(s("mla_ss"), 1)
            link(v.tensor_scalar(rstd[:, :, :], K.ps[:, 0:2, 0:T], 1.0 / 256, EPS, ALU.mult, ALU.add))
            v.reciprocal(rstd[:, :, :], rstd[:, :, :]).then_inc(s("mla_inv"), 1)
            dve.wait_ge(s("mla_rstd"), 1)
            for c in range(4):
                ins = v.scalar_tensor_tensor(out=C[:, c], in0=C[:, c], scalar=K.cols[:, C_QN + c:C_QN + c + 1],
                                             in1=rstd[:, c // 2, :], op0=ALU.mult, op1=ALU.mult)
            ins.then_inc(s("mla_normed"), 1)
            dve.wait_ge(s("krope_turned"), 1)
            link(v.tensor_tensor(rot[:, 0], K.ps[0:ROPE, 2, 0:T], K.sin[:, :], ALU.mult))
            link(v.tensor_tensor(K.krope[:, :], K.krope[:, :], K.cos[:, :], ALU.mult))
            v.tensor_tensor(K.krope[:, :], K.krope[:, :], rot[:, 0], ALU.add).then_inc(s("krope_ready"), 1)
            dve.wait_ge(s("ckv_tm"), 1)
            for r, n in enumerate((P, P, NSAMP)):
                v.tensor_copy(A.ckv[0:n, r, :], K.ps[0:n, 3 + r, 0:256])
            dve.sem_inc(s("ckv_tm_copied"), 1)
            for h in range(MH):
                if h >= 2:
                    dve.wait_ge(s("q_abs_done"), h - 1)
                dve.wait_ge(s("q_head_done"), h + 1)
                v.tensor_copy(qn[:, h % 2], K.ps[0:NOPE, 0, 0:T]).then_inc(s("q_nope_copied"), 1)
                v.tensor_copy(A.qr[:, h], K.ps[0:ROPE, 1, 0:T]).then_inc(s("q_rope_copied"), 1)
                dve.wait_ge(s("q_abs_done"), h + 1)
                v.tensor_copy(A.qa[:, :, h, :], K.ps[:, 3:5, 0:T]).then_inc(s("q_abs_copied"), 1)
                dve.wait_ge(s("q_turned"), h + 1)
                v.tensor_tensor(rot[:, h % 2], K.ps[0:ROPE, 2, 0:T], K.sin[:, :], ALU.mult).then_inc(s("q_turned_read"), 1)
                link(v.tensor_tensor(A.qr[:, h], A.qr[:, h], K.cos[:, :], ALU.mult))
                dve.wait_ge(s("q_turned_read"), h + 1)
                v.tensor_tensor(A.qr[:, h], A.qr[:, h], rot[:, h % 2], ALU.add)

        @block.scalar
        def _(act):
            act.wait_ge(s("mla_inv"), 1)
            nc.scalar.activation(rstd[:, :, :], rstd[:, :, :], ACT.Sqrt).then_inc(s("mla_rstd"), 1)

        @block.tensor
        def _(pe):
            pe.matmul(K.ps[0:ROPE, 2, 0:T], K.turn[:, :], K.krope[:, :], start=True, stop=True).then_inc(s("krope_turned"), 1)
            pe.wait_ge(s("mla_sq"), 1)
            sum_over_partitions(K, pe, K.ps[:, 0, 0:T], [sq[:, 0], sq[:, 1]])
            sum_over_partitions(K, pe, K.ps[:, 1, 0:T], [sq[:, 2], sq[:, 3]]).then_inc(s("mla_ss"), 1)
            pe.wait_ge(s("mla_normed"), 1)
            for r, (t0, n) in enumerate(((0, P), (P, P), (SEQ, NSAMP))):
                for c in range(2):
                    mm = pe.transpose(K.ps[0:n, 3 + r, c * P:(c + 1) * P], C[:, 2 + c, t0:t0 + n], K.ident[:, :])
            mm.then_inc(s("ckv_tm"), 1)
            pe.wait_ge(s("uq_loaded"), 16)
            pe.wait_ge(s("uk_loaded"), 16)
            pe.wait_ge(s("krope_ready"), 1)
            pe.wait_ge(s("ckv_tm_copied"), 1)
            for h in range(MH):
                if h >= 1:
                    pe.wait_ge(s("q_nope_copied"), h)
                    pe.wait_ge(s("q_rope_copied"), h)
                for k in range(2):
                    pe.matmul(K.ps[0:NOPE, 0, 0:T], wuq[:, k, h * 96:h * 96 + NOPE], C[:, k], start=(k == 0), stop=(k == 1))
                for k in range(2):
                    mm = pe.matmul(K.ps[0:ROPE, 1, 0:T], wuq[:, k, h * 96 + NOPE:h * 96 + 96], C[:, k],
                                   start=(k == 0), stop=(k == 1))
                mm.then_inc(s("q_head_done"), 1)
                pe.wait_ge(s("q_nope_copied"), h + 1)
                if h >= 1:
                    pe.wait_ge(s("q_abs_copied"), h)
                for c in range(2):
                    mm = pe.matmul(K.ps[:, 3 + c, 0:T], wuk[:, h, c * P:(c + 1) * P], qn[:, h % 2], start=True, stop=True)
                mm.then_inc(s("q_abs_done"), 1)
                pe.wait_ge(s("q_rope_copied"), h + 1)
                if h >= 1:
                    pe.wait_ge(s("q_turned_read"), h)
                pe.matmul(K.ps[0:ROPE, 2, 0:T], K.turn[:, :], A.qr[:, h], start=True, stop=True).then_inc(s("q_turned"), 1)


def mla_prompt_stage(K, l, A):
    nc, s = K.nc, K.sem
    with (nc.sbuf_tensor("u_pr_p", [P, MH, SEQ], F32) as p, nc.sbuf_tensor("pr_stat", [P, 3, MH], F32) as st,
          nc.sbuf_tensor("u_pr_pT", [P, 2, MH, P], F32) as pT, nc.Block(no_gpsimd_drain=True) as block):
        def scores(n, j):
            return K.ps[:, 2 * j:2 * j + 2, :].rearrange("p b (h k) -> p (b h) k", h=4)

        @block.tensor
        def _(pe):
            for n in range(2):
                if n:
                    pe.wait_ge(s("pr_scores_read"), n)
                q0 = n * P
                for j in range(n + 1):
                    for h in range(MH):
                        out = scores(n, j)[:, h]
                        for c in range(2):
                            pe.matmul(out, A.qa[:, c, h, q0:q0 + P], K.proj[:, KVD0 + c, j * P:(j + 1) * P],
                                      start=(c == 0), stop=False)
                        mm = pe.matmul(out, A.qr[:, h, q0:q0 + P], K.krope[:, j * P:(j + 1) * P], start=False, stop=True)
                mm.then_inc(s("pr_scores"), 1)
                pe.wait_ge(s("pr_p"), n + 1)
                for j in range(n + 1):
                    if n + j >= 1:
                        pe.wait_ge(s("pr_pT_copied"), n + j)
                    for h in range(MH):
                        mm = pe.transpose(K.ps[:, 4 + h // 4, (h % 4) * P:(h % 4 + 1) * P], p[:, h, j * P:(j + 1) * P],
                                          K.ident[:, :])
                    mm.then_inc(s("pr_pT"), 1)
                pe.wait_ge(s("pr_pT_copied"), 1 if n == 0 else 3)
                for g in range(2):
                    if n + g >= 1:
                        pe.wait_ge(s("pr_o_copied"), 2 * n + g)
                    for c in range(2):
                        for j in range(n + 1):
                            mm = pe.matmul(K.ps[:, 6 + c, :], A.ckv[:, j, c * P:(c + 1) * P],
                                           pT[:, j, 4 * g:4 * g + 4].rearrange("p h q -> p (h q)"),
                                           start=(j == 0), stop=(j == n))
                    mm.then_inc(s("pr_o"), 1)

        @block.vector
        def _(dve):
            v, link = nc.vector, lambda ins: K.vc.link(dve, ins)
            for n in range(2):
                W = (n + 1) * P
                dve.wait_ge(s("pr_scores"), n + 1)
                if n:
                    dve.wait_ge(s("pr_pT"), 1)
                for j in range(n):
                    v.tensor_copy(p[:, :, j * P:(j + 1) * P], scores(n, j))
                link(v.tensor_tensor(p[:, :, n * P:W], scores(n, n), K.later[:, :].unsqueeze(1).to_broadcast([P, MH, P]), ALU.add))
                dve.sem_inc(s("pr_scores_read"), 1)
                link(v.tensor_reduce(st[:, 0, :], p[:, :, 0:W], AX.X, ALU.max))
                v.tensor_tensor(p[:, :, 0:W], p[:, :, 0:W], st[:, 0, :].unsqueeze(2).to_broadcast([P, MH, W]), ALU.subtract
                                ).then_inc(s("pr_arg"), 1)
                dve.wait_ge(s("pr_exp"), n + 1)
                link(v.tensor_reduce(st[:, 1, :], p[:, :, 0:W], AX.X, ALU.add))
                link(v.reciprocal(st[:, 2, :], st[:, 1, :]))
                v.tensor_tensor(p[:, :, 0:W], p[:, :, 0:W], st[:, 2, :].unsqueeze(2).to_broadcast([P, MH, W]), ALU.mult
                                ).then_inc(s("pr_p"), 1)
                for j in range(n + 1):
                    dve.wait_ge(s("pr_pT"), n + j + 1)
                    if n:
                        dve.wait_ge(s("pr_o"), 2)
                    v.tensor_copy(pT[:, j].rearrange("p h q -> p (h q)"), K.ps[:, 4:6, :].rearrange("p b c -> p (b c)")
                                  ).then_inc(s("pr_pT_copied"), 1)
                for g in range(2):
                    dve.wait_ge(s("pr_o"), 2 * n + g + 1)
                    v.tensor_copy(A.qa[:, :, 4 * g:4 * g + 4, n * P:(n + 1) * P],
                                  K.ps[:, 6:8, :].rearrange("p c (h q) -> p c h q", h=4)).then_inc(s("pr_o_copied"), 1)

        @block.scalar
        def _(act):
            for n in range(2):
                act.wait_ge(s("pr_arg"), n + 1)
                w = p[:, :, 0:(n + 1) * P]
                nc.scalar.activation(w, w, ACT.Exp, scale=ATT_SCALE).then_inc(s("pr_exp"), 1)


def mla_sample_stage(K, l, A):
    nc, s = K.nc, K.sem
    NK = PAST + NSAMP
    PW = 640
    with ExitStack() as e:
        sb = lambda n, sh: e.enter_context(nc.sbuf_tensor("t_" + n, sh, F32))
        pg = sb("pages", [P, 2, NPAGE, PW])
        p = sb("sa_p", [NSAMP, 2, NK])
        st = sb("sa_stat", [NSAMP, 2, 4])
        spare = K.h[:, :, :].rearrange("p k t -> p (k t)")
        cut = 2 * (NPAGE + 1) * NSAMP
        pT = spare[:, 0:cut].rearrange("p (a j q) -> p a j q", a=2, j=NPAGE + 1)
        qa_b = spare[:, cut:cut + 2 * NB * NSAMP].rearrange("p (c b q) -> p c b q", c=2, b=NB)
        qr_b = K.proj[0:ROPE, XBC0:XBC0 + 2, 0:NB * NSAMP // 2].rearrange("p c (b q) -> p c b q", b=NB // 2)
        block = e.enter_context(nc.Block(no_gpsimd_drain=True))

        @block.sync
        def _(sp):
            for b in range(NB):
                if b >= 2:
                    sp.wait_ge(s("sa_o"), b - 1)
                for j in range(NPAGE):
                    page = sp.value_load(K.table[0:1, b * NPAGE + j:b * NPAGE + j + 1], min_val=0, max_val=K.n_pool - 1)
                    sp.dma_start(pg[:, b % 2, j, :], K.d["pages"][l, bass.ds(page, 1)].rearrange("o p c -> p (o c)")
                                 ).then_inc(s(f"pages_loaded{b % 2}"), 16)

        @block.tensor
        def _(pe):
            pe.wait_ge(s("sa_q"), 1)

            def value(b):
                pe.wait_ge(s("sa_p"), b + 1)
                if b >= 1:
                    pe.wait_ge(s("sa_pT_copied"), b)
                for j in range(NPAGE):
                    pe.transpose(K.ps[:, 4, j * NSAMP:(j + 1) * NSAMP], p[:, b % 2, j * P:(j + 1) * P],
                                 K.ident[0:NSAMP, 0:NSAMP])
                pe.transpose(K.ps[0:NSAMP, 5, 0:NSAMP], p[:, b % 2, PAST:NK], K.ident[0:NSAMP, 0:NSAMP]
                             ).then_inc(s("sa_pT"), 1)
                pe.wait_ge(s("sa_pT_copied"), b + 1)
                if b >= 1:
                    pe.wait_ge(s("sa_o_copied"), b)
                for c in range(2):
                    out = K.ps[:, 6 + c, 0:NSAMP]
                    for j in range(NPAGE):
                        pe.matmul(out, pg[:, b % 2, j, 384 + c * P:384 + (c + 1) * P], pT[:, b % 2, j, :],
                                  start=(j == 0), stop=False)
                    mm = pe.matmul(out, A.ckv[0:NSAMP, 2, c * P:(c + 1) * P], pT[0:NSAMP, b % 2, NPAGE, :],
                                   start=False, stop=True)
                mm.then_inc(s("sa_o"), 1)

            for b in range(NB):
                pe.wait_ge(s(f"pages_loaded{b % 2}"), 16 * NPAGE * (b // 2 + 1))
                if b >= 1:
                    pe.wait_ge(s("sa_scores_read"), b)
                for g in range(2):
                    for c in range(3):
                        lhs = qa_b[:, c, b] if c < 2 else qr_b[:, b // 4, b % 4]
                        rhs = pg[0:P if c < 2 else ROPE, b % 2, 4 * g:4 * g + 4, c * P:(c + 1) * P]
                        pe.matmul(K.ps[0:NSAMP, g, :], lhs, rhs, start=(c == 0), stop=(c == 2))
                for c in range(3):
                    lhs = qa_b[:, c, b] if c < 2 else qr_b[:, b // 4, b % 4]
                    rhs = K.proj[:, KVD0 + c, SEQ:T] if c < 2 else K.krope[:, SEQ:T]
                    mm = pe.matmul(K.ps[0:NSAMP, 2, 0:NSAMP], lhs, rhs, start=(c == 0), stop=(c == 2))
                mm.then_inc(s("sa_scores"), 1)
                if b >= 1:
                    value(b - 1)
            value(NB - 1)

        @block.vector
        def _(dve):
            v, link = nc.vector, lambda ins: K.vc.link(dve, ins)
            for b in range(NB):
                for c in range(2):
                    v.tensor_copy(qa_b[:, c, b].rearrange("p (h t) -> p h t", t=TS), A.qa[:, c, :, SEQ + b * TS:SEQ + (b + 1) * TS])
                link(v.tensor_copy(qr_b[:, b // 4, b % 4].rearrange("p (h t) -> p h t", t=TS), A.qr[:, :, SEQ + b * TS:SEQ + (b + 1) * TS]))
            dve.sem_inc(s("sa_q"), 1)

            def softmax(b):
                S = K.ps[0:NSAMP, 0:3, :].rearrange("p b c -> p (b c)")[:, 0:NK]
                dve.wait_ge(s("sa_scores"), b + 1)
                link(v.tensor_tensor(K.ps[0:NSAMP, 2, 0:NSAMP], K.ps[0:NSAMP, 2, 0:NSAMP], K.own[:, b, :], ALU.add))
                link(v.tensor_reduce(st[:, b % 2, 0:1], S, AX.X, ALU.max))
                v.tensor_scalar(st[:, b % 2, 1:2], st[:, b % 2, 0:1], -ATT_SCALE, None, ALU.mult).then_inc(s("sa_max"), 1)

            def normalise(b):
                dve.wait_ge(s("sa_exp"), b + 1)
                link(v.reciprocal(st[:, b % 2, 3:4], st[:, b % 2, 2:3]))
                v.tensor_scalar(p[:, b % 2, :], p[:, b % 2, :], st[:, b % 2, 3:4], None, ALU.mult).then_inc(s("sa_p"), 1)

            def values(b):
                dve.wait_ge(s("sa_pT"), b + 1)
                if b >= 2:
                    dve.wait_ge(s("sa_o"), b - 1)
                v.tensor_copy(pT[:, b % 2, 0:NPAGE].rearrange("p j q -> p (j q)"), K.ps[:, 4, :])
                link(v.tensor_copy(pT[0:NSAMP, b % 2, NPAGE], K.ps[0:NSAMP, 5, 0:NSAMP]))
                dve.sem_inc(s("sa_pT_copied"), 1)
                dve.wait_ge(s("sa_o"), b + 1)
                v.tensor_copy(A.qa[:, :, :, SEQ + b * TS:SEQ + (b + 1) * TS],
                              K.ps[:, 6:8, 0:NSAMP].rearrange("p c (h t) -> p c h t", t=TS)).then_inc(s("sa_o_copied"), 1)

            for b in range(NB):
                softmax(b)
                normalise(b)
                if b >= 1:
                    values(b - 1)
            values(NB - 1)

        @block.scalar
        def _(act):
            for b in range(NB):
                act.wait_ge(s("sa_max"), b + 1)
                if b >= 2:
                    act.wait_ge(s("sa_pT"), b - 1)
                nc.scalar.activation(p[:, b % 2, :], K.ps[0:NSAMP, 0:3, :].rearrange("p b c -> p (b c)")[:, 0:NK], ACT.Exp,
                                     bias=st[:, b % 2, 1:2], scale=ATT_SCALE, accum_out=st[:, b % 2, 2:3]
                                     ).then_inc(s("sa_exp"), 1)
                act.wait_ge(s("sa_exp"), b + 1)
                act.sem_inc(s("sa_scores_read"), 1)


def mla_value_stage(K, l, A):
    nc, s = K.nc, K.sem
    with nc.sbuf_tensor("u_w_uv", [P, 2, MH, 64], F32) as wuv, nc.Block(no_gpsimd_drain=True) as block:
        @block.sync
        def _(sp):
            sp.dma_start(wuv[:, :, :, :], K.d["w_uv"][l]).then_inc(s("uv_loaded"), 16)

        @block.tensor
        def _(pe):
            pe.wait_ge(s("uv_loaded"), 16)
            for h in range(MH):
                for k in range(2):
                    mm = pe.matmul(K.ps[64 * (h % 2):64 * (h % 2) + 64, h // 2, 0:T], wuv[:, k, h, :], A.qa[:, k, h, :],
                                   start=(k == 0), stop=(k == 1))
            mm.then_inc(s("yc_done"), 1)

        @block.vector
        def _(dve):
            dve.wait_ge(s("yc_done"), 1)
            nc.vector.tensor_copy(K.proj[:, HF0:HF0 + 4, :], K.ps[:, 0:4, 0:T])


def lru_stage(K, l):
    nc, s = K.nc, K.sem
    with ExitStack() as e:
        sb = lambda n, sh: e.enter_context(nc.sbuf_tensor("t_" + n, sh, F32))
        w = sb("lru_w", [P, 2, 4, P])
        r, ig, t1 = sb("lru_r", [P, 4, T]), sb("lru_i", [P, 4, T]), sb("lru_t", [P, 4, T])
        sp_, h0, hout = sb("lru_sp", [P, 4, 4]), sb("lru_h0", [P, 4, NB]), sb("lru_hout", [P, 4, NREQ])
        block = e.enter_context(nc.Block(no_gpsimd_drain=True))
        X, Y = K.proj[:, LX0:LX0 + 4, :], K.proj[:, LY0:LY0 + 4, :]

        @block.sync
        def _(sp):
            sp.dma_start(w[:, :, :, :], K.d["lru_w"][l]).then_inc(s("lru_w_loaded"), 16)
            sp.dma_start(h0[:, :, :], K.d["lru_state"][l]).then_inc(s("lru_h0_loaded"), 16)
            sp.wait_ge(s("lru_out_ready"), 1)
            sp.dma_start(K.d["o_lru"][l], hout[:, :, :]).then_inc(s("lru_stored"), 16)
            sp.wait_ge(s("lru_stored"), 16)

        @block.tensor
        def _(pe):
            pe.wait_ge(s("lru_w_loaded"), 16)
            for n in range(2):
                for c in range(4):
                    mm = pe.matmul(K.ps[:, 4 * n + c, 0:T], w[:, n, c, :], X[:, c], start=True, stop=True)
                mm.then_inc(s("lru_gates"), 1)

        @block.scalar
        def _(act):
            a, link = nc.scalar, lambda ins: K.ac.link(act, ins)
            link(a.activation(sp_[:, 0], K.cols[:, C_LA:C_LA + 4], ACT.Abs))
            link(a.activation(sp_[:, 0], sp_[:, 0], ACT.Exp, scale=-1.0))
            a.activation(sp_[:, 1], sp_[:, 0], ACT.Ln, bias=1.0).then_inc(s("lru_ln"), 1)
            for n, (dst, c0) in enumerate(((r, C_BR), (ig, C_BI))):
                act.wait_ge(s("lru_gates"), n + 1)
                for c in range(4):
                    ins = a.activation(dst[:, c], K.ps[:, 4 * n + c, 0:T], ACT.Sigmoid, bias=K.cols[:, c0 + c:c0 + c + 1])
            ins.then_inc(s("lru_sig"), 1)
            act.wait_ge(s("lru_loga"), 1)
            a.activation(t1[:, :, :], r[:, :, :], ACT.Tanh).then_inc(s("lru_tanh"), 1)
            act.wait_ge(s("lru_tanh"), 1)
            a.activation(r[:, :, :], r[:, :, :], ACT.Exp).then_inc(s("lru_a"), 1)
            act.wait_ge(s("lru_m2"), 1)
            a.activation(t1[:, :, :], t1[:, :, :], ACT.Sqrt).then_inc(s("lru_mult"), 1)
            a.activation(Y, Y, ACT.Gelu_apprx_tanh).then_inc(s("lru_gelu"), 1)

        @block.vector
        def _(dve):
            v, link = nc.vector, lambda ins: K.vc.link(dve, ins)
            link(v.tensor_scalar(sp_[:, 2], K.cols[:, C_LA:C_LA + 4], -1.0, 0.0, ALU.mult, ALU.max))
            dve.wait_ge(s("lru_ln"), 1)
            link(v.tensor_tensor(sp_[:, 2], sp_[:, 2], sp_[:, 1], ALU.add))
            link(v.tensor_scalar(sp_[:, 3], sp_[:, 2], -8.0, None, ALU.mult))
            dve.wait_ge(s("lru_sig"), 1)
            v.tensor_tensor(r[:, :, :], r[:, :, :], sp_[:, 3].unsqueeze(2).to_broadcast([P, 4, T]), ALU.mult
                            ).then_inc(s("lru_loga"), 1)
            link(v.tensor_tensor(ig[:, :, :], ig[:, :, :], X, ALU.mult))
            dve.wait_ge(s("lru_a"), 1)
            link(v.tensor_tensor(X, r[:, :, :], r[:, :, :], ALU.mult))
            link(v.tensor_scalar(X, X, 1.0, -1.0, ALU.add, ALU.mult))
            link(v.tensor_tensor(t1[:, :, :], t1[:, :, :], X, ALU.mult))
            v.tensor_scalar(t1[:, :, :], t1[:, :, :], 1e-30, None, ALU.max).then_inc(s("lru_m2"), 1)
            dve.wait_ge(s("lru_mult"), 1)
            link(v.memset(t1[:, :, 0:1], 1.0))
            link(v.tensor_tensor(t1[:, :, :], t1[:, :, :], ig[:, :, :], ALU.mult))
            dve.wait_ge(s("lru_h0_loaded"), 16)
            link(v.tensor_tensor(h0[:, :, :], h0[:, :, :], sample(r)[:, :, :, 0], ALU.mult))
            link(v.tensor_tensor(sample(t1)[:, :, :, 0], sample(t1)[:, :, :, 0], h0[:, :, :], ALU.add))
            link(v.tensor_tensor(r[:, :, :], r[:, :, :], K.keep[:, :].unsqueeze(1).to_broadcast([P, 4, T]), ALU.mult))
            link(v.tensor_tensor_scan(X.rearrange("p c t -> p (c t)"), r[:, :, :].rearrange("p c t -> p (c t)"),
                                      t1[:, :, :].rearrange("p c t -> p (c t)"), 0.0, ALU.mult, ALU.add))
            v.tensor_copy(hout[:, :, 0:1], X[:, :, SEQ - 1:SEQ])
            v.tensor_copy(hout[:, :, 1:NREQ], sample(X)[:, :, :, TS - 1]).then_inc(s("lru_out_ready"), 1)
            dve.wait_ge(s("lru_gelu"), 1)
            v.tensor_tensor(Y, X, Y, ALU.mult)


def merge_stage(K, l):
    nc, s = K.nc, K.sem
    SL = 4
    SRC = (Z0, HQ0, HF0, LY0)
    with (nc.sbuf_tensor("u_wbr", [P, SL, 4, 512], F32) as wb, nc.sbuf_tensor("mg_tmp", [P, 2, T], F32) as tmp,
          nc.Block(no_gpsimd_drain=True) as block):
        @block.sync
        def _(sp):
            for n in range(12):
                if n >= SL:
                    m = n - SL + 1
                    sp.wait_ge(s("mg_tile"), 4 * min(m, 8) + 2 * max(m - 8, 0))
                src = K.d["w_branch"][l, n] if n < 8 else K.d["w_out"][l, n - 8]
                sp.dma_start(wb[:, n % SL].rearrange("p a b -> p (a b)"), src).then_inc(s(f"mg_loaded{n % SL}"), 16)

        @block.scalar
        def _(act):
            for n in range(4):
                g = K.proj[:, GL0 + 8 * n:GL0 + 8 * n + 8, :]
                nc.scalar.activation(g, g, ACT.Sigmoid).then_inc(s("mg_gates"), 1)

        @block.tensor
        def _(pe):
            for n in range(12):
                pe.wait_ge(s(f"mg_loaded{n % SL}"), 16 * (n // SL + 1))
                if n == 8:
                    pe.wait_ge(s("mg_merged"), 1)
                for m in range(4 if n < 8 else 2):
                    t = 4 * n + m if n < 8 else 32 + 2 * (n - 8) + m
                    if t >= 8:
                        pe.wait_ge(s("mg_read"), t - 7)
                    if n < 8:
                        for k in range(4):
                            mm = pe.matmul(K.ps[:, t % 8, 0:T], wb[:, n % SL, k, m * P:(m + 1) * P],
                                           K.proj[:, SRC[n // 2] + k, :], start=(k == 0), stop=(k == 3))
                    else:
                        w = wb[:, n % SL].rearrange("p a b -> p (a b)").rearrange("p (k c) -> p k c", k=KD)
                        for k in range(KD):
                            mm = pe.matmul(K.ps[:, t % 8, 0:T], w[:, k, m * P:(m + 1) * P], K.h[:, k, :],
                                           start=(k == 0), stop=(k == KD - 1))
                    mm.then_inc(s("mg_tile"), 1)

        @block.vector
        def _(dve):
            v, link = nc.vector, lambda ins: K.vc.link(dve, ins)
            for t in range(32):
                n, m = t // 8, t % 8
                if m == 0:
                    dve.wait_ge(s("mg_gates"), n + 1)
                dve.wait_ge(s("mg_tile"), t + 1)
                if n == 0:
                    v.tensor_tensor(K.h[:, m, :], K.ps[:, t % 8, 0:T], K.proj[:, GL0 + t, :], ALU.mult).then_inc(s("mg_read"), 1)
                else:
                    v.tensor_tensor(tmp[:, t % 2], K.ps[:, t % 8, 0:T], K.proj[:, GL0 + t, :], ALU.mult).then_inc(s("mg_read"), 1)
                    dve.wait_ge(s("mg_read"), t + 1)
                    link(v.tensor_tensor(K.h[:, m, :], K.h[:, m, :], tmp[:, t % 2], ALU.add))
            dve.sem_inc(s("mg_merged"), 1)
            for m in range(KD):
                t = 32 + m
                dve.wait_ge(s("mg_tile"), t + 1)
                residual(K, dve, K.ps[:, t % 8, 0:T], tmp[:, t % 2], 16 + m, m, s("mg_read"), t + 1)


def residual(K, dve, src, tmp, g, m, read, count):
    v = K.nc.vector
    v.scalar_tensor_tensor(out=K.x[:, m, 0:SEQ], in0=src[:, 0:SEQ], scalar=K.mod[:, g, 0:1], in1=K.x[:, m, 0:SEQ],
                           op0=ALU.mult, op1=ALU.add)
    v.tensor_tensor(tmp[:, SEQ:T].rearrange("p (b t) -> p b t", t=TS), src[:, SEQ:T].rearrange("p (b t) -> p b t", t=TS),
                    K.mod[:, g, 1:NREQ].unsqueeze(2).to_broadcast([P, NB, TS]), ALU.mult).then_inc(read, 1)
    dve.wait_ge(read, count)
    v.tensor_tensor(K.x[:, m, SEQ:T], K.x[:, m, SEQ:T], tmp[:, SEQ:T], ALU.add)


def router_stage(K, l):
    nc, s = K.nc, K.sem
    with ExitStack() as e:
        sb = lambda n, sh: e.enter_context(nc.sbuf_tensor("t_" + n, sh, F32))
        w, bias = sb("w_router", [P, KD, 36]), sb("b_router", [1, 36])
        L, g = sb("rt_L", [P, 3, 36]), sb("rt_g", [P, 4, 3, 4])
        ee, st, comb = sb("rt_e", [P, 5, 3, 8]), sb("rt_st", [P, 10, 3]), sb("rt_comb", [P, 3, 32])
        gate, combT = sb("rt_gate", [P, 3, 4, 8]), sb("rt_combT", [NEXP, T])
        block = e.enter_context(nc.Block(no_gpsimd_drain=True))
        REG = ((0, P), (P, P), (SEQ, NSAMP))

        @block.sync
        def _(sp):
            sp.dma_start(w[:, :, :], K.d["w_router"][l]).then_inc(s("rt_w_loaded"), 16)
            sp.dma_start(bias[:, :], K.d["b_router"][l]).then_inc(s("rt_b_loaded"), 16)
            sp.wait_ge(s("rt_combT"), 1)
            sp.dma_start(K.d["combine"], combT[:, :]).then_inc(s("rt_stored"), 16)
            sp.wait_ge(s("rt_stored"), 16)

        @block.tensor
        def _(pe):
            pe.wait_ge(s("rt_w_loaded"), 16)
            pe.wait_ge(s("rt_b_loaded"), 16)
            for r, (t0, n) in enumerate(REG):
                for k in range(KD):
                    pe.matmul(K.ps[0:n, 0, r * 36:(r + 1) * 36], K.h[:, k, t0:t0 + n], w[:, k, :], start=(k == 0), stop=False)
                mm = pe.matmul(K.ps[0:n, 0, r * 36:(r + 1) * 36], K.ones[0:1, 0:n], bias[:, :], start=False, stop=True)
            mm.then_inc(s("rt_logits"), 1)
            pe.wait_ge(s("rt_comb"), 1)
            for r, (t0, n) in enumerate(REG):
                mm = pe.transpose(K.ps[0:NEXP, 1, t0:t0 + n], comb[0:n, r, :], K.ident[0:n, 0:n])
            mm.then_inc(s("rt_turned"), 1)

        @block.vector
        def _(dve):
            v, link = nc.vector, lambda ins: K.vc.link(dve, ins)

            def first_max(x, mx, onehot, tmp, n):
                bc = lambda a: a.unsqueeze(2).to_broadcast([P, 3, n])
                io = K.iota[:, 0:n].unsqueeze(1).to_broadcast([P, 3, n])
                link(v.tensor_reduce(mx, x, AX.X, ALU.max))
                link(v.tensor_tensor(tmp, x, bc(mx), ALU.is_equal))
                link(v.tensor_scalar(tmp, tmp, -100.0, 100.0, ALU.mult, ALU.add))
                link(v.tensor_tensor(tmp, tmp, io, ALU.add))
                link(v.tensor_reduce(st[:, 9], tmp, AX.X, ALU.min))
                link(v.tensor_tensor(onehot, io, bc(st[:, 9]), ALU.is_equal))

            link(v.memset(L[:, 2, :], 0.0))
            dve.wait_ge(s("rt_logits"), 1)
            v.tensor_copy(L[:, 0:2].rearrange("p r c -> p (r c)"), K.ps[:, 0, 0:72])
            link(v.tensor_copy(L[0:NSAMP, 2], K.ps[0:NSAMP, 0, 72:108]))
            G, E = L[:, :, 0:4], L[:, :, 4:36].rearrange("p r (g e) -> p r g e", g=4)
            first_max(G, st[:, 0], g[:, 0], g[:, 1], 4)
            v.tensor_tensor(g[:, 2], G, st[:, 0].unsqueeze(2).to_broadcast([P, 3, 4]), ALU.subtract).then_inc(s("rt_garg"), 1)
            link(v.tensor_tensor(gate[:, :, :, :], E, g[:, 0].unsqueeze(3).to_broadcast([P, 3, 4, 8]), ALU.mult))
            link(v.tensor_tensor(ee[:, 0], gate[:, :, 0, :], gate[:, :, 1, :], ALU.add))
            link(v.tensor_tensor(ee[:, 1], gate[:, :, 2, :], gate[:, :, 3, :], ALU.add))
            link(v.tensor_tensor(ee[:, 0], ee[:, 0], ee[:, 1], ALU.add))
            first_max(ee[:, 0], st[:, 1], ee[:, 1], ee[:, 2], 8)
            link(v.scalar_tensor_tensor(out=ee[:, 2], in0=ee[:, 1], scalar=-BIG, in1=ee[:, 0], op0=ALU.mult, op1=ALU.add))
            first_max(ee[:, 2], st[:, 2], ee[:, 3], ee[:, 4], 8)
            v.tensor_tensor(st[:, 3], st[:, 2], st[:, 1], ALU.subtract).then_inc(s("rt_darg"), 1)
            dve.wait_ge(s("rt_exp"), 1)
            link(v.tensor_reduce(st[:, 5], g[:, 3], AX.X, ALU.add))
            link(v.tensor_scalar(st[:, 6], st[:, 4], 1.0, None, ALU.add))
            link(v.tensor_tensor(st[:, 6], st[:, 6], st[:, 5], ALU.mult))
            link(v.reciprocal(st[:, 7], st[:, 6]))
            link(v.tensor_tensor(st[:, 8], st[:, 7], st[:, 4], ALU.mult))
            v.tensor_tensor(ee[:, 1], ee[:, 1], st[:, 7].unsqueeze(2).to_broadcast([P, 3, 8]), ALU.mult)
            link(v.tensor_tensor(ee[:, 3], ee[:, 3], st[:, 8].unsqueeze(2).to_broadcast([P, 3, 8]), ALU.mult))
            link(v.tensor_tensor(ee[:, 1], ee[:, 1], ee[:, 3], ALU.add))
            v.tensor_tensor(comb[:, :, :].rearrange("p r (g e) -> p r g e", g=4),
                            ee[:, 1].unsqueeze(2).to_broadcast([P, 3, 4, 8]),
                            g[:, 0].unsqueeze(3).to_broadcast([P, 3, 4, 8]), ALU.mult).then_inc(s("rt_comb"), 1)
            dve.wait_ge(s("rt_turned"), 1)
            v.tensor_copy(combT[:, :], K.ps[0:NEXP, 1, 0:T]).then_inc(s("rt_combT"), 1)

        @block.scalar
        def _(act):
            act.wait_ge(s("rt_garg"), 1)
            nc.scalar.activation(g[:, 3], g[:, 2], ACT.Exp)
            act.wait_ge(s("rt_darg"), 1)
            nc.scalar.activation(st[:, 4], st[:, 3], ACT.Exp).then_inc(s("rt_exp"), 1)


def experts_stage(K, l):
    nc, s = K.nc, K.sem
    with ExitStack() as e:
        sb = lambda n, sh: e.enter_context(nc.sbuf_tensor("t_" + n, sh, F32))
        wg, wd = sb("w_gate_up", [P, 2, KD, 2 * HID]), sb("w_down", [P, 2, 2, D])
        cb, hid = sb("moe_comb", [P, 2, T]), sb("moe_hid", [P, 2, 2, T])
        acc, tmp = sb("moe_acc", [P, KD, T]), sb("moe_tmp", [P, 2, T])
        block = e.enter_context(nc.Block(no_gpsimd_drain=True))

        @block.sync
        def _(sp):
            for i0, i1 in ((0, 1), (1, NEXP // 2)):
                with sp.Fori(i0, i1) as i:
                    for j in range(2):
                        if i0:
                            sp.wait_ge(s("moe_gu_done"), (i - 1) * 8 + 4 * j + 4)
                        sp.dma_start(wg[:, j], K.d["w_gate_up"][l, bass.ds(i * 2 + j, 1)].rearrange("o p k n -> p (o k) n")
                                     ).then_inc(s(f"moe_gu_loaded{j}"), 16)
                    for j in range(2):
                        if i0:
                            sp.wait_ge(s("moe_down_done"), (i - 1) * 8 + 8)
                            sp.wait_ge(s("moe_hid"), (i - 1) * 4 + 4)
                        sp.dma_start(wd[:, j], K.d["w_down"][l, bass.ds(i * 2 + j, 1)].rearrange("o p k n -> p (o k) n")
                                     ).then_inc(s(f"moe_down_loaded{j}"), 16)
                        sp.dma_start(cb[:, j], K.d["combine"][bass.ds(i * 2 + j, 1), :].to_broadcast([P, T])
                                     ).then_inc(s(f"moe_comb_loaded{j}"), 16)

        @block.tensor
        def _(pe):
            for i0, i1 in ((0, 1), (1, NEXP // 2)):
                with pe.Fori(i0, i1) as i:
                    for j in range(2):
                        pe.wait_ge(s(f"moe_gu_loaded{j}"), i * 16 + 16)
                        for f in range(2):
                            if i0 or j:
                                pe.wait_ge(s("moe_hid"), i * 4 + 2 * j + f - 1)
                            for g in range(2):
                                for k in range(KD):
                                    mm = pe.matmul(K.ps[:, 2 * f + g, 0:T], wg[:, j, k, g * HID + f * P:g * HID + (f + 1) * P],
                                                   K.h[:, k, :], start=(k == 0), stop=(k == KD - 1))
                                mm.then_inc(s("moe_gu_done"), 1)
                    for j in range(2):
                        pe.wait_ge(s(f"moe_down_loaded{j}"), i * 16 + 16)
                    pe.wait_ge(s("moe_hid"), i * 4 + 4)
                    for m in range(KD):
                        if i0 or m >= 4:
                            pe.wait_ge(s("moe_down_read"), i * 8 + m - 3)
                        for j in range(2):
                            for f in range(2):
                                mm = pe.matmul(K.ps[:, 4 + m % 4, 0:T], wd[:, j, f, m * P:(m + 1) * P], hid[:, j, f, :],
                                               start=(j + f == 0), stop=(j + f == 2))
                        mm.then_inc(s("moe_down_done"), 1)

        @block.scalar
        def _(act):
            for i0, i1 in ((0, 1), (1, NEXP // 2)):
                with act.Fori(i0, i1) as i:
                    for j in range(2):
                        for f in range(2):
                            act.wait_ge(s("moe_gu_done"), i * 8 + 4 * j + 2 * f + 1)
                            if i0:
                                act.wait_ge(s("moe_down_done"), (i - 1) * 8 + 8)
                            nc.scalar.activation(hid[:, j, f, :], K.ps[:, 2 * f, 0:T], ACT.Silu).then_inc(s("moe_silu"), 1)

        @block.vector
        def _(dve):
            v, link = nc.vector, lambda ins: K.vc.link(dve, ins)
            link(v.memset(acc[:, :, :], 0.0))
            with dve.Fori(0, NEXP // 2) as i:
                for j in range(2):
                    dve.wait_ge(s(f"moe_comb_loaded{j}"), i * 16 + 16)
                    for f in range(2):
                        n = 2 * j + f
                        dve.wait_ge(s("moe_silu"), i * 4 + n + 1)
                        dve.wait_ge(s("moe_gu_done"), i * 8 + 2 * n + 2)
                        v.tensor_tensor(hid[:, j, f, :], hid[:, j, f, :], K.ps[:, 2 * f + 1, 0:T], ALU.mult
                                        ).then_inc(s("moe_gated"), 1)
                        dve.wait_ge(s("moe_gated"), i * 4 + n + 1)
                        v.tensor_tensor(hid[:, j, f, :], hid[:, j, f, :], cb[:, j, :], ALU.mult).then_inc(s("moe_hid"), 1)
                for m in range(KD):
                    dve.wait_ge(s("moe_down_done"), i * 8 + m + 1)
                    v.tensor_tensor(acc[:, m, :], acc[:, m, :], K.ps[:, 4 + m % 4, 0:T], ALU.add).then_inc(s("moe_down_read"), 1)
            dve.wait_ge(s("moe_down_read"), KD * NEXP // 2)
            for m in range(KD):
                residual(K, dve, acc[:, m, :], tmp[:, m % 2], 40 + m, m, s("moe_residual"), m + 1)


def build(nc, d, n_pool):
    K = Core()
    K.nc, K.d, K.n_pool = nc, d, n_pool
    with ExitStack() as ctx:
        def sb(name, shape, dt=F32):
            return ctx.enter_context(nc.sbuf_tensor("s_" + name, shape, dt))

        once = {n: ctx.enter_context(nc.semaphore(n)) for n in ("consts_loaded", "silu_c_ready")}
        phase_sems, phase = {}, [ExitStack()]

        def sem(name):
            if name not in phase_sems:
                phase_sems[name] = phase[0].enter_context(nc.semaphore(name))
            return phase_sems[name]

        def end_phase():
            with nc.Block(no_gpsimd_drain=True) as block:
                @block.sync
                def _(sp):
                    for semaphore in phase_sems.values():
                        sp.sem_clear(semaphore)
            phase_sems.clear()
            phase[0].close()
            phase[0] = ExitStack()
            K.vc, K.ac = Chain(sem("dve_step")), Chain(sem("act_step"))

        K.sem = sem
        K.ps = ctx.enter_context(nc.psum_tensor("ps", [P, 8, 512], F32))
        K.x, K.h, K.proj = sb("x", [P, KD, T]), sb("h", [P, KD, T]), sb("proj", [P, NPROJ, T])
        K.dt, K.acs, K.wend, K.krope = sb("dt", [NH, T]), sb("acs", [NH, T]), sb("wend", [NH, T]), sb("krope", [ROPE, T])
        K.acol = sb("acol", [NH, 1])
        K.cols, K.mod, K.gain = sb("cols", [P, NCOLS]), sb("mod", [P, 48, NREQ]), sb("gain", [P, 2, 8, NREQ])
        K.silu_c, K.fin, K.table = sb("silu_c", [P, KD, NREQ]), sb("fin", [P, KD]), sb("table", [1, NB * NPAGE], I32)
        consts = {}
        for name, arr in constants().items():
            if name == "mask":
                continue
            consts[name] = sb("k_" + name, list(arr.shape))
        K.ident, K.ones, K.causal, K.keep = (consts[n] for n in ("ident", "ones", "causal", "keep"))
        K.selhead, K.selpair, K.ownb, K.own = (consts[n] for n in ("selhead", "selpair", "ownb", "own"))
        K.cos, K.sin, K.turn, K.eye = (consts[n] for n in ("cos", "sin", "turn", "eye"))
        K.later, K.iota = consts["later"], consts["iota"]
        with nc.Block(no_gpsimd_drain=True) as block:
            @block.sync
            def _(sp):
                for dst, name in ((K.x, "x"), (K.silu_c, "c"), (K.fin, "fin"), (K.table, "table")):
                    sp.dma_start(whole(dst), d[name]).then_inc(once["consts_loaded"], 16)
                for name, dst in consts.items():
                    sp.dma_start(whole(dst), d["k_" + name]).then_inc(once["consts_loaded"], 16)
                sp.wait_ge(once["consts_loaded"], 16 * (4 + len(consts)))

            @block.scalar
            def _(act):
                act.wait_ge(once["consts_loaded"], 16 * (4 + len(consts)))
                nc.scalar.activation(K.silu_c[:, :, :], K.silu_c[:, :, :], ACT.Silu).then_inc(once["silu_c_ready"], 1)
                act.wait_ge(once["silu_c_ready"], 1)
        with nc.Fori(0, DEPTH) as l:
            K.vc, K.ac = Chain(sem("dve_step")), Chain(sem("act_step"))
            modulation_stage(K, l)
            norm_stage(K, 0, "n1")
            projection_stage(K, l)
            conv_stage(K, l)
            ssd_stage(K, l)
            with ExitStack() as e:
                G = Core()
                G.b, G.k, G.A = (e.enter_context(nc.sbuf_tensor(n, [P, 4, T], F32)) for n in ("hg_b", "hg_k", "hg_A"))
                G.A01 = e.enter_context(nc.sbuf_tensor("u_hg_A01", [P, 4, P], F32))
                G.eye = K.eye
                hgrn_gates_stage(K, l, G)
                hgrn_scores_stage(K, l, G)
                hgrn_output_stage(K, l, G)
            end_phase()
            with ExitStack() as e:
                A = Core()
                A.qa = e.enter_context(nc.sbuf_tensor("u_mla_qa", [P, 2, MH, T], F32))
                A.ckv = e.enter_context(nc.sbuf_tensor("u_mla_ckv", [P, 3, 256], F32))
                A.qr = K.proj[0:ROPE, HI0:HI0 + MH, :]
                mla_project_stage(K, l, A)
                mla_prompt_stage(K, l, A)
                mla_sample_stage(K, l, A)
                mla_value_stage(K, l, A)
            lru_stage(K, l)
            merge_stage(K, l)
            norm_stage(K, 1, "n2")
            router_stage(K, l)
            experts_stage(K, l)
            end_phase()
        norm_stage(K, 2, "nf")
        with nc.Block(no_gpsimd_drain=True) as block:
            @block.sync
            def _(sp):
                sp.dma_start(d["o_y"], K.h[:, :, :]).then_inc(sem("y_stored"), 16)
                sp.wait_ge(sem("y_stored"), 16)


def whole(t):
    return t[tuple(slice(None) for _ in t.shape)]


def constants():
    f = np.float32
    i, j = np.arange(P)[:, None], np.arange(P)[None, :]
    own64 = (i[:64] // TS == j[:, :64] // TS)
    causal = np.zeros((P, SEQ + P + NSAMP), f)
    causal[:, 0:P] = j >= i
    causal[:, P:SEQ] = 1
    causal[:, SEQ:SEQ + P] = j >= i
    causal[:64, SEQ + P:] = own64 & (j[:, :64] >= i[:64])
    selhead = np.zeros((NH, NH, P), f)
    selpair = np.zeros((NH, 4, P), f)
    for h in range(NH):
        selhead[h, h, :] = 1
        selpair[h, h // 2, 64 * (h % 2):64 * (h % 2) + 64] = 1
    keep = np.ones((P, T), f)
    keep[:, 0] = 0
    keep[:, SEQ::TS] = 0
    ownb = (np.arange(NSAMP)[:, None] // TS == np.arange(NB)[None, :]).astype(f)
    pos = np.concatenate([np.arange(SEQ), PAST + np.arange(NSAMP) % TS]).astype(f)
    half = ROPE // 2
    inv = (f(10000.0) ** (-np.arange(half, dtype=f) * f(2.0) / f(ROPE))).astype(f)
    ang = (pos[None, :] * inv[:, None]).astype(f)
    cos, sin = (np.concatenate([g(ang), g(ang)]).astype(f) for g in (np.cos, np.sin))
    turn = np.zeros((ROPE, ROPE), f)
    for n in range(half):
        turn[n + half, n] = -1
        turn[n, n + half] = 1
    eye = np.zeros((P, T), f)
    mask = np.zeros((P, len(HG_LEVELS) - 1, T), np.int32)
    for t0, n in ((0, P), (P, P), (SEQ, NSAMP)):
        a, b = i[:n], j[:, :n]
        eye[:n, t0:t0 + n] = a == b
        for q, L in enumerate(HG_LEVELS[:-1]):
            mask[:n, q, t0:t0 + n] = (a // L == b // L) & (a % L < L // 2) & (b % L >= L // 2)
    later = np.where(j > i, f(-BIG), f(0)).astype(f)
    own = np.full((NSAMP, NB, NSAMP), -BIG, f)
    for b in range(NB):
        for h in range(MH):
            for t in range(TS):
                own[h * TS + t, b, b * TS:b * TS + t + 1] = 0
    iota = np.tile(np.arange(8, dtype=f), (P, 1))
    return dict(ident=np.eye(P, dtype=f), ones=np.ones((P, P), f), causal=causal, selhead=selhead, selpair=selpair,
                keep=keep, ownb=ownb, cos=cos, sin=sin, turn=turn, eye=eye, mask=mask, later=later, own=own, iota=iota)


OUTS = {"o_y": (P, KD, T), "o_conv": (DEPTH, P, 10, NREQ, 3), "o_ssm": (DEPTH, P, 4, NREQ, NST),
        "o_hgrn": (DEPTH, 4, P, NREQ, P), "o_ckv": (DEPTH, P, 2, T), "o_krope": (DEPTH, ROPE, T),
        "o_lru": (DEPTH, P, 4, NREQ)}


def lay_out(w):
    A = {k: np.asarray(v) for k, v in w.items()}
    Lr = DEPTH
    fm = lambda a: np.moveaxis(a.reshape(*a.shape[:-1], a.shape[-1] // P, P), (-1, -2), (0, 1))
    d = {}
    d["x"] = fm(np.concatenate([A["x_prompt"].reshape(SEQ, D), A["x_sample"].reshape(NSAMP, D)]))
    d["c"] = fm(np.concatenate([A["c_prompt"], A["c_sample"]]))
    d["fin"] = A["final_norm_g"].reshape(KD, P).T
    d["table"] = A["page_table"].reshape(1, NB * NPAGE)
    rows = lambda a: a.reshape(Lr, -1, P).transpose(0, 2, 1)
    first = np.zeros((Lr, P, 1), np.float32)
    first[1:] = 1
    taps = np.concatenate([A["ssd_conv_w"], A["lru_conv_w"]], axis=2).reshape(Lr, 4, 10, P).transpose(0, 3, 2, 1).reshape(Lr, P, 40)
    head = np.zeros((Lr, P, 2), np.float32)
    head[:, :NH, 0] = A["ssd_dt_bias"]
    head[:, :NH, 1] = A["ssd_a_log"]
    hg = rows(A["hg_lb_raw"])
    hg0, hg1 = np.stack([hg[0]] * Lr), np.stack([hg[1]] * Lr)
    dsk = np.broadcast_to(A["ssd_d"].reshape(Lr, 4, 2, 1), (Lr, 4, 2, 64)).reshape(Lr, 4, P).transpose(0, 2, 1)
    d["cols"] = np.concatenate([
        rows(A["norm1_g"]), rows(A["norm2_g"]), rows(A["b_mod"]), taps,
        rows(np.concatenate([A["ssd_conv_b"], A["lru_conv_b"]], axis=1)), rows(A["ssd_norm_g"]), hg0, hg1, first,
        rows(A["hg_norm_g"]), rows(A["mla_q_norm_g"]), rows(A["mla_kv_norm_g"]), rows(A["lru_b_r"]), rows(A["lru_b_i"]),
        rows(A["lru_a"]), dsk, head], axis=2)
    panels = lambda a, n: a.reshape(Lr, a.shape[1] // P, P, a.shape[2] // n, n).transpose(0, 3, 2, 1, 4)
    d["w_mod"] = panels(A["w_mod"], 512)
    W = A["w_in"]
    d["w_in"] = panels(np.concatenate([W[:, :, 0:1280], W[:, :, 1288:3848], W[:, :, 3880:]], axis=2), 256)
    d["w_small"] = np.concatenate([W[:, :, 1280:1288], W[:, :, 3848:3880]], axis=2).reshape(Lr, KD, P, 40).transpose(0, 2, 1, 3)
    st = np.concatenate([A["state_ssm_conv"], A["state_lru_conv"]], axis=3)
    d["conv_state"] = st.reshape(Lr, NB, 3, 10, P).transpose(0, 4, 3, 1, 2)
    S = A["state_ssm"]
    d["ssm_T"] = S.reshape(Lr, NB, 2, 4, HD, NST).transpose(0, 2, 5, 1, 3, 4).reshape(Lr, P, NB, 256)
    d["ssm_P"] = S.reshape(Lr, NB, 4, 2, HD, NST).transpose(0, 3, 4, 2, 1, 5).reshape(Lr, P, 4, NB, NST)
    d["hgrn"] = A["state_hgrn"].transpose(0, 2, 3, 1, 4)
    d["lru_state"] = A["state_lru"].reshape(Lr, NB, 4, P).transpose(0, 3, 2, 1)
    C, R = A["cache_kv_latent"], A["cache_k_rope"]
    n_pool = C.shape[1]
    pages = np.zeros((Lr, n_pool, P, 640), np.float32)
    pages[..., 0:256] = C.reshape(Lr, n_pool, P, 2, P).transpose(0, 1, 4, 3, 2).reshape(Lr, n_pool, P, 256)
    pages[:, :, 0:ROPE, 256:384] = R.transpose(0, 1, 3, 2)
    pages[..., 384:640] = C
    d["pages"] = pages
    d["w_uq"] = A["mla_w_uq"].reshape(Lr, 2, P, 768).transpose(0, 2, 1, 3)
    U = A["mla_w_ukv"].reshape(Lr, 256, MH, 128)
    d["w_uk"] = U[..., :64].transpose(0, 3, 2, 1)
    d["w_uv"] = U[..., 64:].reshape(Lr, 2, P, MH, 64).transpose(0, 2, 1, 3, 4)
    lw = np.zeros((Lr, P, 2, 4, P), np.float32)
    for n, name in enumerate(("lru_w_r", "lru_w_i")):
        B = A[name].reshape(Lr, 4, 2, 64, 64)
        for q in range(2):
            lw[:, 64 * q:64 * q + 64, n, :, 64 * q:64 * q + 64] = B[:, :, q].transpose(0, 2, 1, 3)
    d["lru_w"] = lw
    d["w_branch"] = A["w_branch"].reshape(Lr, 4, 4, P, 2, 512).transpose(0, 1, 4, 3, 2, 5).reshape(Lr, 8, P, 2048)
    d["w_out"] = A["w_out"].reshape(Lr, KD, P, 4, 256).transpose(0, 3, 2, 1, 4).reshape(Lr, 4, P, 2048)
    d["w_router"] = np.concatenate([A["moe_w_grp"], A["moe_w_rt"]], axis=2).reshape(Lr, KD, P, 36).transpose(0, 2, 1, 3)
    d["b_router"] = np.concatenate([A["moe_b_grp"], A["moe_b_rt"]], axis=1).reshape(Lr, 1, 36)
    GU = np.concatenate([A["moe_w_gate"], A["moe_w_up"]], axis=3)
    d["w_gate_up"] = GU.reshape(Lr, NEXP, KD, P, 2 * HID).transpose(0, 1, 3, 2, 4)
    d["w_down"] = A["moe_w_down"].reshape(Lr, NEXP, 2, P, D).transpose(0, 1, 3, 2, 4)
    for k, v in constants().items():
        d["k_" + k] = v
    return {k: np.ascontiguousarray(v) for k, v in d.items()}, n_pool


def outputs(r):
    y = r["o_y"].transpose(2, 1, 0).reshape(T, D)
    conv = r["o_conv"].transpose(0, 3, 4, 2, 1).reshape(DEPTH, NREQ, 3, 1280)
    ssm = r["o_ssm"].reshape(DEPTH, 2, HD, 4, NREQ, NST).transpose(0, 4, 3, 1, 2, 5).reshape(DEPTH, NREQ, NH, HD, NST)
    hgrn = r["o_hgrn"].transpose(0, 3, 1, 2, 4)
    ckv = r["o_ckv"].transpose(0, 3, 2, 1).reshape(DEPTH, T, 256)
    kr = r["o_krope"].transpose(0, 2, 1)
    lru = r["o_lru"].transpose(0, 3, 2, 1).reshape(DEPTH, NREQ, 512)
    res = [y[:SEQ].reshape(1, SEQ, D), y[SEQ:].reshape(NB, TS, D)]
    for sl, tok, shape in ((slice(0, 1), slice(0, SEQ), (DEPTH, 1, SEQ, -1)), (slice(1, NREQ), slice(SEQ, T), (DEPTH, NB, TS, -1))):
        res += [ckv[:, tok].reshape(shape), kr[:, tok].reshape(shape), ssm[:, sl], conv[:, sl, :, :768], hgrn[:, sl],
                lru[:, sl], conv[:, sl, :, 768:]]
    return tuple(np.ascontiguousarray(a) for a in res)


def kernel(**inputs):
    import concourse.bacc as bacc
    from concourse.bass_utils import run_bass_kernel_spmd

    nc = bacc.Bacc("TRN2", target_bir_lowering=False, num_devices=1)
    arrays, n_pool = lay_out(inputs)
    d = {n: nc.dram_tensor(n, a.shape, mybir.dt.from_np(a.dtype), kind="ExternalInput").ap() for n, a in arrays.items()}
    for n, shape in OUTS.items():
        d[n] = nc.dram_tensor(n, shape, F32, kind="ExternalOutput").ap()
    d["combine"] = nc.dram_tensor("combine", (NEXP, T), F32, kind="Internal").ap()
    build(nc, d, n_pool)
    r = run_bass_kernel_spmd(nc, [arrays], core_ids=[0])
    return outputs(r.results[0])
```

```python
from contextlib import ExitStack

import concourse.bass as bass
import numpy as np
from concourse import mybir

ALU = mybir.AluOpType
ACT = mybir.ActivationFunctionType
AX = mybir.AxisListType
F32 = mybir.dt.float32
I32 = mybir.dt.int32
U32 = mybir.dt.uint32

P = 128
DEPTH, D, SEQ, NB, TS = 2, 1024, 256, 8, 8
NSAMP = NB * TS
T = SEQ + NSAMP
KD = D // P
NREQ = 1 + NB
PAST, PAGE = 1024, 128
NPAGE = PAST // PAGE
EPS = 1e-6
NH, HD, NST = 8, 64, 64
HG_LEVELS = (2, 4, 8, 16, 32, 64, 128, 256)
MH, NOPE, ROPE = 8, 64, 32
ATT_SCALE = float((NOPE + ROPE) ** -0.5)
NEXP, HID = 32, 256
CAP, SLOTS = 64, 4
IN_SLOTS = 5
MAX_PASS = -(-T // CAP)
BIG = 1e30

Z0, XBC0, HQ0, HF0, HI0, HG0, QD0, KVD0, LX0, LY0, GL0 = 0, 4, 10, 14, 18, 22, 26, 28, 30, 34, 38
NPROJ = 70
C_N1, C_N2, C_BMOD, C_CW, C_CB, C_SSDN, C_HG0, C_HG1, C_SEL, C_HGN, C_QN, C_KVN, C_BR, C_BI, C_LA, C_DSK, C_DTB, C_ALOG = (
    0, 8, 16, 64, 104, 114, 118, 122, 126, 127, 128, 130, 132, 136, 140, 144, 148, 149)
NCOLS = 150


class Chain:

    def __init__(self, sem):
        self.sem, self.n = sem, 0

    def link(self, eng, ins):
        self.n += 1
        ins.then_inc(self.sem, 1)
        eng.wait_ge(self.sem, self.n)


class Core:
    pass


def prompt(ap):
    return ap[:, :, 0:SEQ]


def sample(ap):
    return ap[:, :, SEQ:T].rearrange("p k (b t) -> p k b t", t=TS)


def mod_product(K, pe, bank, silu_c, panel, first, last):
    for q in range(4):
        mm = pe.matmul(K.ps[32 * q:32 * q + NREQ, bank, :], silu_c, panel[:, q * 512:(q + 1) * 512], start=first, stop=last)
    return mm


def spare_panel(wmod):
    return wmod[:, 2, 0:1024].rearrange("p (n c) -> p n c", n=2)


def mod_rows(K, dst, bank, part):
    for q in range(4):
        ins = K.nc.vector.tensor_copy(dst[32 * q:32 * q + NREQ, part, :], K.ps[32 * q:32 * q + NREQ, bank, :])
    return ins


def mod_turn(K, pe, rows, part, bank):
    for m in range(4):
        mm = pe.transpose(K.ps[:, bank, m * P:(m + 1) * P], rows[:, part, m * P:(m + 1) * P], K.ident[:, :])
    return mm


def mod_add_bias(K, bank, i):
    return K.nc.vector.tensor_tensor(
        K.mod[:, 16 * i:16 * i + 16, :].rearrange("p (q m) r -> p q m r", q=4),
        K.ps[:, bank, :].rearrange("p (m q r) -> p q m r", m=4, q=4)[:, :, :, 0:NREQ],
        K.cols[:, C_BMOD + 16 * i:C_BMOD + 16 * i + 16].rearrange("p (q m) -> p q m", q=4).unsqueeze(3
                                                                 ).to_broadcast([P, 4, 4, NREQ]), ALU.add)


def norm_gain(K, n, c):
    return K.nc.vector.scalar_tensor_tensor(out=K.gain[:, n], in0=K.mod[:, 24 * n + 8:24 * n + 16, :], scalar=1.0,
                                            in1=K.cols[:, c:c + 8].unsqueeze(2).to_broadcast([P, 8, NREQ]),
                                            op0=ALU.add, op1=ALU.mult)


def load_in_panel(K, sp, l, n, j, win):
    sp.dma_start(win[:, j], K.d["w_in"][l, n].rearrange("o p k n -> p (o k) n")).then_inc(K.sem(f"in_loaded{j}"), 16)


def load_late_mod(K, sp, l, k, wmod):
    for n in range(2):
        sp.dma_start(wmod[:, n], K.d["w_mod"][l, n + 1, k].rearrange("o p n -> p (o n)")).then_inc(K.sem(f"late_loaded{n}"), 16)


def first_norm_stage(K, l, win, wmod):
    nc, s = K.nc, K.sem
    rows = spare_panel(wmod)
    with nc.sbuf_tensor("n1_rstd_row", [P, T], F32) as rstd, nc.Block(no_gpsimd_drain=True) as block:
        @block.sync
        def _(sp):
            for k in range(KD):
                if k >= 4:
                    sp.wait_ge(s("mod_used"), k - 3)
                sp.dma_start(wmod[:, k % 4], K.d["w_mod"][l, 0, k]).then_inc(s(f"mod_loaded{k % 4}"), 16)
            for j in range(IN_SLOTS):
                load_in_panel(K, sp, l, slice(j, j + 1), j, win)
            sp.wait_ge(s("mod_used"), 6)
            load_late_mod(K, sp, l, slice(0, 1), wmod)

        @block.scalar
        def _(act):
            act.dma_start(K.cols[:, :], K.d["cols"][l]).then_inc(s("cols_loaded"), 16)
            act.wait_ge(s("n1_inv"), 1)
            nc.scalar.activation(rstd[:, :], rstd[:, :], ACT.Sqrt).then_inc(s("n1_rstd"), 1)

        @block.tensor
        def _(pe):
            pe.wait_ge(s("n1_squares"), 1)
            sum_over_partitions(K, pe, K.ps[:, 0, 0:T], [K.h[:, k, :] for k in range(KD)]).then_inc(s("n1_sum"), 1)
            for k in range(KD):
                pe.wait_ge(s(f"mod_loaded{k % 4}"), 16 * (k // 4 + 1))
                mod_product(K, pe, 1, K.silu_c[:, k, :], wmod[:, k % 4], k == 0, k == KD - 1).then_inc(s("mod_used"), 1)
            pe.wait_ge(s("mod_rows_copied"), 1)
            mod_turn(K, pe, rows, 0, 2).then_inc(s("mod_turned"), 1)

        @block.vector
        def _(dve):
            v, link = nc.vector, lambda ins: K.vc.link(dve, ins)
            v.tensor_tensor(K.h[:, :, :], K.x[:, :, :], K.x[:, :, :], ALU.mult).then_inc(s("n1_squares"), 1)
            dve.wait_ge(s("n1_sum"), 1)
            link(v.tensor_scalar(rstd[:, :], K.ps[:, 0, 0:T], 1.0 / D, EPS, ALU.mult, ALU.add))
            v.reciprocal(rstd[:, :], rstd[:, :]).then_inc(s("n1_inv"), 1)
            dve.wait_ge(s("n1_rstd"), 1)
            link(v.tensor_tensor(K.h[:, :, :], K.x[:, :, :], rstd[:, :].unsqueeze(1).to_broadcast([P, KD, T]), ALU.mult))
            dve.wait_ge(s("mod_used"), KD - 1)
            link(v.memset(rows[:, 0, :], 0.0))
            dve.wait_ge(s("mod_used"), KD)
            mod_rows(K, rows, 1, 0).then_inc(s("mod_rows_copied"), 1)
            dve.wait_ge(s("cols_loaded"), 16)
            dve.wait_ge(s("mod_turned"), 1)
            link(mod_add_bias(K, 2, 0))
            link(norm_gain(K, 0, C_N1))
            apply_gain_and_shift(K, link, 0)


def apply_gain_and_shift(K, link, n):
    v = K.nc.vector
    for op, a in ((ALU.mult, K.gain[:, n]), (ALU.add, K.mod[:, 24 * n:24 * n + 8, :])):
        v.tensor_tensor(prompt(K.h), prompt(K.h), a[:, :, 0:1].to_broadcast([P, KD, SEQ]), op)
        link(v.tensor_tensor(sample(K.h), sample(K.h), a[:, :, 1:NREQ].unsqueeze(3).to_broadcast([P, KD, NB, TS]), op))


def sum_over_partitions(K, pe, out, tiles, start=True):
    for n, tile in enumerate(tiles):
        mm = pe.matmul(out, K.ones[:, :], tile, start=(n == 0), stop=(n == len(tiles) - 1))
    return mm


def norm_stage(K, n, tag):
    nc, s = K.nc, K.sem
    with nc.sbuf_tensor(tag + "_rstd_row", [P, T], F32) as rstd, nc.Block(no_gpsimd_drain=True) as block:
        @block.vector
        def _(dve):
            v, link = nc.vector, lambda ins: K.vc.link(dve, ins)
            v.tensor_tensor(K.h[:, :, :], K.x[:, :, :], K.x[:, :, :], ALU.mult).then_inc(s(tag + "_squares"), 1)
            dve.wait_ge(s(tag + "_sum"), 1)
            link(v.tensor_scalar(rstd[:, :], K.ps[:, 0, 0:T], 1.0 / D, EPS, ALU.mult, ALU.add))
            v.reciprocal(rstd[:, :], rstd[:, :]).then_inc(s(tag + "_inv"), 1)
            dve.wait_ge(s(tag + "_rstd"), 1)
            link(v.tensor_tensor(K.h[:, :, :], K.x[:, :, :], rstd[:, :].unsqueeze(1).to_broadcast([P, KD, T]), ALU.mult))
            if n == 2:
                v.tensor_tensor(K.h[:, :, :], K.h[:, :, :], K.fin[:, :].unsqueeze(2).to_broadcast([P, KD, T]), ALU.mult)
                return
            apply_gain_and_shift(K, link, n)

        @block.tensor
        def _(pe):
            pe.wait_ge(s(tag + "_squares"), 1)
            sum_over_partitions(K, pe, K.ps[:, 0, 0:T], [K.h[:, k, :] for k in range(KD)]).then_inc(s(tag + "_sum"), 1)

        @block.scalar
        def _(act):
            act.wait_ge(s(tag + "_inv"), 1)
            nc.scalar.activation(rstd[:, :], rstd[:, :], ACT.Sqrt).then_inc(s(tag + "_rstd"), 1)


def projection_stage(K, l, win, wmod):
    nc, s = K.nc, K.sem
    SL, PB = IN_SLOTS, 5
    MOD, SMALL = 5, 7
    rows = spare_panel(wmod)
    with (nc.sbuf_tensor("u_wsmall", [P, KD, ROPE + NH], F32) as wsm, nc.sbuf_tensor("silu_c_k", [P, NREQ], F32) as silu_k,
          nc.Block(no_gpsimd_drain=True) as block):
        @block.sync
        def _(sp):
            with sp.Fori(1, 7) as i:
                for j in range(SL):
                    sp.wait_ge(s("in_evacuated"), (i - 1) * 2 * SL + 2 * j + 2)
                    load_in_panel(K, sp, l, bass.ds(i * SL + j, 1), j, win)
                sp.wait_ge(s("late_used"), i)
                load_late_mod(K, sp, l, bass.ds(i, 1), wmod)
            sp.wait_ge(s("late_used"), KD - 1)
            load_late_mod(K, sp, l, slice(KD - 1, KD), wmod)

        @block.scalar
        def _(act):
            act.dma_start(wsm[:, :, :], K.d["w_small"][l]).then_inc(s("small_loaded"), 16)
            nc.scalar.copy(silu_k[:, :], K.silu_c[:, 0, :]).then_inc(s("silu_k_ready"), 1)
            with act.Fori(1, KD) as k:
                act.wait_ge(s("late_used"), k)
                nc.scalar.copy(silu_k[:, :], K.silu_c[:, bass.ds(k, 1), :].rearrange("p o r -> p (o r)")
                               ).then_inc(s("silu_k_ready"), 1)

        @block.tensor
        def _(pe):
            def late_mod(k, first, last):
                pe.wait_ge(s("silu_k_ready"), k + 1)
                for n in range(2):
                    mm = mod_product(K, pe, MOD + n, silu_k[:, :], wmod[:, n], first, last)
                mm.then_inc(s("late_used"), 1)

            for i0, i1 in ((0, 1), (1, 7)):
                with pe.Fori(i0, i1) as i:
                    for t in range(2 * SL):
                        j, m = t // 2, t % 2
                        if m == 0:
                            pe.wait_ge(s(f"in_loaded{j}"), i * 16 + 16)
                        if i0 or t >= PB:
                            pe.wait_ge(s("in_evacuated"), i * 2 * SL + t - PB + 1)
                        for k in range(KD):
                            mm = pe.matmul(K.ps[:, t % PB, 0:T], win[:, j, k, m * P:(m + 1) * P], K.h[:, k, :],
                                           start=(k == 0), stop=(k == KD - 1))
                        mm.then_inc(s("in_tile_done"), 1)
                    for n in range(2):
                        pe.wait_ge(s(f"late_loaded{n}"), i * 16 + 16)
                    late_mod(i, i0 == 0, False)
            pe.wait_ge(s("small_loaded"), 16)
            for k in range(KD):
                mm = pe.matmul(K.ps[0:ROPE + NH, SMALL, 0:T], wsm[:, k, :], K.h[:, k, :], start=(k == 0), stop=(k == KD - 1))
            mm.then_inc(s("small_done"), 1)
            for n in range(2):
                pe.wait_ge(s(f"late_loaded{n}"), 16 * KD)
            late_mod(KD - 1, False, True)
            pe.wait_ge(s("late_rows_copied"), 1)
            pe.wait_ge(s("in_evacuated"), 14 * SL)
            mod_turn(K, pe, rows, 0, 0)
            mod_turn(K, pe, rows, 1, 1).then_inc(s("late_turned"), 1)

        @block.vector
        def _(dve):
            v, link = nc.vector, lambda ins: K.vc.link(dve, ins)
            link(v.memset(rows[:, :, :], 0.0))
            with dve.Fori(0, 7) as i:
                for t in range(2 * SL):
                    dve.wait_ge(s("in_tile_done"), i * 2 * SL + t + 1)
                    nc.vector.tensor_copy(K.proj[:, bass.ds(i * 2 * SL + t, 1), :], K.ps[:, t % PB:t % PB + 1, 0:T]
                                          ).then_inc(s("in_evacuated"), 1)
            dve.wait_ge(s("small_done"), 1)
            v.tensor_copy(K.krope[:, :], K.ps[0:ROPE, SMALL, 0:T])
            v.tensor_copy(K.dt[:, :], K.ps[ROPE:ROPE + NH, SMALL, 0:T])
            dve.wait_ge(s("late_used"), KD)
            mod_rows(K, rows, MOD, 0)
            mod_rows(K, rows, MOD + 1, 1).then_inc(s("late_rows_copied"), 1)
            dve.wait_ge(s("late_turned"), 1)
            mod_add_bias(K, 0, 1)
            link(mod_add_bias(K, 1, 2))
            norm_gain(K, 1, C_N2)


def conv_stage(K, l):
    nc, s = K.nc, K.sem
    W3, SEG = 3, TS + 3
    XL = W3 + SEQ + NB * SEG
    YL = XL - W3
    S0 = W3 + SEQ
    with (nc.sbuf_tensor("u_xx", [P, 10, XL], F32) as xx, nc.sbuf_tensor("conv_y", [P, 10, YL + 3], F32) as y,
          nc.sbuf_tensor("u_conv_in", [P, 10, NB, W3], F32) as cin, nc.sbuf_tensor("conv_out", [P, 10, NREQ, W3], F32) as cout,
          nc.sbuf_tensor("u_dt_tmp", [NH, 4, T], F32) as dtt,
          nc.Block(no_gpsimd_drain=True) as block):
        seg = xx[:, :, S0:XL].rearrange("p c (b t) -> p c b t", t=SEG)
        segy = y[:, :, S0:YL + 3].rearrange("p c (b t) -> p c b t", t=SEG)

        @block.sync
        def _(sp):
            sp.dma_start(cin[:, :, :, :], K.d["conv_state"][l]).then_inc(s("conv_in_loaded"), 16)
            sp.wait_ge(s("conv_out_ready"), 1)
            sp.dma_start(K.d["o_conv"][l], cout[:, :, :, :]).then_inc(s("conv_stored"), 16)
            sp.wait_ge(s("conv_stored"), 16)

        @block.vector
        def _(dve):
            v, link = nc.vector, lambda ins: K.vc.link(dve, ins)
            v.memset(xx[:, :, 0:W3], 0.0)
            for c0, n, p0 in ((0, 6, XBC0), (6, 4, LX0)):
                v.tensor_copy(xx[:, c0:c0 + n, W3:S0], prompt(K.proj)[:, p0:p0 + n, :])
                for b in range(NB):
                    v.tensor_copy(xx[:, c0:c0 + n, S0 + b * SEG + W3:S0 + (b + 1) * SEG],
                                  K.proj[:, p0:p0 + n, SEQ + b * TS:SEQ + (b + 1) * TS])
            dve.wait_ge(s("conv_in_loaded"), 16)
            link(v.tensor_copy(seg[:, :, :, 0:W3], cin[:, :, :, :]))
            v.tensor_copy(cout[:, :, 0, :], xx[:, :, SEQ:S0])
            v.tensor_copy(cout[:, :, 1:NREQ, :], seg[:, :, :, TS:SEG]).then_inc(s("conv_out_ready"), 1)
            for w in range(4):
                for c in range(10):
                    tap = K.cols[:, C_CW + 4 * c + w:C_CW + 4 * c + w + 1]
                    if w == 0:
                        ins = v.tensor_scalar(y[:, c, 0:YL], xx[:, c, 0:YL], tap, K.cols[:, C_CB + c:C_CB + c + 1],
                                              ALU.mult, ALU.add)
                    else:
                        ins = v.scalar_tensor_tensor(out=y[:, c, 0:YL], in0=xx[:, c, w:w + YL], scalar=tap,
                                                     in1=y[:, c, 0:YL], op0=ALU.mult, op1=ALU.add)
                link(ins)
            v.tensor_copy(prompt(K.proj)[:, LX0:LX0 + 4, :], y[:, 6:10, 0:SEQ])
            v.tensor_copy(sample(K.proj)[:, LX0:LX0 + 4], segy[:, 6:10, :, 0:TS]).then_inc(s("conv_done"), 1)
            dve.wait_ge(s("dt_ready"), 1)
            link(v.scalar_tensor_tensor(out=K.dt[:, :], in0=dtt[:, 0, :], scalar=0.0, in1=dtt[:, 2, :],
                                        op0=ALU.max, op1=ALU.add))
            link(v.tensor_scalar(dtt[:, 3, :], K.dt[:, :], K.acol[:, 0:1], -1.0, ALU.mult, ALU.mult))
            link(v.tensor_tensor_scan(K.acs[:, :], K.keep[0:NH, :], dtt[:, 3, :], 0.0, ALU.mult, ALU.add))
            v.tensor_tensor(dtt[:, 0, 0:SEQ], K.acs[:, SEQ - 1:SEQ].to_broadcast([NH, SEQ]), K.acs[:, 0:SEQ], ALU.subtract)
            ac = K.acs[:, SEQ:T].rearrange("p (b t) -> p b t", t=TS)
            v.tensor_tensor(dtt[:, 0, SEQ:T].rearrange("p (b t) -> p b t", t=TS),
                            ac[:, :, TS - 1:TS].to_broadcast([NH, NB, TS]), ac, ALU.subtract).then_inc(s("wend_arg"), 1)
            dve.wait_ge(s("wend_exp"), 1)
            v.tensor_tensor(K.wend[:, :], dtt[:, 1, :], K.dt[:, :], ALU.mult)

        @block.scalar
        def _(act):
            a, link = nc.scalar, lambda ins: K.ac.link(act, ins)
            link(a.activation(dtt[:, 0, :], K.dt[:, :], ACT.Identity, bias=K.cols[0:NH, C_DTB:C_DTB + 1]))
            link(a.activation(dtt[:, 1, :], dtt[:, 0, :], ACT.Abs))
            link(a.activation(K.acol[:, :], K.cols[0:NH, C_ALOG:C_ALOG + 1], ACT.Exp))
            link(a.activation(dtt[:, 1, :], dtt[:, 1, :], ACT.Exp, scale=-1.0))
            a.activation(dtt[:, 2, :], dtt[:, 1, :], ACT.Ln, bias=1.0).then_inc(s("dt_ready"), 1)
            act.wait_ge(s("wend_arg"), 1)
            a.activation(dtt[:, 1, :], dtt[:, 0, :], ACT.Exp).then_inc(s("wend_exp"), 1)
            act.wait_ge(s("conv_done"), 1)
            a.activation(prompt(K.proj)[:, XBC0:XBC0 + 6, :], y[:, 0:6, 0:SEQ], ACT.Silu)
            a.activation(sample(K.proj)[:, XBC0:XBC0 + 6], segy[:, 0:6, :, 0:TS], ACT.Silu)


def ssd_stage(K, l):
    nc, s = K.nc, K.sem
    REG = ((0, P, 0, SEQ, 0), (P, P, P, P, SEQ), (SEQ, NSAMP, SEQ, NSAMP, SEQ + P))
    SC = SEQ + P + NSAMP
    with ExitStack() as e:
        sb = lambda n, sh: e.enter_context(nc.sbuf_tensor("t_" + n, sh, F32))
        xT, bT, rT = sb("ssd_xT", [P, 3, 512]), sb("ssd_bT", [P, 3, P]), sb("ssd_rT", [P, 3, 3, NH])
        xdt, xw = sb("ssd_xdt", [P, 3, 512]), sb("ssd_xw", [P, 3, 512])
        bmask = sb("ssd_bmask", [NSAMP, 2, NB, NST])
        cbm = sb("ssd_cbm", [P, 2, SC])
        E, M = sb("ssd_E", [P, 2, SC]), sb("ssd_M", [P, 2, SC])
        h0T = sb("ssd_h0T", [P, NB, 256])
        h0 = sb("ssd_h0", [P, 4, NB, NST])
        hout = sb("ssd_hout", [P, 4, NREQ, NST])
        ep = sb("ssd_ep", [P, 4, NSAMP])
        zs, yi = sb("ssd_zs", [P, 4, T]), sb("ssd_yi", [P, 4, NSAMP])
        rstd = sb("ssd_rstd", [P, T])
        block = e.enter_context(nc.Block(no_gpsimd_drain=True))
        XB, BB, CB = K.proj[:, XBC0:XBC0 + 4], K.proj[:, XBC0 + 4], K.proj[:, XBC0 + 5]

        @block.sync
        def _(sp):
            sp.dma_start(h0T[:, :, :], K.d["ssm_T"][l]).then_inc(s("h0T_loaded"), 16)
            sp.dma_start(h0[:, :, :, :], K.d["ssm_P"][l]).then_inc(s("h0_loaded"), 16)
            sp.wait_ge(s("ssm_out_ready"), 1)
            sp.dma_start(K.d["o_ssm"][l], hout[:, :, :, :]).then_inc(s("ssm_stored"), 16)
            sp.wait_ge(s("ssm_stored"), 16)

        @block.tensor
        def _(pe):
            for r, (s0, n, _, _, _) in enumerate(REG):
                for c in range(4):
                    mm = pe.transpose(K.ps[0:n, r, c * P:(c + 1) * P], XB[:, c, s0:s0 + n], K.ident[:, :])
                mm = pe.transpose(K.ps[0:n, 3, r * P:(r + 1) * P], BB[:, s0:s0 + n], K.ident[:, :])
                for q, row in enumerate((K.acs, K.dt, K.wend)):
                    mm = pe.transpose(K.ps[0:n, 4, (r * 3 + q) * NH:(r * 3 + q + 1) * NH], row[:, s0:s0 + n],
                                      K.ident[0:NH, 0:NH])
            mm.then_inc(s("ssd_tm"), 1)
            for g in range(2):
                for s0, n, t0, m, c0 in REG:
                    mm = pe.matmul(K.ps[0:n, 5 + g, c0:c0 + m], BB[64 * g:64 * g + 64, s0:s0 + n],
                                   CB[64 * g:64 * g + 64, t0:t0 + m], start=True, stop=True)
            mm.then_inc(s("ssd_cb"), 1)
            for q in range(4):
                mm = pe.matmul(K.ps[:, 7, q * NSAMP:(q + 1) * NSAMP], K.selpair[:, q, :], K.acs[:, SEQ:T],
                               start=True, stop=True)
            mm.then_inc(s("ssd_acspair"), 1)
            pe.wait_ge(s("h0T_loaded"), 16)
            pe.wait_ge(s("ssd_ep"), 1)
            pe.wait_ge(s("ssd_tm_copied"), 1)
            for q in range(4):
                g = q // 2
                for b in range(NB):
                    mm = pe.matmul(K.ps[:, 7 - 3 * g, q * NSAMP + b * TS:q * NSAMP + (b + 1) * TS],
                                   h0T[64 * g:64 * g + 64, b, (q % 2) * P:(q % 2 + 1) * P],
                                   CB[64 * g:64 * g + 64, SEQ + b * TS:SEQ + (b + 1) * TS], start=True, stop=True)
            mm.then_inc(s("ssd_inter"), 1)
            for h in range(NH):
                if h >= 2:
                    pe.wait_ge(s("ssd_seg"), h - 1)
                pe.matmul(K.ps[:, h % 2, 0:T], K.selhead[:, h, :], K.acs[:, :], start=True, stop=True
                          ).then_inc(s("ssd_acsb"), 1)
                if h >= 1:
                    ssd_y(K, pe, h - 1, REG, xdt, M)
            ssd_y(K, pe, NH - 1, REG, xdt, M)
            pe.wait_ge(s("ssd_xw"), 1)
            for q in range(4):
                g = q // 2
                for r in range(2):
                    mm = pe.matmul(K.ps[:, 4, q * NST:(q + 1) * NST], xw[:, r, q * P:(q + 1) * P],
                                   bT[:, r, 64 * g:64 * g + 64], start=(r == 0), stop=(r == 1))
            mm.then_inc(s("ssd_state_p"), 1)
            for q in range(4):
                g = q // 2
                if q >= 2:
                    pe.wait_ge(s("ssd_state_used"), q - 1)
                pe.matmul(K.ps[:, 5 + q % 2, :], xw[0:NSAMP, 2, q * P:(q + 1) * P],
                          bmask[:, g].rearrange("p b n -> p (b n)"), start=True, stop=True).then_inc(s("ssd_state"), 1)
            pe.wait_ge(s("ssd_sq"), 1)
            sum_over_partitions(K, pe, K.ps[:, 7, 0:T], [zs[:, q, :] for q in range(4)]).then_inc(s("ssd_ss"), 1)

        @block.vector
        def _(dve):
            v, link = nc.vector, lambda ins: K.vc.link(dve, ins)
            v.memset(cbm[:, :, :], 0.0)
            v.memset(E[:, :, :], 0.0)
            v.memset(xT[:, 2, :], 0.0)
            link(v.memset(rT[:, 2], 0.0))
            dve.wait_ge(s("ssd_tm"), 1)
            v.tensor_copy(xT[:, 0:2, :], K.ps[:, 0:2, :])
            v.tensor_copy(xT[0:NSAMP, 2, :], K.ps[0:NSAMP, 2, :])
            v.tensor_copy(bT[:, 0:2, :].rearrange("p r n -> p (r n)"), K.ps[:, 3, 0:2 * P])
            v.tensor_copy(bT[0:NSAMP, 2, :], K.ps[0:NSAMP, 3, 2 * P:3 * P])
            v.tensor_copy(rT[:, 0:2].rearrange("p r q h -> p (r q h)"), K.ps[:, 4, 0:6 * NH])
            link(v.tensor_copy(rT[0:NSAMP, 2].rearrange("p q h -> p (q h)"), K.ps[0:NSAMP, 4, 6 * NH:9 * NH]))
            for out, q in ((xdt, 1), (xw, 2)):
                for r in range(3):
                    ins = v.tensor_tensor(out[:, r].rearrange("p (h d) -> p h d", h=NH),
                                          xT[:, r].rearrange("p (h d) -> p h d", h=NH),
                                          rT[:, r, q, :].unsqueeze(2).to_broadcast([P, NH, HD]), ALU.mult)
                if q == 1:
                    ins.then_inc(s("ssd_tm_copied"), 1)
            for g in range(2):
                ins = v.tensor_tensor(bmask[:, g], bT[0:NSAMP, 2, 64 * g:64 * g + 64].unsqueeze(1).to_broadcast([NSAMP, NB, NST]),
                                      K.ownb[:, :].unsqueeze(2).to_broadcast([NSAMP, NB, NST]), ALU.mult)
            ins.then_inc(s("ssd_xw"), 1)
            dve.wait_ge(s("ssd_cb"), 1)
            for g in range(2):
                v.tensor_tensor(cbm[:, g, 0:SEQ + P], K.ps[:, 5 + g, 0:SEQ + P], K.causal[:, 0:SEQ + P], ALU.mult)
                link(v.tensor_tensor(cbm[0:NSAMP, g, SEQ + P:SC], K.ps[0:NSAMP, 5 + g, SEQ + P:SC],
                                     K.causal[0:NSAMP, SEQ + P:SC], ALU.mult))
            dve.wait_ge(s("ssd_inter"), 1)
            for g in range(2):
                link(v.tensor_tensor(yi[:, 2 * g:2 * g + 2, :],
                                     K.ps[:, 7 - 3 * g, 2 * g * NSAMP:2 * (g + 1) * NSAMP].rearrange("p (q t) -> p q t", q=2),
                                     ep[:, 2 * g:2 * g + 2, :], ALU.mult))

            def decayed(h):
                dve.wait_ge(s("ssd_E"), h + 1)
                if h >= 2:
                    dve.wait_ge(s("ssd_y"), h - 1)
                v.tensor_tensor(M[:, h % 2, :], E[:, h % 2, :], cbm[:, h // 4, :], ALU.mult).then_inc(s("ssd_M"), 1)

            def pair_y(q):
                dve.wait_ge(s("ssd_y"), 2 * q + 2)
                link(v.scalar_tensor_tensor(out=K.proj[:, Z0 + q, :], in0=XB[:, q, :],
                                            scalar=K.cols[:, C_DSK + q:C_DSK + q + 1], in1=K.ps[:, 2 + q % 2, 0:T],
                                            op0=ALU.mult, op1=ALU.add))
                link(v.tensor_tensor(K.proj[:, Z0 + q, SEQ:T], K.proj[:, Z0 + q, SEQ:T], yi[:, q, :], ALU.add))
                v.tensor_tensor(K.proj[:, Z0 + q, :], K.proj[:, Z0 + q, :], zs[:, q, :], ALU.mult).then_inc(s("ssd_pair"), 1)

            dve.wait_ge(s("ssd_zs"), 1)
            for h in range(NH):
                dve.wait_ge(s("ssd_acsb"), h + 1)
                if h >= 2:
                    dve.wait_ge(s("ssd_M"), h - 1)
                for r, (s0, n, t0, m, c0) in enumerate(REG):
                    ins = v.tensor_scalar(E[0:n, h % 2, c0:c0 + m], K.ps[0:n, h % 2, t0:t0 + m], rT[0:n, r, 0, h:h + 1],
                                          0.0, ALU.subtract, ALU.min)
                ins.then_inc(s("ssd_seg"), 1)
                if h >= 1:
                    decayed(h - 1)
                if h >= 3 and h % 2:
                    pair_y(h // 2 - 1)
            decayed(NH - 1)
            pair_y(3)
            dve.wait_ge(s("ssd_pair"), 4)
            v.tensor_tensor(zs[:, :, :], K.proj[:, Z0:Z0 + 4, :], K.proj[:, Z0:Z0 + 4, :], ALU.mult).then_inc(s("ssd_sq"), 1)
            dve.wait_ge(s("h0_loaded"), 16)
            dve.wait_ge(s("ssd_state_p"), 1)
            link(v.tensor_copy(hout[:, :, 0, :], K.ps[:, 4, 0:4 * NST].rearrange("p (q n) -> p q n", q=4)))
            for q in range(4):
                end = ep[:, q, :].rearrange("p (b t) -> p b t", t=TS)[:, :, TS - 1:TS].to_broadcast([P, NB, NST])
                link(v.tensor_tensor(hout[:, q, 1:NREQ, :], h0[:, q], end, ALU.mult))
                dve.wait_ge(s("ssd_state"), q + 1)
                v.tensor_tensor(hout[:, q, 1:NREQ, :], hout[:, q, 1:NREQ, :],
                                K.ps[:, 5 + q % 2, :].rearrange("p (b n) -> p b n", b=NB), ALU.add
                                ).then_inc(s("ssd_state_used"), 1)
            dve.wait_ge(s("ssd_ss"), 1)
            link(v.tensor_scalar(rstd[:, :], K.ps[:, 7, 0:T], 1.0 / 512, EPS, ALU.mult, ALU.add))
            v.reciprocal(rstd[:, :], rstd[:, :]).then_inc(s("ssd_inv"), 1)
            dve.wait_ge(s("ssd_rstd"), 1)
            for q in range(4):
                v.scalar_tensor_tensor(out=K.proj[:, Z0 + q, :], in0=K.proj[:, Z0 + q, :],
                                       scalar=K.cols[:, C_SSDN + q:C_SSDN + q + 1], in1=rstd[:, :],
                                       op0=ALU.mult, op1=ALU.mult)
            dve.wait_ge(s("ssd_state_used"), 4)
            dve.sem_inc(s("ssm_out_ready"), 1)

        @block.scalar
        def _(act):
            a = nc.scalar
            a.activation(zs[:, :, :], K.proj[:, Z0:Z0 + 4, :], ACT.Silu).then_inc(s("ssd_zs"), 1)
            act.wait_ge(s("ssd_acspair"), 1)
            a.activation(ep[:, :, :].rearrange("p q t -> p (q t)"), K.ps[:, 7, 0:4 * NSAMP], ACT.Exp).then_inc(s("ssd_ep"), 1)
            for h in range(NH):
                act.wait_ge(s("ssd_seg"), h + 1)
                a.activation(E[:, h % 2, :], E[:, h % 2, :], ACT.Exp).then_inc(s("ssd_E"), 1)
            act.wait_ge(s("ssd_inv"), 1)
            a.activation(rstd[:, :], rstd[:, :], ACT.Sqrt).then_inc(s("ssd_rstd"), 1)


def ssd_y(K, pe, h, REG, xdt, M):
    q, s = h // 2, K.sem
    if h % 2 == 0 and q >= 2:
        pe.wait_ge(s("ssd_pair"), q - 1)
    pe.wait_ge(s("ssd_M"), h + 1)
    for r, (s0, n, t0, m, c0) in enumerate(REG):
        mm = pe.matmul(K.ps[64 * (h % 2):64 * (h % 2) + 64, 2 + q % 2, t0:t0 + m], xdt[0:n, r, h * HD:(h + 1) * HD],
                       M[0:n, h % 2, c0:c0 + m], start=(r != 1), stop=(r != 0))
    mm.then_inc(s("ssd_y"), 1)


def hgrn_gates_stage(K, l, G):
    nc, s = K.nc, K.sem
    with (nc.sbuf_tensor("u_hg_t", [P, 3, 4, T], F32) as t, nc.sbuf_tensor("hg_lb", [P, 4, 4], F32) as lb,
          nc.Block(no_gpsimd_drain=True) as block):
        x = K.proj[:, HF0:HF0 + 4, :]
        @block.scalar
        def _(act):
            a, link = nc.scalar, lambda ins: K.ac.link(act, ins)
            act.wait_ge(s("lb_diff"), 1)
            a.activation(lb[:, 3, :], lb[:, 3, :], ACT.Sigmoid).then_inc(s("lb_sig"), 1)
            a.activation(G.k[:, :, :], x, ACT.Sigmoid, scale=-1.0).then_inc(s("hg_sig"), 1)
            link(a.activation(t[:, 0], x, ACT.Abs))
            a.activation(t[:, 0], t[:, 0], ACT.Exp, scale=-1.0).then_inc(s("hg_eabs"), 1)
            act.wait_ge(s("hg_arg"), 1)
            a.activation(t[:, 1], t[:, 1], ACT.Exp)
            a.activation(t[:, 2], t[:, 2], ACT.Exp).then_inc(s("hg_e"), 1)
            act.wait_ge(s("hg_numer"), 1)
            a.activation(t[:, 1], t[:, 1], ACT.Ln).then_inc(s("hg_ln"), 1)
            act.wait_ge(s("hg_eabs"), 1)
            a.activation(t[:, 0], t[:, 0], ACT.Ln, bias=1.0).then_inc(s("hg_ln"), 1)

        @block.vector
        def _(dve):
            v, link = nc.vector, lambda ins: K.vc.link(dve, ins)
            bc = lambda c: c.unsqueeze(2).to_broadcast([P, 4, T])
            v.tensor_tensor(lb[:, 3, :], K.cols[:, C_HG1:C_HG1 + 4], K.cols[:, C_HG0:C_HG0 + 4], ALU.subtract
                            ).then_inc(s("lb_diff"), 1)
            v.tensor_scalar(t[:, 1], x, 0.0, None, ALU.min)
            v.tensor_scalar(t[:, 2], x, 0.0, -1.0, ALU.max, ALU.mult).then_inc(s("hg_arg"), 1)
            dve.wait_ge(s("lb_sig"), 1)
            link(v.tensor_scalar(lb[:, 0, :], lb[:, 3, :], K.cols[:, C_SEL:C_SEL + 1], None, ALU.mult))
            v.tensor_scalar(lb[:, 1, :], lb[:, 0, :], -1.0, 1.0, ALU.mult, ALU.add)
            link(v.tensor_scalar(lb[:, 2, :], lb[:, 0, :], 0.0, None, ALU.is_equal))
            dve.wait_ge(s("hg_sig"), 1)
            v.tensor_tensor(G.k[:, :, :], G.k[:, :, :], bc(lb[:, 1, :]), ALU.mult)
            dve.wait_ge(s("hg_e"), 1)
            link(v.tensor_tensor(t[:, 2], t[:, 2], bc(lb[:, 0, :]), ALU.mult))
            link(v.tensor_tensor(t[:, 1], t[:, 1], t[:, 2], ALU.add))
            v.tensor_scalar(t[:, 1], t[:, 1], LN_FLOOR, None, ALU.max).then_inc(s("hg_numer"), 1)
            dve.wait_ge(s("hg_numer"), 1)
            link(v.tensor_scalar(t[:, 2], x, -LOG_LN_FLOOR, 0.0, ALU.add, ALU.min))
            link(v.tensor_tensor(t[:, 2], t[:, 2], bc(lb[:, 2, :]), ALU.mult))
            dve.wait_ge(s("hg_ln"), 2)
            link(v.tensor_tensor(t[:, 1], t[:, 1], t[:, 0], ALU.subtract))
            link(v.tensor_tensor(t[:, 1], t[:, 1], t[:, 2], ALU.add))
            for h in range(4):
                v.tensor_tensor_scan(G.b[:, h, :], K.keep[:, :], t[:, 1, h, :], 0.0, ALU.mult, ALU.add)


def hgrn_scores_stage(K, l, G):
    nc, s = K.nc, K.sem
    TILES = ((0, P), (P, P), (SEQ, NSAMP))
    with (nc.sbuf_tensor("u_hg_D", [P, 2, 4, T], F32) as Dk, nc.sbuf_tensor("hg_mask", [P, len(HG_LEVELS) - 1, T], I32) as mask,
          nc.Block(no_gpsimd_drain=True) as block):
        q = K.proj[:, HQ0:HQ0 + 4, :]
        NL = len(HG_LEVELS)

        @block.sync
        def _(sp):
            sp.dma_start(mask[:, :, :], K.d["k_mask"]).then_inc(s("hg_mask_loaded"), 16)

        def halves(ap, L):
            if L <= TS:
                w = ap.rearrange("p h (n c) -> p (h n) c", c=L)
            else:
                w = ap[:, :, 0:SEQ].rearrange("p h (n c) -> p h n c", c=L)
            if L <= TS:
                return w[:, :, 0:L // 2], w[:, :, L // 2:L], w[:, :, L // 2 - 1:L // 2].to_broadcast([P, 4 * T // L, L // 2])
            return (w[:, :, :, 0:L // 2], w[:, :, :, L // 2:L],
                    w[:, :, :, L // 2 - 1:L // 2].to_broadcast([P, 4, SEQ // L, L // 2]))

        def width(L):
            return T if L <= TS else SEQ

        @block.vector
        def _(dve):
            v, link = nc.vector, lambda ins: K.vc.link(dve, ins)
            link(v.memset(G.A[:, :, SEQ:T], 0.0))

            def decays(n):
                L = HG_LEVELS[n]
                if n >= 2:
                    dve.wait_ge(s("hg_gram"), n)
                b1, b2, ref = halves(G.b, L)
                d1, d2, _ = halves(Dk[:, n % 2], L)
                v.tensor_tensor(d1, ref, b1, ALU.subtract)
                v.tensor_tensor(d2, b2, ref, ALU.subtract).then_inc(s("hg_seg"), 1)

            decays(0)
            dve.wait_ge(s("hg_mask_loaded"), 16)
            dve.wait_ge(s("hg_gram"), 1)
            v.tensor_tensor(G.A[:, :, 0:SEQ], K.ps[:, 4:8, 0:SEQ], G.eye[:, 0:SEQ].unsqueeze(1).to_broadcast([P, 4, SEQ]), ALU.mult)
            link(v.tensor_tensor(G.A[0:NSAMP, :, SEQ:T], K.ps[0:NSAMP, 4:8, SEQ:T],
                                 G.eye[0:NSAMP, SEQ:T].unsqueeze(1).to_broadcast([NSAMP, 4, NSAMP]), ALU.mult))
            dve.sem_inc(s("hg_bank_free"), 1)
            for n, L in enumerate(HG_LEVELS):
                dve.wait_ge(s("hg_D"), n + 1)
                d1, d2, _ = halves(Dk[:, n % 2], L)
                k1, _, _ = halves(G.k, L)
                _, q2, _ = halves(q, L)
                v.tensor_tensor(d1, d1, k1, ALU.mult)
                v.tensor_tensor(d2, d2, q2, ALU.mult).then_inc(s("hg_W"), 1)
                if n + 1 < NL:
                    decays(n + 1)
                dve.wait_ge(s("hg_gram"), n + 2)
                B0 = 4 * (n % 2)
                if L == 256:
                    v.tensor_copy(G.A01[:, :, :], K.ps[:, B0:B0 + 4, 0:P])
                    continue
                m = mask[:, n, 0:SEQ].unsqueeze(1).to_broadcast([P, 4, SEQ])
                ins = v.copy_predicated(G.A[:, :, 0:SEQ], m, K.ps[:, B0:B0 + 4, 0:SEQ])
                if L <= TS:
                    m = mask[0:NSAMP, n, SEQ:T].unsqueeze(1).to_broadcast([NSAMP, 4, NSAMP])
                    ins = v.copy_predicated(G.A[0:NSAMP, :, SEQ:T], m, K.ps[0:NSAMP, B0:B0 + 4, SEQ:T])
                ins.then_inc(s("hg_bank_free"), 1)
                dve.wait_ge(s("hg_bank_free"), n + 2)

        @block.scalar
        def _(act):
            for n, L in enumerate(HG_LEVELS):
                act.wait_ge(s("hg_seg"), n + 1)
                w = Dk[:, n % 2, :, 0:width(L)]
                nc.scalar.activation(w, w, ACT.Exp).then_inc(s("hg_D"), 1)

        @block.tensor
        def _(pe):
            for h in range(4):
                for t0, n in TILES:
                    mm = pe.matmul(K.ps[0:n, 4 + h, t0:t0 + n], G.k[:, h, t0:t0 + n], q[:, h, t0:t0 + n], start=True, stop=True)
            mm.then_inc(s("hg_gram"), 1)
            for n, L in enumerate(HG_LEVELS):
                pe.wait_ge(s("hg_W"), n + 1)
                if n >= 1:
                    pe.wait_ge(s("hg_bank_free"), n)
                W = Dk[:, n % 2]
                for h in range(4):
                    if L == 256:
                        mm = pe.matmul(K.ps[:, 4 * (n % 2) + h, 0:P], W[:, h, 0:P], W[:, h, P:SEQ], start=True, stop=True)
                        continue
                    for t0, w in TILES[:3 if L <= TS else 2]:
                        mm = pe.matmul(K.ps[0:w, 4 * (n % 2) + h, t0:t0 + w], W[:, h, t0:t0 + w], W[:, h, t0:t0 + w],
                                       start=True, stop=True)
                mm.then_inc(s("hg_gram"), 1)


def hgrn_output_stage(K, l, G):
    nc, s = K.nc, K.sem
    REG = ((0, P), (P, P), (SEQ, NSAMP))
    with ExitStack() as e:
        sb = lambda n, sh: e.enter_context(nc.sbuf_tensor("t_" + n, sh, F32))
        vT, kwT = sb("hg_vT", [P, 3, 4, P]), sb("hg_kwT", [P, 3, 4, P])
        kw, qe = sb("hg_kw", [P, 4, T]), sb("hg_qe", [P, 4, NSAMP])
        vm, s0 = sb("hg_vm", [NSAMP, 2, NB, P]), sb("hg_s0", [P, 2, NB, P])
        sout = sb("hg_sout", [P, 2, NREQ, P])
        be, rstd = sb("hg_be", [P, 4, NB]), sb("hg_rstd", [P, 4, T])
        block = e.enter_context(nc.Block(no_gpsimd_drain=True))
        O = K.proj[:, HQ0:HQ0 + 4, :]

        @block.sync
        def _(sp):
            for h in range(4):
                if h >= 2:
                    sp.wait_ge(s("hg_state_ready"), h - 1)
                sp.dma_start(s0[:, h % 2], K.d["hgrn"][l, h]).then_inc(s(f"hg_s0_loaded{h % 2}"), 16)
            for h in range(4):
                sp.wait_ge(s("hg_state_ready"), h + 1)
                sp.dma_start(K.d["o_hgrn"][l, h], sout[:, h % 2]).then_inc(s(f"hg_stored{h % 2}"), 16)
            for j in range(2):
                sp.wait_ge(s(f"hg_stored{j}"), 32)

        @block.vector
        def _(dve):
            v, link = nc.vector, lambda ins: K.vc.link(dve, ins)
            bS = sample(G.b)
            v.tensor_copy(be[:, :, :], bS[:, :, :, TS - 1])
            v.tensor_tensor(prompt(kw), G.b[:, :, SEQ - 1:SEQ].to_broadcast([P, 4, SEQ]), prompt(G.b), ALU.subtract)
            v.tensor_tensor(sample(kw), bS[:, :, :, TS - 1:TS].to_broadcast([P, 4, NB, TS]), bS, ALU.subtract
                            ).then_inc(s("hg_kw_arg"), 1)
            dve.wait_ge(s("hg_kw_exp"), 1)
            v.tensor_tensor(qe[:, :, :], qe[:, :, :], O[:, :, SEQ:T], ALU.mult)
            v.tensor_tensor(kw[:, :, :], kw[:, :, :], G.k[:, :, :], ALU.mult).then_inc(s("hg_kw"), 1)
            for n, (dst, sig) in enumerate(((vT, "hg_vT"), (kwT, "hg_kwT"))):
                dve.wait_ge(s("hg_tm"), n + 1)
                v.tensor_copy(dst[:, 0:2].rearrange("p r h c -> p r (h c)"), K.ps[:, 0 + 3 * n:2 + 3 * n, :])
                v.tensor_copy(dst[0:NSAMP, 2].rearrange("p h c -> p (h c)"), K.ps[0:NSAMP, 2 + 3 * n, :]).then_inc(s(sig), 1)
            dve.wait_ge(s("hg_vT"), 1)
            for h in range(4):
                if h >= 2:
                    dve.wait_ge(s("hg_state"), h - 1)
                v.tensor_tensor(vm[:, h % 2], vT[0:NSAMP, 2, h].unsqueeze(1).to_broadcast([NSAMP, NB, P]),
                                K.ownb[:, :].unsqueeze(2).to_broadcast([NSAMP, NB, P]), ALU.mult).then_inc(s("hg_vm"), 1)
                dve.wait_ge(s(f"hg_s0_loaded{h % 2}"), 16 * (h // 2 + 1))
                if h >= 2:
                    dve.wait_ge(s(f"hg_stored{h % 2}"), 16 * (h // 2))
                link(v.tensor_tensor(sout[:, h % 2, 1:NREQ], s0[:, h % 2], be[:, h].unsqueeze(2).to_broadcast([P, NB, P]), ALU.mult))
                dve.wait_ge(s("hg_o"), h + 1)
                v.tensor_copy(O[:, h, :], K.ps[:, 0, 0:T]).then_inc(s("hg_o_copied"), 1)
                dve.wait_ge(s("hg_state"), h + 1)
                v.tensor_copy(sout[:, h % 2, 0], K.ps[:, 1, 0:P])
                so = sout[:, h % 2, 1:NREQ].rearrange("p (a b) n -> p a (b n)", a=2)
                v.tensor_tensor(so, so, K.ps[:, 2:4, :], ALU.add).then_inc(s("hg_state_ready"), 1)
            dve.wait_ge(s("hg_o_copied"), 4)
            v.tensor_tensor(kw[:, :, :], O, O, ALU.mult).then_inc(s("hg_sq"), 1)
            dve.wait_ge(s("hg_ss"), 1)
            link(v.tensor_scalar(rstd[:, :, :], K.ps[:, 4:8, 0:T], 1.0 / P, EPS, ALU.mult, ALU.add))
            v.reciprocal(rstd[:, :, :], rstd[:, :, :]).then_inc(s("hg_inv"), 1)
            dve.wait_ge(s("hg_rstd"), 1)
            link(v.scalar_tensor_tensor(out=O, in0=O, scalar=K.cols[:, C_HGN:C_HGN + 1], in1=rstd[:, :, :],
                                        op0=ALU.mult, op1=ALU.mult))
            v.tensor_tensor(O, O, K.proj[:, HG0:HG0 + 4, :], ALU.mult)

        @block.scalar
        def _(act):
            a = nc.scalar
            act.wait_ge(s("hg_kw_arg"), 1)
            a.activation(kw[:, :, :], kw[:, :, :], ACT.Exp)
            a.activation(qe[:, :, :], G.b[:, :, SEQ:T], ACT.Exp)
            a.activation(be[:, :, :], be[:, :, :], ACT.Exp).then_inc(s("hg_kw_exp"), 1)
            a.activation(K.proj[:, HG0:HG0 + 4, :], K.proj[:, HG0:HG0 + 4, :], ACT.Silu)
            act.wait_ge(s("hg_inv"), 1)
            a.activation(rstd[:, :, :], rstd[:, :, :], ACT.Sqrt).then_inc(s("hg_rstd"), 1)

        @block.tensor
        def _(pe):
            for h in range(4):
                for r, (t0, n) in enumerate(REG):
                    mm = pe.transpose(K.ps[0:n, r, h * P:(h + 1) * P], K.proj[:, HI0 + h, t0:t0 + n], K.ident[:, :])
            mm.then_inc(s("hg_tm"), 1)
            pe.wait_ge(s("hg_kw"), 1)
            for h in range(4):
                for r, (t0, n) in enumerate(REG):
                    mm = pe.transpose(K.ps[0:n, 3 + r, h * P:(h + 1) * P], kw[:, h, t0:t0 + n], K.ident[:, :])
            mm.then_inc(s("hg_tm"), 1)
            pe.wait_ge(s("hg_kwT"), 1)
            for h in range(4):
                if h >= 1:
                    pe.wait_ge(s("hg_o_copied"), h)
                    pe.wait_ge(s("hg_state_ready"), h)
                o = K.ps[:, 0, :]
                pe.matmul(o[:, 0:P], vT[:, 0, h], G.A[:, h, 0:P], start=True, stop=True)
                pe.matmul(o[:, P:SEQ], vT[:, 0, h], G.A01[:, h], start=True, stop=False)
                pe.matmul(o[:, P:SEQ], vT[:, 1, h], G.A[:, h, P:SEQ], start=False, stop=True)
                pe.wait_ge(s(f"hg_s0_loaded{h % 2}"), 16 * (h // 2 + 1))
                pe.matmul(o[:, SEQ:T], vT[0:NSAMP, 2, h], G.A[0:NSAMP, h, SEQ:T], start=True, stop=False)
                for b in range(NB):
                    mm = pe.matmul(o[:, SEQ + b * TS:SEQ + (b + 1) * TS], s0[:, h % 2, b], qe[:, h, b * TS:(b + 1) * TS],
                                   start=False, stop=(b == NB - 1))
                mm.then_inc(s("hg_o"), 1)
                pe.matmul(K.ps[:, 1, 0:P], kwT[:, 0, h], vT[:, 0, h], start=True, stop=False)
                pe.matmul(K.ps[:, 1, 0:P], kwT[:, 1, h], vT[:, 1, h], start=False, stop=True)
                pe.wait_ge(s("hg_vm"), h + 1)
                for j in range(2):
                    mm = pe.matmul(K.ps[:, 2 + j, :], kwT[0:NSAMP, 2, h],
                                   vm[:, h % 2, 4 * j:4 * j + 4].rearrange("p b n -> p (b n)"), start=True, stop=True)
                mm.then_inc(s("hg_state"), 1)
            pe.wait_ge(s("hg_sq"), 1)
            for h in range(4):
                mm = pe.matmul(K.ps[:, 4 + h, 0:T], K.ones[:, :], kw[:, h, :], start=True, stop=True)
            mm.then_inc(s("hg_ss"), 1)


LN_FLOOR = 1e-18
LOG_LN_FLOOR = -41.44653167389282


def mla_project_stage(K, l, A):
    nc, s = K.nc, K.sem
    with ExitStack() as e:
        sb = lambda n, sh: e.enter_context(nc.sbuf_tensor("t_" + n, sh, F32))
        wuq, wuk = sb("w_uq", [P, 2, 768]), sb("w_uk", [NOPE, MH, 256])
        sq, rstd = sb("mla_sq", [P, 4, T]), sb("mla_rstd", [P, 2, T])
        qn, rot = sb("mla_qn", [NOPE, 2, T]), sb("mla_rot", [ROPE, 2, T])
        block = e.enter_context(nc.Block(no_gpsimd_drain=True))
        C = K.proj[:, QD0:QD0 + 4, :]

        @block.sync
        def _(sp):
            sp.dma_start(wuq[:, :, :], K.d["w_uq"][l]).then_inc(s("uq_loaded"), 16)
            sp.dma_start(wuk[:, :, :], K.d["w_uk"][l]).then_inc(s("uk_loaded"), 16)
            sp.wait_ge(s("mla_normed"), 1)
            sp.dma_start(K.d["o_ckv"][l], K.proj[:, KVD0:KVD0 + 2, :]).then_inc(s("ckv_stored"), 16)
            sp.wait_ge(s("krope_ready"), 1)
            sp.dma_start(K.d["o_krope"][l], K.krope[:, :]).then_inc(s("krope_stored"), 16)
            sp.wait_ge(s("ckv_stored"), 16)
            sp.wait_ge(s("krope_stored"), 16)

        @block.vector
        def _(dve):
            v, link = nc.vector, lambda ins: K.vc.link(dve, ins)
            v.tensor_tensor(sq[:, :, :], C, C, ALU.mult).then_inc(s("mla_sq"), 1)
            dve.wait_ge(s("mla_ss"), 1)
            link(v.tensor_scalar(rstd[:, :, :], K.ps[:, 0:2, 0:T], 1.0 / 256, EPS, ALU.mult, ALU.add))
            v.reciprocal(rstd[:, :, :], rstd[:, :, :]).then_inc(s("mla_inv"), 1)
            dve.wait_ge(s("mla_rstd"), 1)
            for c in range(4):
                ins = v.scalar_tensor_tensor(out=C[:, c], in0=C[:, c], scalar=K.cols[:, C_QN + c:C_QN + c + 1],
                                             in1=rstd[:, c // 2, :], op0=ALU.mult, op1=ALU.mult)
            ins.then_inc(s("mla_normed"), 1)
            dve.wait_ge(s("krope_turned"), 1)
            link(v.tensor_tensor(rot[:, 0], K.ps[0:ROPE, 2, 0:T], K.sin[:, :], ALU.mult))
            link(v.tensor_tensor(K.krope[:, :], K.krope[:, :], K.cos[:, :], ALU.mult))
            v.tensor_tensor(K.krope[:, :], K.krope[:, :], rot[:, 0], ALU.add).then_inc(s("krope_ready"), 1)
            dve.wait_ge(s("ckv_tm"), 1)
            for r, n in enumerate((P, P, NSAMP)):
                v.tensor_copy(A.ckv[0:n, r, :], K.ps[0:n, 3 + r, 0:256])
            dve.sem_inc(s("ckv_tm_copied"), 1)
            for h in range(MH):
                if h >= 2:
                    dve.wait_ge(s("q_abs_done"), h - 1)
                dve.wait_ge(s("q_head_done"), h + 1)
                v.tensor_copy(qn[:, h % 2], K.ps[0:NOPE, 0, 0:T]).then_inc(s("q_nope_copied"), 1)
                v.tensor_copy(A.qr[:, h], K.ps[0:ROPE, 1, 0:T]).then_inc(s("q_rope_copied"), 1)
                dve.wait_ge(s("q_abs_done"), h + 1)
                v.tensor_copy(A.qa[:, :, h, :], K.ps[:, 3:5, 0:T]).then_inc(s("q_abs_copied"), 1)
                dve.wait_ge(s("q_turned"), h + 1)
                v.tensor_tensor(rot[:, h % 2], K.ps[0:ROPE, 2, 0:T], K.sin[:, :], ALU.mult).then_inc(s("q_turned_read"), 1)
                link(v.tensor_tensor(A.qr[:, h], A.qr[:, h], K.cos[:, :], ALU.mult))
                dve.wait_ge(s("q_turned_read"), h + 1)
                v.tensor_tensor(A.qr[:, h], A.qr[:, h], rot[:, h % 2], ALU.add)

        @block.scalar
        def _(act):
            act.wait_ge(s("mla_inv"), 1)
            nc.scalar.activation(rstd[:, :, :], rstd[:, :, :], ACT.Sqrt).then_inc(s("mla_rstd"), 1)

        @block.tensor
        def _(pe):
            pe.matmul(K.ps[0:ROPE, 2, 0:T], K.turn[:, :], K.krope[:, :], start=True, stop=True).then_inc(s("krope_turned"), 1)
            pe.wait_ge(s("mla_sq"), 1)
            sum_over_partitions(K, pe, K.ps[:, 0, 0:T], [sq[:, 0], sq[:, 1]])
            sum_over_partitions(K, pe, K.ps[:, 1, 0:T], [sq[:, 2], sq[:, 3]]).then_inc(s("mla_ss"), 1)
            pe.wait_ge(s("mla_normed"), 1)
            for r, (t0, n) in enumerate(((0, P), (P, P), (SEQ, NSAMP))):
                for c in range(2):
                    mm = pe.transpose(K.ps[0:n, 3 + r, c * P:(c + 1) * P], C[:, 2 + c, t0:t0 + n], K.ident[:, :])
            mm.then_inc(s("ckv_tm"), 1)
            pe.wait_ge(s("uq_loaded"), 16)
            pe.wait_ge(s("uk_loaded"), 16)
            pe.wait_ge(s("krope_ready"), 1)
            pe.wait_ge(s("ckv_tm_copied"), 1)
            for h in range(MH):
                if h >= 1:
                    pe.wait_ge(s("q_nope_copied"), h)
                    pe.wait_ge(s("q_rope_copied"), h)
                for k in range(2):
                    pe.matmul(K.ps[0:NOPE, 0, 0:T], wuq[:, k, h * 96:h * 96 + NOPE], C[:, k], start=(k == 0), stop=(k == 1))
                for k in range(2):
                    mm = pe.matmul(K.ps[0:ROPE, 1, 0:T], wuq[:, k, h * 96 + NOPE:h * 96 + 96], C[:, k],
                                   start=(k == 0), stop=(k == 1))
                mm.then_inc(s("q_head_done"), 1)
                pe.wait_ge(s("q_nope_copied"), h + 1)
                if h >= 1:
                    pe.wait_ge(s("q_abs_copied"), h)
                for c in range(2):
                    mm = pe.matmul(K.ps[:, 3 + c, 0:T], wuk[:, h, c * P:(c + 1) * P], qn[:, h % 2], start=True, stop=True)
                mm.then_inc(s("q_abs_done"), 1)
                pe.wait_ge(s("q_rope_copied"), h + 1)
                if h >= 1:
                    pe.wait_ge(s("q_turned_read"), h)
                pe.matmul(K.ps[0:ROPE, 2, 0:T], K.turn[:, :], A.qr[:, h], start=True, stop=True).then_inc(s("q_turned"), 1)


def mla_prompt_stage(K, l, A):
    nc, s = K.nc, K.sem
    pT = K.h[:, :, :].rearrange("p k t -> p (k t)")[:, 0:2 * MH * P].rearrange("p (j h q) -> p j h q", j=2, h=MH)
    with (nc.sbuf_tensor("u_pr_p", [P, MH, SEQ], F32) as p, nc.sbuf_tensor("pr_stat", [P, 3, MH], F32) as st,
          nc.Block(no_gpsimd_drain=True) as block):
        @block.sync
        def _(sp):
            for g in range(2):
                load_keys(K, sp, l, g, page_numbers(K, sp, 0, g), A.keys)

        def scores(n, j):
            return K.ps[:, 2 * j:2 * j + 2, :].rearrange("p b (h k) -> p (b h) k", h=4)

        @block.tensor
        def _(pe):
            for n in range(2):
                if n:
                    pe.wait_ge(s("pr_scores_read"), n)
                q0 = n * P
                for j in range(n + 1):
                    for h in range(MH):
                        out = scores(n, j)[:, h]
                        for c in range(2):
                            pe.matmul(out, A.qa[:, c, h, q0:q0 + P], K.proj[:, KVD0 + c, j * P:(j + 1) * P],
                                      start=(c == 0), stop=False)
                        mm = pe.matmul(out, A.qr[:, h, q0:q0 + P], K.krope[:, j * P:(j + 1) * P], start=False, stop=True)
                mm.then_inc(s("pr_scores"), 1)
                pe.wait_ge(s("pr_p"), n + 1)
                for j in range(n + 1):
                    if n + j >= 1:
                        pe.wait_ge(s("pr_pT_copied"), n + j)
                    for h in range(MH):
                        mm = pe.transpose(K.ps[:, 4 + h // 4, (h % 4) * P:(h % 4 + 1) * P], p[:, h, j * P:(j + 1) * P],
                                          K.ident[:, :])
                    mm.then_inc(s("pr_pT"), 1)
                pe.wait_ge(s("pr_pT_copied"), 1 if n == 0 else 3)
                for g in range(2):
                    if n + g >= 1:
                        pe.wait_ge(s("pr_o_copied"), 2 * n + g)
                    for c in range(2):
                        for j in range(n + 1):
                            mm = pe.matmul(K.ps[:, 6 + c, :], A.ckv[:, j, c * P:(c + 1) * P],
                                           pT[:, j, 4 * g:4 * g + 4].rearrange("p h q -> p (h q)"),
                                           start=(j == 0), stop=(j == n))
                    mm.then_inc(s("pr_o"), 1)

        @block.vector
        def _(dve):
            v, link = nc.vector, lambda ins: K.vc.link(dve, ins)
            for n in range(2):
                W = (n + 1) * P
                dve.wait_ge(s("pr_scores"), n + 1)
                if n:
                    dve.wait_ge(s("pr_pT"), 1)
                for j in range(n):
                    v.tensor_copy(p[:, :, j * P:(j + 1) * P], scores(n, j))
                link(v.tensor_tensor(p[:, :, n * P:W], scores(n, n), K.later[:, :].unsqueeze(1).to_broadcast([P, MH, P]), ALU.add))
                dve.sem_inc(s("pr_scores_read"), 1)
                link(v.tensor_reduce(st[:, 0, :], p[:, :, 0:W], AX.X, ALU.max))
                v.tensor_tensor(p[:, :, 0:W], p[:, :, 0:W], st[:, 0, :].unsqueeze(2).to_broadcast([P, MH, W]), ALU.subtract
                                ).then_inc(s("pr_arg"), 1)
                dve.wait_ge(s("pr_exp"), n + 1)
                link(v.tensor_reduce(st[:, 1, :], p[:, :, 0:W], AX.X, ALU.add))
                link(v.reciprocal(st[:, 2, :], st[:, 1, :]))
                v.tensor_tensor(p[:, :, 0:W], p[:, :, 0:W], st[:, 2, :].unsqueeze(2).to_broadcast([P, MH, W]), ALU.mult
                                ).then_inc(s("pr_p"), 1)
                for j in range(n + 1):
                    dve.wait_ge(s("pr_pT"), n + j + 1)
                    if n:
                        dve.wait_ge(s("pr_o"), 2)
                    v.tensor_copy(pT[:, j].rearrange("p h q -> p (h q)"), K.ps[:, 4:6, :].rearrange("p b c -> p (b c)")
                                  ).then_inc(s("pr_pT_copied"), 1)
                for g in range(2):
                    dve.wait_ge(s("pr_o"), 2 * n + g + 1)
                    v.tensor_copy(A.qa[:, :, 4 * g:4 * g + 4, n * P:(n + 1) * P],
                                  K.ps[:, 6:8, :].rearrange("p c (h q) -> p c h q", h=4)).then_inc(s("pr_o_copied"), 1)

        @block.scalar
        def _(act):
            for n in range(2):
                act.wait_ge(s("pr_arg"), n + 1)
                w = p[:, :, 0:(n + 1) * P]
                nc.scalar.activation(w, w, ACT.Exp, scale=ATT_SCALE).then_inc(s("pr_exp"), 1)
                load_values(K, act, l, n, page_numbers(K, act, 0, n), A.values)


def page_numbers(K, eng, n, g):
    return [(r, j, eng.value_load(K.table[0:1, (2 * n + r) * NPAGE + j:(2 * n + r) * NPAGE + j + 1],
                                  min_val=0, max_val=K.n_pool - 1))
            for j in range(g * NPAGE // 2, (g + 1) * NPAGE // 2) for r in range(2)]


def load_keys(K, eng, l, g, pages, dst):
    for r, j, page in pages:
        eng.dma_start(dst[:, r, j, :], K.d["pages_k"][l, bass.ds(page, 1)].rearrange("o p c -> p (o c)")
                      ).then_inc(K.sem(f"keys_loaded{g}"), 16)


def load_values(K, eng, l, g, pages, dst):
    for r, j, page in pages:
        eng.dma_start(dst[:, r, j, :], K.d["pages_v"][l, bass.ds(page, 1)].rearrange("o p c -> p (o c)")
                      ).then_inc(K.sem(f"values_loaded{g}"), 16)


def mla_sample_stage(K, l, A):
    nc, s = K.nc, K.sem
    NK, PAIRS, HALF = PAST + NSAMP, NB // 2, NPAGE // 2
    PER_HALF = 16 * 2 * HALF
    with ExitStack() as e:
        sb = lambda n, sh: e.enter_context(nc.sbuf_tensor("t_" + n, sh, F32))
        p, o, st = sb("sa_p", [P, NK]), sb("sa_o", [P, 256]), sb("sa_stat", [P, 4])
        spare = K.h[:, :, :].rearrange("p k t -> p (k t)")
        cut = (NPAGE + 1) * P
        pT = spare[:, 0:cut].rearrange("p (j q) -> p j q", j=NPAGE + 1)
        qa_b = spare[:, cut:cut + 2 * NB * NSAMP].rearrange("p (c b q) -> p c b q", c=2, b=NB)
        qr_b = K.proj[0:ROPE, XBC0:XBC0 + 2, 0:NB * NSAMP // 2].rearrange("p c (b q) -> p c b q", b=NB // 2)
        block = e.enter_context(nc.Block(no_gpsimd_drain=True))
        rows = lambda r: slice(r * NSAMP, (r + 1) * NSAMP)

        @block.sync
        def _(sp):
            for n in range(1, PAIRS):
                for g in range(2):
                    pages = page_numbers(K, sp, n, g)
                    sp.wait_ge(s("keys_used"), 2 * n - 1 + g)
                    load_keys(K, sp, l, g, pages, A.keys)

        def turn_o(pe, n):
            pe.wait_ge(s("sa_o_scaled"), n + 1)
            if n:
                pe.wait_ge(s("sa_o_copied"), n)
            for c in range(2):
                mm = pe.transpose(K.ps[:, 7, c * P:(c + 1) * P], o[:, c * P:(c + 1) * P], K.ident[:, :])
            mm.then_inc(s("sa_o_turned"), 1)

        @block.tensor
        def _(pe):
            def query(b, c):
                return qa_b[:, c, b] if c < 2 else qr_b[:, b // 4, b % 4]

            pe.wait_ge(s("sa_q"), 1)
            for n in range(PAIRS):
                if n:
                    pe.wait_ge(s("sa_exp"), n)
                for g in range(2):
                    pe.wait_ge(s(f"keys_loaded{g}"), PER_HALF * (n + 1))
                    for c in range(3):
                        for r in range(2):
                            keys = A.keys[0:P if c < 2 else ROPE, r, HALF * g:HALF * (g + 1), c * P:(c + 1) * P]
                            mm = pe.matmul(K.ps[rows(r), g, :], query(2 * n + r, c), keys, start=(c == 0), stop=(c == 2))
                    mm.then_inc(s("keys_used"), 1)
                for c in range(3):
                    own = K.proj[:, KVD0 + c, SEQ:T] if c < 2 else K.krope[:, SEQ:T]
                    for r in range(2):
                        mm = pe.matmul(K.ps[rows(r), 2, 0:NSAMP], query(2 * n + r, c), own, start=(c == 0), stop=(c == 2))
                mm.then_inc(s("sa_scores"), 1)
                if n:
                    turn_o(pe, n - 1)
                pe.wait_ge(s("sa_exp"), n + 1)
                pe.transpose(K.ps[0:NSAMP, 3, 0:P], p[:, PAST:NK], K.ident[:, :])
                for g in range(2):
                    for j in range(HALF):
                        mm = pe.transpose(K.ps[:, 4 + g, j * P:(j + 1) * P], p[:, (HALF * g + j) * P:(HALF * g + j + 1) * P],
                                          K.ident[:, :])
                    mm.then_inc(s("sa_pT"), 1)
                for g in range(2):
                    pe.wait_ge(s(f"sa_pT_copied{g}"), n + 1)
                    pe.wait_ge(s(f"values_loaded{g}"), PER_HALF * (n + 1))
                    if g == 0:
                        for r in range(2):
                            pe.matmul(K.ps[rows(r), 6, 0:256], pT[0:NSAMP, NPAGE, rows(r)], A.ckv[0:NSAMP, 2, :],
                                      start=True, stop=False)
                    for j in range(HALF * g, HALF * (g + 1)):
                        for r in range(2):
                            mm = pe.matmul(K.ps[rows(r), 6, 0:256], pT[:, j, rows(r)], A.values[:, r, j, :],
                                           start=False, stop=(j == NPAGE - 1))
                    mm.then_inc(s("values_used"), 1)
            turn_o(pe, PAIRS - 1)

        @block.vector
        def _(dve):
            v, link = nc.vector, lambda ins: K.vc.link(dve, ins)

            def store_o(n):
                dve.wait_ge(s("sa_o_turned"), n + 1)
                for r in range(2):
                    t0 = SEQ + (2 * n + r) * TS
                    ins = v.tensor_copy(A.qa[:, :, :, t0:t0 + TS], K.ps[:, 7, 0:2 * P].rearrange(
                        "p (c r h t) -> p c r h t", c=2, r=2, h=MH)[:, :, r])
                ins.then_inc(s("sa_o_copied"), 1)

            for b in range(NB):
                for c in range(2):
                    v.tensor_copy(qa_b[:, c, b].rearrange("p (h t) -> p h t", t=TS), A.qa[:, c, :, SEQ + b * TS:SEQ + (b + 1) * TS])
                ins = v.tensor_copy(qr_b[:, b // 4, b % 4].rearrange("p (h t) -> p h t", t=TS), A.qr[:, :, SEQ + b * TS:SEQ + (b + 1) * TS])
            link(ins)
            dve.sem_inc(s("sa_q"), 1)
            for n in range(PAIRS):
                S = K.ps[:, 0:3, :].rearrange("p b c -> p (b c)")[:, 0:NK]
                dve.wait_ge(s("sa_scores"), n + 1)
                link(v.tensor_tensor(K.ps[:, 2, 0:NSAMP], K.ps[:, 2, 0:NSAMP], K.own[:, n, :], ALU.add))
                link(v.tensor_reduce(st[:, 0:1], S, AX.X, ALU.max))
                v.tensor_scalar(st[:, 1:2], st[:, 0:1], -ATT_SCALE, None, ALU.mult).then_inc(s("sa_max"), 1)
                if n:
                    store_o(n - 1)
                dve.wait_ge(s("sa_exp"), n + 1)
                link(v.reciprocal(st[:, 3:4], st[:, 2:3]))
                dve.wait_ge(s("sa_pT"), 2 * n + 1)
                v.tensor_copy(pT[0:NSAMP, NPAGE], K.ps[0:NSAMP, 3, 0:P])
                v.tensor_copy(pT[:, 0:HALF].rearrange("p j q -> p (j q)"), K.ps[:, 4, :]).then_inc(s("sa_pT_copied0"), 1)
                dve.wait_ge(s("values_used"), 2 * n + 2)
                v.tensor_scalar(o[:, :], K.ps[:, 6, 0:256], st[:, 3:4], None, ALU.mult).then_inc(s("sa_o_scaled"), 1)
            store_o(PAIRS - 1)

        @block.scalar
        def _(act):
            for n in range(PAIRS):
                if n:
                    act.wait_ge(s("values_used"), 2 * n - 1)
                    load_values(K, act, l, 0, pages0, A.values)
                act.wait_ge(s("sa_max"), n + 1)
                nc.scalar.activation(p[:, :], K.ps[:, 0:3, :].rearrange("p b c -> p (b c)")[:, 0:NK], ACT.Exp,
                                     bias=st[:, 1:2], scale=ATT_SCALE, accum_out=st[:, 2:3]).then_inc(s("sa_exp"), 1)
                if n:
                    act.wait_ge(s("values_used"), 2 * n)
                    load_values(K, act, l, 1, pages1, A.values)
                act.wait_ge(s("sa_pT"), 2 * n + 2)
                nc.scalar.copy(pT[:, HALF:NPAGE].rearrange("p j q -> p (j q)"), K.ps[:, 5, :]).then_inc(s("sa_pT_copied1"), 1)
                if n + 1 < PAIRS:
                    pages0, pages1 = (page_numbers(K, act, n + 1, g) for g in range(2))


def mla_value_stage(K, l, A):
    nc, s = K.nc, K.sem
    with nc.sbuf_tensor("u_w_uv", [P, 2, MH, 64], F32) as wuv, nc.Block(no_gpsimd_drain=True) as block:
        @block.sync
        def _(sp):
            sp.dma_start(wuv[:, :, :, :], K.d["w_uv"][l]).then_inc(s("uv_loaded"), 16)

        @block.tensor
        def _(pe):
            pe.wait_ge(s("uv_loaded"), 16)
            for h in range(MH):
                for k in range(2):
                    mm = pe.matmul(K.ps[64 * (h % 2):64 * (h % 2) + 64, h // 2, 0:T], wuv[:, k, h, :], A.qa[:, k, h, :],
                                   start=(k == 0), stop=(k == 1))
            mm.then_inc(s("yc_done"), 1)

        @block.vector
        def _(dve):
            dve.wait_ge(s("yc_done"), 1)
            nc.vector.tensor_copy(K.proj[:, HF0:HF0 + 4, :], K.ps[:, 0:4, 0:T])


def lru_stage(K, l):
    nc, s = K.nc, K.sem
    with ExitStack() as e:
        sb = lambda n, sh: e.enter_context(nc.sbuf_tensor("t_" + n, sh, F32))
        w = sb("lru_w", [P, 2, 4, P])
        r, ig, t1 = sb("lru_r", [P, 4, T]), sb("lru_i", [P, 4, T]), sb("lru_t", [P, 4, T])
        sp_, h0, hout = sb("lru_sp", [P, 4, 4]), sb("lru_h0", [P, 4, NB]), sb("lru_hout", [P, 4, NREQ])
        block = e.enter_context(nc.Block(no_gpsimd_drain=True))
        X, Y = K.proj[:, LX0:LX0 + 4, :], K.proj[:, LY0:LY0 + 4, :]

        @block.sync
        def _(sp):
            sp.dma_start(w[:, :, :, :], K.d["lru_w"][l]).then_inc(s("lru_w_loaded"), 16)
            sp.dma_start(h0[:, :, :], K.d["lru_state"][l]).then_inc(s("lru_h0_loaded"), 16)
            sp.wait_ge(s("lru_out_ready"), 1)
            sp.dma_start(K.d["o_lru"][l], hout[:, :, :]).then_inc(s("lru_stored"), 16)
            sp.wait_ge(s("lru_stored"), 16)

        @block.tensor
        def _(pe):
            pe.wait_ge(s("lru_w_loaded"), 16)
            for n in range(2):
                for c in range(4):
                    mm = pe.matmul(K.ps[:, 4 * n + c, 0:T], w[:, n, c, :], X[:, c], start=True, stop=True)
                mm.then_inc(s("lru_gates"), 1)

        @block.scalar
        def _(act):
            a, link = nc.scalar, lambda ins: K.ac.link(act, ins)
            link(a.activation(sp_[:, 0], K.cols[:, C_LA:C_LA + 4], ACT.Abs))
            link(a.activation(sp_[:, 0], sp_[:, 0], ACT.Exp, scale=-1.0))
            a.activation(sp_[:, 1], sp_[:, 0], ACT.Ln, bias=1.0).then_inc(s("lru_ln"), 1)
            for n, (dst, c0) in enumerate(((r, C_BR), (ig, C_BI))):
                act.wait_ge(s("lru_gates"), n + 1)
                for c in range(4):
                    ins = a.activation(dst[:, c], K.ps[:, 4 * n + c, 0:T], ACT.Sigmoid, bias=K.cols[:, c0 + c:c0 + c + 1])
            ins.then_inc(s("lru_sig"), 1)
            act.wait_ge(s("lru_loga"), 1)
            a.activation(t1[:, :, :], r[:, :, :], ACT.Tanh).then_inc(s("lru_tanh"), 1)
            act.wait_ge(s("lru_tanh"), 1)
            a.activation(r[:, :, :], r[:, :, :], ACT.Exp).then_inc(s("lru_a"), 1)
            act.wait_ge(s("lru_m2"), 1)
            a.activation(t1[:, :, :], t1[:, :, :], ACT.Sqrt).then_inc(s("lru_mult"), 1)
            a.activation(Y, Y, ACT.Gelu_apprx_tanh).then_inc(s("lru_gelu"), 1)

        @block.vector
        def _(dve):
            v, link = nc.vector, lambda ins: K.vc.link(dve, ins)
            link(v.tensor_scalar(sp_[:, 2], K.cols[:, C_LA:C_LA + 4], -1.0, 0.0, ALU.mult, ALU.max))
            dve.wait_ge(s("lru_ln"), 1)
            link(v.tensor_tensor(sp_[:, 2], sp_[:, 2], sp_[:, 1], ALU.add))
            link(v.tensor_scalar(sp_[:, 3], sp_[:, 2], -8.0, None, ALU.mult))
            dve.wait_ge(s("lru_sig"), 1)
            v.tensor_tensor(r[:, :, :], r[:, :, :], sp_[:, 3].unsqueeze(2).to_broadcast([P, 4, T]), ALU.mult
                            ).then_inc(s("lru_loga"), 1)
            link(v.tensor_tensor(ig[:, :, :], ig[:, :, :], X, ALU.mult))
            dve.wait_ge(s("lru_a"), 1)
            link(v.tensor_tensor(X, r[:, :, :], r[:, :, :], ALU.mult))
            link(v.tensor_scalar(X, X, 1.0, -1.0, ALU.add, ALU.mult))
            link(v.tensor_tensor(t1[:, :, :], t1[:, :, :], X, ALU.mult))
            v.tensor_scalar(t1[:, :, :], t1[:, :, :], 1e-30, None, ALU.max).then_inc(s("lru_m2"), 1)
            dve.wait_ge(s("lru_mult"), 1)
            link(v.memset(t1[:, :, 0:1], 1.0))
            link(v.tensor_tensor(t1[:, :, :], t1[:, :, :], ig[:, :, :], ALU.mult))
            dve.wait_ge(s("lru_h0_loaded"), 16)
            link(v.tensor_tensor(h0[:, :, :], h0[:, :, :], sample(r)[:, :, :, 0], ALU.mult))
            link(v.tensor_tensor(sample(t1)[:, :, :, 0], sample(t1)[:, :, :, 0], h0[:, :, :], ALU.add))
            link(v.tensor_tensor(r[:, :, :], r[:, :, :], K.keep[:, :].unsqueeze(1).to_broadcast([P, 4, T]), ALU.mult))
            link(v.tensor_tensor_scan(X.rearrange("p c t -> p (c t)"), r[:, :, :].rearrange("p c t -> p (c t)"),
                                      t1[:, :, :].rearrange("p c t -> p (c t)"), 0.0, ALU.mult, ALU.add))
            v.tensor_copy(hout[:, :, 0:1], X[:, :, SEQ - 1:SEQ])
            v.tensor_copy(hout[:, :, 1:NREQ], sample(X)[:, :, :, TS - 1]).then_inc(s("lru_out_ready"), 1)
            dve.wait_ge(s("lru_gelu"), 1)
            v.tensor_tensor(Y, X, Y, ALU.mult)


def merge_stage(K, l):
    nc, s = K.nc, K.sem
    SL = 4
    SRC = (Z0, HQ0, HF0, LY0)
    with (nc.sbuf_tensor("u_wbr", [P, SL, 4, 512], F32) as wb, nc.sbuf_tensor("mg_tmp", [P, 2, T], F32) as tmp,
          nc.Block(no_gpsimd_drain=True) as block):
        @block.sync
        def _(sp):
            for n in range(12):
                if n >= SL:
                    m = n - SL + 1
                    sp.wait_ge(s("mg_tile"), 4 * min(m, 8) + 2 * max(m - 8, 0))
                src = K.d["w_branch"][l, n] if n < 8 else K.d["w_out"][l, n - 8]
                sp.dma_start(wb[:, n % SL].rearrange("p a b -> p (a b)"), src).then_inc(s(f"mg_loaded{n % SL}"), 16)

        @block.scalar
        def _(act):
            for n in range(4):
                g = K.proj[:, GL0 + 8 * n:GL0 + 8 * n + 8, :]
                nc.scalar.activation(g, g, ACT.Sigmoid).then_inc(s("mg_gates"), 1)

        @block.tensor
        def _(pe):
            for n in range(12):
                pe.wait_ge(s(f"mg_loaded{n % SL}"), 16 * (n // SL + 1))
                if n == 8:
                    pe.wait_ge(s("mg_merged"), 1)
                for m in range(4 if n < 8 else 2):
                    t = 4 * n + m if n < 8 else 32 + 2 * (n - 8) + m
                    if t >= 8:
                        pe.wait_ge(s("mg_read"), t - 7)
                    if n < 8:
                        for k in range(4):
                            mm = pe.matmul(K.ps[:, t % 8, 0:T], wb[:, n % SL, k, m * P:(m + 1) * P],
                                           K.proj[:, SRC[n // 2] + k, :], start=(k == 0), stop=(k == 3))
                    else:
                        w = wb[:, n % SL].rearrange("p a b -> p (a b)").rearrange("p (k c) -> p k c", k=KD)
                        for k in range(KD):
                            mm = pe.matmul(K.ps[:, t % 8, 0:T], w[:, k, m * P:(m + 1) * P], K.h[:, k, :],
                                           start=(k == 0), stop=(k == KD - 1))
                    mm.then_inc(s("mg_tile"), 1)

        @block.vector
        def _(dve):
            v, link = nc.vector, lambda ins: K.vc.link(dve, ins)
            for t in range(32):
                n, m = t // 8, t % 8
                if m == 0:
                    dve.wait_ge(s("mg_gates"), n + 1)
                dve.wait_ge(s("mg_tile"), t + 1)
                if n == 0:
                    v.tensor_tensor(K.h[:, m, :], K.ps[:, t % 8, 0:T], K.proj[:, GL0 + t, :], ALU.mult).then_inc(s("mg_read"), 1)
                else:
                    v.tensor_tensor(tmp[:, t % 2], K.ps[:, t % 8, 0:T], K.proj[:, GL0 + t, :], ALU.mult).then_inc(s("mg_read"), 1)
                    dve.wait_ge(s("mg_read"), t + 1)
                    link(v.tensor_tensor(K.h[:, m, :], K.h[:, m, :], tmp[:, t % 2], ALU.add))
            dve.sem_inc(s("mg_merged"), 1)
            for m in range(KD):
                t = 32 + m
                dve.wait_ge(s("mg_tile"), t + 1)
                residual(K, dve, K.ps[:, t % 8, 0:T], tmp[:, t % 2], 16 + m, m, s("mg_read"), t + 1)


def residual(K, dve, src, tmp, g, m, read, count):
    v = K.nc.vector
    v.scalar_tensor_tensor(out=K.x[:, m, 0:SEQ], in0=src[:, 0:SEQ], scalar=K.mod[:, g, 0:1], in1=K.x[:, m, 0:SEQ],
                           op0=ALU.mult, op1=ALU.add)
    v.tensor_tensor(tmp[:, SEQ:T].rearrange("p (b t) -> p b t", t=TS), src[:, SEQ:T].rearrange("p (b t) -> p b t", t=TS),
                    K.mod[:, g, 1:NREQ].unsqueeze(2).to_broadcast([P, NB, TS]), ALU.mult).then_inc(read, 1)
    dve.wait_ge(read, count)
    v.tensor_tensor(K.x[:, m, SEQ:T], K.x[:, m, SEQ:T], tmp[:, SEQ:T], ALU.add)


def router_stage(K, l, R):
    nc, s = K.nc, K.sem
    with ExitStack() as e:
        sb = lambda n, sh: e.enter_context(nc.sbuf_tensor("t_" + n, sh, F32))
        w, bias = sb("w_router", [P, KD, 36]), sb("b_router", [1, 36])
        L, g = sb("rt_L", [P, 3, 36]), sb("rt_g", [P, 4, 3, 4])
        ee, st, gate = sb("rt_e", [P, 5, 3, 8]), sb("rt_st", [P, 10, 3]), sb("rt_gate", [P, 3, 4, 8])
        sel, tmp32 = sb("rt_sel", [P, 3, 3, NEXP]), sb("rt_tmp32", [P, 3, NEXP])
        total = sb("rt_total", [1, 2 + MAX_PASS])
        block = e.enter_context(nc.Block(no_gpsimd_drain=True))
        REG = ((0, P), (P, P), (SEQ, NSAMP))

        @block.sync
        def _(sp):
            sp.dma_start(w[:, :, :], K.d["w_router"][l]).then_inc(s("rt_w_loaded"), 16)
            sp.dma_start(bias[:, :], K.d["b_router"][l]).then_inc(s("rt_b_loaded"), 16)

        @block.tensor
        def _(pe):
            pe.wait_ge(s("rt_w_loaded"), 16)
            pe.wait_ge(s("rt_b_loaded"), 16)
            for r, (t0, n) in enumerate(REG):
                for k in range(KD):
                    pe.matmul(K.ps[0:n, 0, r * 36:(r + 1) * 36], K.h[:, k, t0:t0 + n], w[:, k, :], start=(k == 0), stop=False)
                mm = pe.matmul(K.ps[0:n, 0, r * 36:(r + 1) * 36], K.ones[0:1, 0:n], bias[:, :], start=False, stop=True)
            mm.then_inc(s("rt_logits"), 1)
            for r, (t0, n) in enumerate(REG):
                if r == 2:
                    pe.wait_ge(s("h_tm_copied"), 1)
                for k in range(KD):
                    mm = pe.transpose(K.ps[0:n, 4 + 2 * (r % 2) + k // 4, (k % 4) * P:(k % 4 + 1) * P],
                                      K.h[:, k, t0:t0 + n], K.ident[:, :])
                mm.then_inc(s("h_tm"), 1)
            pe.wait_ge(s("rt_sel"), 1)
            for r, (t0, n) in enumerate(REG):
                for q in range(r):
                    pe.matmul(K.ps[0:n, 2, r * NEXP:(r + 1) * NEXP], K.ones[:, 0:n], sel[:, 2, q, :], start=(q == 0), stop=False)
                pe.matmul(K.ps[0:n, 2, r * NEXP:(r + 1) * NEXP], K.causal[0:n, 0:n], sel[0:n, 2, r, :], start=(r == 0), stop=True)
            for r, (t0, n) in enumerate(REG):
                mm = pe.matmul(K.ps[0:32, 3, 0:NEXP], K.ones[0:n, 0:32], sel[0:n, 2, r, :], start=(r == 0), stop=(r == 2))
            mm.then_inc(s("rt_counts"), 1)

        @block.vector
        def _(dve):
            v, link = nc.vector, lambda ins: K.vc.link(dve, ins)

            def first_max(x, mx, onehot, tmp, n):
                bc = lambda a: a.unsqueeze(2).to_broadcast([P, 3, n])
                io = K.iota[:, 0:n].unsqueeze(1).to_broadcast([P, 3, n])
                link(v.tensor_reduce(mx, x, AX.X, ALU.max))
                link(v.tensor_tensor(tmp, x, bc(mx), ALU.is_equal))
                link(v.tensor_scalar(tmp, tmp, -100.0, 100.0, ALU.mult, ALU.add))
                link(v.tensor_tensor(tmp, tmp, io, ALU.add))
                link(v.tensor_reduce(st[:, 9], tmp, AX.X, ALU.min))
                link(v.tensor_tensor(onehot, io, bc(st[:, 9]), ALU.is_equal))

            link(v.memset(L[:, 2, :], 0.0))
            dve.wait_ge(s("rt_logits"), 1)
            v.tensor_copy(L[:, 0:2].rearrange("p r c -> p (r c)"), K.ps[:, 0, 0:72])
            link(v.tensor_copy(L[0:NSAMP, 2], K.ps[0:NSAMP, 0, 72:108]))
            G, E = L[:, :, 0:4], L[:, :, 4:36].rearrange("p r (g e) -> p r g e", g=4)
            first_max(G, st[:, 0], g[:, 0], g[:, 1], 4)
            v.tensor_tensor(g[:, 2], G, st[:, 0].unsqueeze(2).to_broadcast([P, 3, 4]), ALU.subtract).then_inc(s("rt_garg"), 1)
            link(v.tensor_tensor(gate[:, :, :, :], E, g[:, 0].unsqueeze(3).to_broadcast([P, 3, 4, 8]), ALU.mult))
            link(v.tensor_tensor(ee[:, 0], gate[:, :, 0, :], gate[:, :, 1, :], ALU.add))
            link(v.tensor_tensor(ee[:, 1], gate[:, :, 2, :], gate[:, :, 3, :], ALU.add))
            link(v.tensor_tensor(ee[:, 0], ee[:, 0], ee[:, 1], ALU.add))
            first_max(ee[:, 0], st[:, 1], ee[:, 1], ee[:, 2], 8)
            link(v.scalar_tensor_tensor(out=ee[:, 2], in0=ee[:, 1], scalar=-BIG, in1=ee[:, 0], op0=ALU.mult, op1=ALU.add))
            first_max(ee[:, 2], st[:, 2], ee[:, 3], ee[:, 4], 8)
            v.tensor_tensor(st[:, 3], st[:, 2], st[:, 1], ALU.subtract).then_inc(s("rt_darg"), 1)
            for n in range(2):
                link(v.tensor_tensor(sel[:, n].rearrange("p r (g e) -> p r g e", g=4),
                                     ee[:, 1 + 2 * n].unsqueeze(2).to_broadcast([P, 3, 4, 8]),
                                     g[:, 0].unsqueeze(3).to_broadcast([P, 3, 4, 8]), ALU.mult))
            v.tensor_tensor(sel[:, 2], sel[:, 0], sel[:, 1], ALU.add).then_inc(s("rt_sel"), 1)
            dve.wait_ge(s("rt_exp"), 1)
            link(v.tensor_reduce(st[:, 5], g[:, 3], AX.X, ALU.add))
            link(v.tensor_scalar(st[:, 6], st[:, 4], 1.0, None, ALU.add))
            link(v.tensor_tensor(st[:, 6], st[:, 6], st[:, 5], ALU.mult))
            link(v.reciprocal(st[:, 7], st[:, 6]))
            link(v.tensor_tensor(st[:, 8], st[:, 7], st[:, 4], ALU.mult))
            v.tensor_copy(R.w[:, 0], st[:, 7])
            v.tensor_copy(R.w[:, 1], st[:, 8])
            dve.wait_ge(s("rt_counts"), 1)
            link(v.memset(R.pos[:, :, :], -1.0))
            v.tensor_tensor(tmp32[:, 0:2, :], sel[:, 2, 0:2], K.ps[:, 2, 0:2 * NEXP].rearrange("p (r e) -> p r e", r=2), ALU.mult)
            link(v.tensor_tensor(tmp32[0:NSAMP, 2, :], sel[0:NSAMP, 2, 2], K.ps[0:NSAMP, 2, 2 * NEXP:3 * NEXP], ALU.mult))
            v.tensor_scalar(R.pos[:, 0:2, 0:NEXP], tmp32[:, 0:2], -1.0, None, ALU.add)
            link(v.tensor_scalar(R.pos[0:NSAMP, 2, 0:NEXP], tmp32[0:NSAMP, 2], -1.0, None, ALU.add))
            for n in range(2):
                for q, of_expert in enumerate((R.pos[:, :, 0:NEXP], K.first_slot[:, :].unsqueeze(1).to_broadcast([P, 3, NEXP]))):
                    link(v.tensor_tensor(tmp32[:, :, :], of_expert, sel[:, n], ALU.mult))
                    link(v.tensor_reduce(R.place[:, q, n], tmp32[:, :, :], AX.X, ALU.add))
            link(v.tensor_reduce(total[:, 0:1], K.ps[0:1, 3, 0:NEXP], AX.X, ALU.max))
            link(v.tensor_scalar(total[:, 2:2 + MAX_PASS], K.first_slot[0:1, 0:MAX_PASS], total[:, 0:1], None, ALU.is_lt))
            link(v.tensor_reduce(total[:, 1:2], total[:, 2:2 + MAX_PASS], AX.X, ALU.add))
            v.tensor_copy(R.passes[:, :], total[:, 1:2])
        @block.scalar
        def _(act):
            for r, (t0, n) in enumerate(REG):
                act.wait_ge(s("h_tm"), r + 1)
                nc.scalar.copy(R.hT[0:n, r, :], K.ps[0:n, 4 + 2 * (r % 2):6 + 2 * (r % 2), :].rearrange("p b c -> p (b c)")
                               ).then_inc(s("h_tm_copied"), 1)
            act.wait_ge(s("rt_garg"), 1)
            nc.scalar.activation(g[:, 3], g[:, 2], ACT.Exp)
            act.wait_ge(s("rt_darg"), 1)
            nc.scalar.activation(st[:, 4], st[:, 3], ACT.Exp).then_inc(s("rt_exp"), 1)


def load_expert(K, sp, l, e, j):
    s = K.sem
    sp.dma_start(K.gate_up[:, j], K.d["w_gate_up"][l, e].rearrange("o p k n -> p (o k) n")).then_inc(s(f"gu_loaded{j}"), 16)


def load_down(K, sp, l, e, j, wd):
    sp.dma_start(wd[:, j], K.d["w_down"][l, e].rearrange("o p k n -> p (o k) n")).then_inc(K.sem(f"down_loaded{j}"), 16)


def experts_stage(K, l, R, turn):
    nc, s = K.nc, K.sem
    TILES = ((0, P), (1, P), (2, NSAMP))
    PAIRS = NEXP // 2
    NI = PAIRS // 2
    LOOPS = ((0, 1), (1, NI - 1), (NI - 1, NI))
    G0, X0, GU, HT, DN = 0, 2, 4, 5, 6
    with ExitStack() as e_:
        sb = lambda n, sh: e_.enter_context(nc.sbuf_tensor("t_" + n, sh, F32))
        wd = sb("w_down", [P, SLOTS, 2, D])
        pick, xt, xf = sb("ex_pick", [P, 2, 3, 2, CAP]), sb("ex_xt", [P, D]), sb("ex_xf", [P, 2, KD, P])
        hid, hf, y = sb("ex_hid", [P, 2, HID]), sb("ex_hf", [P, 2, 2, P]), sb("ex_y", [P, 2, D])
        block = e_.enter_context(nc.Block(no_gpsimd_drain=True))

        def pairs(eng):
            for i0, i1 in LOOPS:
                with eng.Fori(i0, i1) as i:
                    for b in range(2):
                        yield i, b, i * 2 + b, i0 == 0, i1 == NI

        @block.sync
        def _(sp):
            with sp.If(turn > 0):
                for j in range(SLOTS):
                    load_expert(K, sp, l, slice(j, j + 1), j)
            for j in range(SLOTS):
                load_down(K, sp, l, slice(j, j + 1), j, wd)
            with sp.Fori(1, NI) as i:
                for b in range(2):
                    sp.wait_ge(s("gu_done"), (i - 1) * 2 + b + 1)
                    for j in (2 * b, 2 * b + 1):
                        load_expert(K, sp, l, bass.ds(i * SLOTS + j, 1), j)
                    sp.wait_ge(s("down_done"), (i - 1) * 2 + b + 1)
                    for j in (2 * b, 2 * b + 1):
                        load_down(K, sp, l, bass.ds(i * SLOTS + j, 1), j, wd)

        @block.tensor
        def _(pe):
            def gather(q, b, first):
                pe.wait_ge(s("pick_ready"), q + 1)
                if not first:
                    pe.wait_ge(s("xt_ready"), q)
                for half in range(2):
                    for r, n in TILES:
                        mm = pe.matmul(K.ps[:, G0 + half, :], pick[0:n, b, r].rearrange("p e c -> p (e c)"),
                                       R.hT[0:n, r, half * 512:(half + 1) * 512], start=(r == 0), stop=(r == 2))
                mm.then_inc(s("gathered"), 1)

            def turn_x(q, first):
                pe.wait_ge(s("xt_ready"), q + 1)
                if not first:
                    pe.wait_ge(s("xf_ready"), q)
                for k in range(KD):
                    mm = pe.transpose(K.ps[:, X0 + k // 4, (k % 4) * P:(k % 4 + 1) * P], xt[:, k * P:(k + 1) * P], K.ident[:, :])
                mm.then_inc(s("x_turned"), 1)

            gather(0, 0, True)
            turn_x(0, True)
            gather(1, 1, False)
            for i, b, p, head, tail in pairs(pe):
                first = head and b == 0
                pe.wait_ge(s("xf_ready"), p + 1)
                for j in (2 * b, 2 * b + 1):
                    pe.wait_ge(s(f"gu_loaded{j}"), i * 16 + 16)
                if not first:
                    pe.wait_ge(s("hid_ready"), p)
                for k in range(KD):
                    for q in range(2):
                        rows = slice(q * CAP, (q + 1) * CAP)
                        mm = pe.matmul(K.ps[rows, GU, :], xf[:, b, k, rows], K.gate_up[:, 2 * b + q, k, :],
                                       start=(k == 0), stop=(k == KD - 1))
                mm.then_inc(s("gu_done"), 1)
                if not (tail and b == 1):
                    turn_x(p + 1, False)
                pe.wait_ge(s("hid_ready"), p + 1)
                if not first:
                    pe.wait_ge(s("hf_ready"), p)
                for f in range(2):
                    mm = pe.transpose(K.ps[:, HT, f * P:(f + 1) * P], hid[:, b, f * P:(f + 1) * P], K.ident[:, :])
                mm.then_inc(s("hid_turned"), 1)
                if not tail:
                    gather(p + 2, b, False)
                pe.wait_ge(s("hf_ready"), p + 1)
                for j in (2 * b, 2 * b + 1):
                    pe.wait_ge(s(f"down_loaded{j}"), i * 16 + 16)
                if not first:
                    pe.wait_ge(s("y_low"), p)
                    pe.wait_ge(s("y_high"), p)
                for half in range(2):
                    for f in range(2):
                        for q in range(2):
                            rows = slice(q * CAP, (q + 1) * CAP)
                            mm = pe.matmul(K.ps[rows, DN + half, :], hf[:, b, f, rows],
                                           wd[:, 2 * b + q, f, half * 512:(half + 1) * 512], start=(f == 0), stop=(f == 1))
                mm.then_inc(s("down_done"), 1)

        @block.vector
        def _(dve):
            v = nc.vector

            def choose(experts, b):
                v.tensor_tensor(pick[:, b], R.pos[:, :, experts].unsqueeze(3).to_broadcast([P, 3, 2, CAP]),
                                K.slot[:, :].unsqueeze(1).unsqueeze(1).to_broadcast([P, 3, 2, CAP]), ALU.is_equal
                                ).then_inc(s("pick_ready"), 1)

            def copy_x(q, b):
                dve.wait_ge(s("x_turned"), q + 1)
                v.tensor_copy(xf[:, b].rearrange("p k c -> p (k c)"), K.ps[:, X0:X0 + 2, :].rearrange("p a c -> p (a c)")
                              ).then_inc(s("xf_ready"), 1)

            choose(slice(0, 2), 0)
            choose(slice(2, 4), 1)
            copy_x(0, 0)
            for i, b, p, head, tail in pairs(dve):
                if not tail:
                    dve.wait_ge(s("gathered"), p + 1)
                    choose(bass.ds((i + 1) * SLOTS + 2 * b, 2), b)
                dve.wait_ge(s("gate_ready"), p + 1)
                v.tensor_tensor(hid[:, b], hid[:, b], K.ps[:, GU, HID:2 * HID], ALU.mult).then_inc(s("hid_ready"), 1)
                if not (tail and b == 1):
                    copy_x(p + 1, 1 - b)
                dve.wait_ge(s("hid_turned"), p + 1)
                v.tensor_copy(hf[:, b].rearrange("p f c -> p (f c)"), K.ps[:, HT, 0:2 * P]).then_inc(s("hf_ready"), 1)
                dve.wait_ge(s("down_done"), p + 1)
                if not head:
                    dve.wait_ge(s(f"y_stored{b}"), i * 16)
                v.tensor_copy(y[:, b, 0:512], K.ps[:, DN, :]).then_inc(s("y_low"), 1)

        @block.scalar
        def _(act):
            a = nc.scalar

            def copy_gathered(q):
                act.wait_ge(s("gathered"), q + 1)
                a.copy(xt[:, :], K.ps[:, G0:G0 + 2, :].rearrange("p a c -> p (a c)")).then_inc(s("xt_ready"), 1)

            copy_gathered(0)
            act.wait_ge(s("x_turned"), 1)
            copy_gathered(1)
            for i, b, p, head, tail in pairs(act):
                act.wait_ge(s("gu_done"), p + 1)
                if not head:
                    act.wait_ge(s("hid_turned"), p - 1)
                a.activation(hid[:, b], K.ps[:, GU, 0:HID], ACT.Silu).then_inc(s("gate_ready"), 1)
                if not tail:
                    act.wait_ge(s("x_turned"), p + 2)
                    copy_gathered(p + 2)
                act.wait_ge(s("down_done"), p + 1)
                if not head:
                    act.wait_ge(s(f"y_stored{b}"), i * 16)
                a.copy(y[:, b, 512:D], K.ps[:, DN + 1, :]).then_inc(s("y_high"), 1)
                act.wait_ge(s("y_low"), p + 1)
                act.wait_ge(s("y_high"), p + 1)
                act.dma_start(K.d["rows"][bass.ds(p * P, P), :], y[:, b, :]).then_inc(s(f"y_stored{b}"), 16)
            for b in range(2):
                act.wait_ge(s(f"y_stored{b}"), NI * 16)


def combine_stage(K, l, R):
    nc, s = K.nc, K.sem
    flat = K.proj[:, :, :].rearrange("p n t -> p (n t)")
    yr = flat[:, 0:6 * D].rearrange("p (n r c) -> p n r c", n=2, r=3)
    with (nc.sbuf_tensor("u_cb_tmp", [P, 2, T], F32) as tmp, nc.sbuf_tensor("cb_w", [P, 5, 6], F32) as w,
          nc.sbuf_tensor("cb_row", [P, 2, 3], U32) as row, nc.Block(no_gpsimd_drain=True) as block):
        place, first = (R.place[:, q].rearrange("p n r -> p (n r)") for q in range(2))

        @block.gpsimd
        def _(pool):
            pool.wait_ge(s("rows_known"), 1)
            for r, n in ((0, P), (1, P), (2, NSAMP)):
                for q in range(2):
                    pool.indirect_dma_start(out=yr[0:n, q, r, :], out_offset=None, in_=K.d["rows"],
                                            in_offset=bass.IndirectOffsetOnAxis(ap=row[0:n, q, r:r + 1], axis=0)
                                            ).then_inc(K.rows_loaded[r], 16)

        @block.vector
        def _(dve):
            v, link = nc.vector, lambda ins: K.vc.link(dve, ins)
            v.tensor_scalar(w[:, 0], place, 0.0, None, ALU.is_ge)
            v.tensor_scalar(w[:, 1], place, CAP - 0.5, None, ALU.is_lt)
            link(v.tensor_scalar(w[:, 2], place, 0.0, CAP - 1.0, ALU.max, ALU.min))
            link(v.tensor_tensor(w[:, 2], w[:, 2], first, ALU.add))
            v.tensor_copy(row[:, :, :].rearrange("p n r -> p (n r)"), w[:, 2]).then_inc(s("rows_known"), 1)
            link(v.tensor_tensor(w[:, 3], w[:, 0], w[:, 1], ALU.mult))
            link(v.tensor_tensor(w[:, 4], w[:, 3], R.w[:, :, :].rearrange("p n r -> p (n r)"), ALU.mult))
            v.tensor_scalar(place, place, -float(CAP), None, ALU.add)
            v.tensor_scalar(R.pos[:, :, :], R.pos[:, :, :], -float(CAP), None, ALU.add)
            for r, n in ((0, P), (1, P), (2, NSAMP)):
                dve.wait_ge(K.rows_loaded[r], 32)
                link(v.tensor_scalar(yr[0:n, 0, r], yr[0:n, 0, r], w[0:n, 4, r:r + 1], None, ALU.mult))
                v.scalar_tensor_tensor(out=yr[0:n, 0, r], in0=yr[0:n, 1, r], scalar=w[0:n, 4, 3 + r:4 + r], in1=yr[0:n, 0, r],
                                       op0=ALU.mult, op1=ALU.add).then_inc(s("rows_summed"), 1)
            dve.wait_ge(s("moe_fm"), 1)
            for m in range(KD):
                residual(K, dve, K.ps[:, m, 0:T], tmp[:, m % 2], 40 + m, m, s("moe_residual"), m + 1)

        @block.tensor
        def _(pe):
            for r, (t0, n) in enumerate(((0, P), (P, P), (SEQ, NSAMP))):
                pe.wait_ge(s("rows_summed"), r + 1)
                for k in range(KD):
                    mm = pe.transpose(K.ps[:, k, t0:t0 + n], yr[0:n, 0, r, k * P:(k + 1) * P], K.ident[0:n, 0:n])
            mm.then_inc(s("moe_fm"), 1)




def build(nc, d, n_pool):
    K = Core()
    K.nc, K.d, K.n_pool = nc, d, n_pool
    with ExitStack() as ctx:
        def sb(name, shape, dt=F32):
            return ctx.enter_context(nc.sbuf_tensor("s_" + name, shape, dt))

        once = {n: ctx.enter_context(nc.semaphore(n)) for n in ("consts_loaded", "silu_c_ready")}
        K.rows_loaded = [ctx.enter_context(nc.semaphore(f"rows_loaded{r}")) for r in range(3)]
        phase_sems, phase = {}, [ExitStack()]

        def sem(name):
            if name not in phase_sems:
                phase_sems[name] = phase[0].enter_context(nc.semaphore(name))
            return phase_sems[name]

        def end_phase():
            with nc.Block(no_gpsimd_drain=True) as block:
                @block.sync
                def _(sp):
                    for semaphore in (*phase_sems.values(), *K.rows_loaded):
                        sp.sem_clear(semaphore)
            phase_sems.clear()
            phase[0].close()
            phase[0] = ExitStack()
            K.vc, K.ac = Chain(sem("dve_step")), Chain(sem("act_step"))

        K.sem = sem
        K.ps = ctx.enter_context(nc.psum_tensor("ps", [P, 8, 512], F32))
        K.x, K.h, K.proj = sb("x", [P, KD, T]), sb("h", [P, KD, T]), sb("proj", [P, NPROJ, T])
        K.dt, K.acs, K.wend, K.krope = sb("dt", [NH, T]), sb("acs", [NH, T]), sb("wend", [NH, T]), sb("krope", [ROPE, T])
        K.acol = sb("acol", [NH, 1])
        K.cols, K.mod, K.gain = sb("cols", [P, NCOLS]), sb("mod", [P, 48, NREQ]), sb("gain", [P, 2, 8, NREQ])
        K.silu_c, K.fin, K.table = sb("silu_c", [P, KD, NREQ]), sb("fin", [P, KD]), sb("table", [1, NB * NPAGE], I32)
        consts = {}
        for name, arr in constants().items():
            if name == "mask":
                continue
            consts[name] = sb("k_" + name, list(arr.shape))
        K.ident, K.ones, K.causal, K.keep = (consts[n] for n in ("ident", "ones", "causal", "keep"))
        K.selhead, K.selpair, K.ownb, K.own = (consts[n] for n in ("selhead", "selpair", "ownb", "own"))
        K.cos, K.sin, K.turn, K.eye = (consts[n] for n in ("cos", "sin", "turn", "eye"))
        K.later, K.iota, K.slot, K.first_slot = (consts[n] for n in ("later", "iota", "slot", "first_slot"))
        with nc.Block(no_gpsimd_drain=True) as block:
            @block.sync
            def _(sp):
                for dst, name in ((K.x, "x"), (K.silu_c, "c"), (K.fin, "fin"), (K.table, "table")):
                    sp.dma_start(whole(dst), d[name]).then_inc(once["consts_loaded"], 16)
                for name, dst in consts.items():
                    sp.dma_start(whole(dst), d["k_" + name]).then_inc(once["consts_loaded"], 16)
                sp.wait_ge(once["consts_loaded"], 16 * (4 + len(consts)))

            @block.scalar
            def _(act):
                act.wait_ge(once["consts_loaded"], 16 * (4 + len(consts)))
                nc.scalar.activation(K.silu_c[:, :, :], K.silu_c[:, :, :], ACT.Silu).then_inc(once["silu_c_ready"], 1)
                act.wait_ge(once["silu_c_ready"], 1)
        with nc.Fori(0, DEPTH) as l:
            K.vc, K.ac = Chain(sem("dve_step")), Chain(sem("act_step"))
            with (nc.sbuf_tensor("w_in_panels", [P, IN_SLOTS, KD, 256], F32) as win,
                  nc.sbuf_tensor("w_mod_panels", [P, 4, 2048], F32) as wmod):
                first_norm_stage(K, l, win, wmod)
                projection_stage(K, l, win, wmod)
            conv_stage(K, l)
            ssd_stage(K, l)
            with ExitStack() as e:
                G = Core()
                G.b, G.k, G.A = (e.enter_context(nc.sbuf_tensor(n, [P, 4, T], F32)) for n in ("hg_b", "hg_k", "hg_A"))
                G.A01 = e.enter_context(nc.sbuf_tensor("u_hg_A01", [P, 4, P], F32))
                G.eye = K.eye
                hgrn_gates_stage(K, l, G)
                hgrn_scores_stage(K, l, G)
                hgrn_output_stage(K, l, G)
            end_phase()
            with ExitStack() as e:
                A = Core()
                A.qa = e.enter_context(nc.sbuf_tensor("u_mla_qa", [P, 2, MH, T], F32))
                A.ckv = e.enter_context(nc.sbuf_tensor("u_mla_ckv", [P, 3, 256], F32))
                A.qr = K.proj[0:ROPE, HI0:HI0 + MH, :]
                mla_project_stage(K, l, A)
                A.keys = e.enter_context(nc.sbuf_tensor("page_keys", [P, 2, NPAGE, 384], F32))
                A.values = e.enter_context(nc.sbuf_tensor("page_values", [P, 2, NPAGE, 256], F32))
                mla_prompt_stage(K, l, A)
                mla_sample_stage(K, l, A)
                mla_value_stage(K, l, A)
            lru_stage(K, l)
            merge_stage(K, l)
            K.gate_up = K.proj[:, :, :].rearrange("p n t -> p (n t)")[:, 0:SLOTS * KD * 2 * HID].rearrange(
                "p (j k n) -> p j k n", j=SLOTS, k=KD)
            with nc.Block(no_gpsimd_drain=True) as block:
                @block.sync
                def _(sp):
                    for j in range(SLOTS):
                        load_expert(K, sp, l, slice(j, j + 1), j)
            norm_stage(K, 1, "n2")
            with ExitStack() as e:
                R = Core()
                R.hT = e.enter_context(nc.sbuf_tensor("h_tm_", [P, 3, D], F32))
                R.pos = e.enter_context(nc.sbuf_tensor("rt_pos", [P, 3, NEXP + 1], F32))
                R.w = e.enter_context(nc.sbuf_tensor("rt_w", [P, 2, 3], F32))
                R.place = e.enter_context(nc.sbuf_tensor("rt_place", [P, 2, 2, 3], F32))
                R.passes = e.enter_context(nc.sbuf_tensor("rt_passes", [1, 1], I32))
                router_stage(K, l, R)
                passes = nc.values_load(R.passes[0:1, 0:1], min_val=1, max_val=MAX_PASS)
                K.vc = Chain(sem("pass_dve_step"))
                with nc.Fori(0, passes) as turn:
                    experts_stage(K, l, R, turn)
                    combine_stage(K, l, R)
                    end_phase()
        norm_stage(K, 2, "nf")
        with nc.Block(no_gpsimd_drain=True) as block:
            @block.sync
            def _(sp):
                sp.dma_start(d["o_y"], K.h[:, :, :]).then_inc(sem("y_stored"), 16)
                sp.wait_ge(sem("y_stored"), 16)


def whole(t):
    return t[tuple(slice(None) for _ in t.shape)]


def constants():
    f = np.float32
    i, j = np.arange(P)[:, None], np.arange(P)[None, :]
    own64 = (i[:64] // TS == j[:, :64] // TS)
    causal = np.zeros((P, SEQ + P + NSAMP), f)
    causal[:, 0:P] = j >= i
    causal[:, P:SEQ] = 1
    causal[:, SEQ:SEQ + P] = j >= i
    causal[:64, SEQ + P:] = own64 & (j[:, :64] >= i[:64])
    selhead = np.zeros((NH, NH, P), f)
    selpair = np.zeros((NH, 4, P), f)
    for h in range(NH):
        selhead[h, h, :] = 1
        selpair[h, h // 2, 64 * (h % 2):64 * (h % 2) + 64] = 1
    keep = np.ones((P, T), f)
    keep[:, 0] = 0
    keep[:, SEQ::TS] = 0
    ownb = (np.arange(NSAMP)[:, None] // TS == np.arange(NB)[None, :]).astype(f)
    pos = np.concatenate([np.arange(SEQ), PAST + np.arange(NSAMP) % TS]).astype(f)
    half = ROPE // 2
    inv = (f(10000.0) ** (-np.arange(half, dtype=f) * f(2.0) / f(ROPE))).astype(f)
    ang = (pos[None, :] * inv[:, None]).astype(f)
    cos, sin = (np.concatenate([g(ang), g(ang)]).astype(f) for g in (np.cos, np.sin))
    turn = np.zeros((ROPE, ROPE), f)
    for n in range(half):
        turn[n + half, n] = -1
        turn[n, n + half] = 1
    eye = np.zeros((P, T), f)
    mask = np.zeros((P, len(HG_LEVELS) - 1, T), np.int32)
    for t0, n in ((0, P), (P, P), (SEQ, NSAMP)):
        a, b = i[:n], j[:, :n]
        eye[:n, t0:t0 + n] = a == b
        for q, L in enumerate(HG_LEVELS[:-1]):
            mask[:n, q, t0:t0 + n] = (a // L == b // L) & (a % L < L // 2) & (b % L >= L // 2)
    later = np.where(j > i, f(-BIG), f(0)).astype(f)
    own = np.full((P, NB // 2, NSAMP), -BIG, f)
    for b in range(NB):
        for h in range(MH):
            for t in range(TS):
                own[(b % 2) * NSAMP + h * TS + t, b // 2, b * TS:b * TS + t + 1] = 0
    iota = np.tile(np.arange(8, dtype=f), (P, 1))
    slot = np.tile(np.arange(CAP, dtype=f), (P, 1))
    first_slot = np.tile(np.arange(NEXP, dtype=f) * CAP, (P, 1))
    return dict(ident=np.eye(P, dtype=f), ones=np.ones((P, P), f), causal=causal, selhead=selhead, selpair=selpair,
                keep=keep, ownb=ownb, cos=cos, sin=sin, turn=turn, eye=eye, mask=mask, later=later, own=own, iota=iota, slot=slot,
                first_slot=first_slot)


OUTS = {"o_y": (P, KD, T), "o_conv": (DEPTH, P, 10, NREQ, 3), "o_ssm": (DEPTH, P, 4, NREQ, NST),
        "o_hgrn": (DEPTH, 4, P, NREQ, P), "o_ckv": (DEPTH, P, 2, T), "o_krope": (DEPTH, ROPE, T),
        "o_lru": (DEPTH, P, 4, NREQ)}


SCRATCH = {"rows": ((NEXP * CAP, D), F32)}


def lay_out(w):
    A = {k: np.asarray(v) for k, v in w.items()}
    Lr = DEPTH
    fm = lambda a: np.moveaxis(a.reshape(*a.shape[:-1], a.shape[-1] // P, P), (-1, -2), (0, 1))
    d = {}
    d["x"] = fm(np.concatenate([A["x_prompt"].reshape(SEQ, D), A["x_sample"].reshape(NSAMP, D)]))
    d["c"] = fm(np.concatenate([A["c_prompt"], A["c_sample"]]))
    d["fin"] = A["final_norm_g"].reshape(KD, P).T
    d["table"] = A["page_table"].reshape(1, NB * NPAGE)
    rows = lambda a: a.reshape(Lr, -1, P).transpose(0, 2, 1)
    first = np.zeros((Lr, P, 1), np.float32)
    first[1:] = 1
    taps = np.concatenate([A["ssd_conv_w"], A["lru_conv_w"]], axis=2).reshape(Lr, 4, 10, P).transpose(0, 3, 2, 1).reshape(Lr, P, 40)
    head = np.zeros((Lr, P, 2), np.float32)
    head[:, :NH, 0] = A["ssd_dt_bias"]
    head[:, :NH, 1] = A["ssd_a_log"]
    hg = rows(A["hg_lb_raw"])
    hg0, hg1 = np.stack([hg[0]] * Lr), np.stack([hg[1]] * Lr)
    dsk = np.broadcast_to(A["ssd_d"].reshape(Lr, 4, 2, 1), (Lr, 4, 2, 64)).reshape(Lr, 4, P).transpose(0, 2, 1)
    d["cols"] = np.concatenate([
        rows(A["norm1_g"]), rows(A["norm2_g"]), rows(A["b_mod"]), taps,
        rows(np.concatenate([A["ssd_conv_b"], A["lru_conv_b"]], axis=1)), rows(A["ssd_norm_g"]), hg0, hg1, first,
        rows(A["hg_norm_g"]), rows(A["mla_q_norm_g"]), rows(A["mla_kv_norm_g"]), rows(A["lru_b_r"]), rows(A["lru_b_i"]),
        rows(A["lru_a"]), dsk, head], axis=2)
    panels = lambda a, n: a.reshape(Lr, a.shape[1] // P, P, a.shape[2] // n, n).transpose(0, 3, 2, 1, 4)
    d["w_mod"] = A["w_mod"].reshape(Lr, KD, P, 3, 2048).transpose(0, 3, 1, 2, 4)
    W = A["w_in"]
    d["w_in"] = panels(np.concatenate([W[:, :, 0:1280], W[:, :, 1288:3848], W[:, :, 3880:]], axis=2), 256)
    d["w_small"] = np.concatenate([W[:, :, 3848:3880], W[:, :, 1280:1288]], axis=2).reshape(Lr, KD, P, 40).transpose(0, 2, 1, 3)
    st = np.concatenate([A["state_ssm_conv"], A["state_lru_conv"]], axis=3)
    d["conv_state"] = st.reshape(Lr, NB, 3, 10, P).transpose(0, 4, 3, 1, 2)
    S = A["state_ssm"]
    d["ssm_T"] = S.reshape(Lr, NB, 2, 4, HD, NST).transpose(0, 2, 5, 1, 3, 4).reshape(Lr, P, NB, 256)
    d["ssm_P"] = S.reshape(Lr, NB, 4, 2, HD, NST).transpose(0, 3, 4, 2, 1, 5).reshape(Lr, P, 4, NB, NST)
    d["hgrn"] = A["state_hgrn"].transpose(0, 2, 3, 1, 4)
    d["lru_state"] = A["state_lru"].reshape(Lr, NB, 4, P).transpose(0, 3, 2, 1)
    C, R = A["cache_kv_latent"], A["cache_k_rope"]
    n_pool = C.shape[1]
    keys = np.zeros((Lr, n_pool, P, 384), np.float32)
    keys[..., 0:256] = C.reshape(Lr, n_pool, P, 2, P).transpose(0, 1, 4, 3, 2).reshape(Lr, n_pool, P, 256)
    keys[:, :, 0:ROPE, 256:384] = R.transpose(0, 1, 3, 2)
    d["pages_k"], d["pages_v"] = keys, C
    d["w_uq"] = A["mla_w_uq"].reshape(Lr, 2, P, 768).transpose(0, 2, 1, 3)
    U = A["mla_w_ukv"].reshape(Lr, 256, MH, 128)
    d["w_uk"] = U[..., :64].transpose(0, 3, 2, 1)
    d["w_uv"] = U[..., 64:].reshape(Lr, 2, P, MH, 64).transpose(0, 2, 1, 3, 4)
    lw = np.zeros((Lr, P, 2, 4, P), np.float32)
    for n, name in enumerate(("lru_w_r", "lru_w_i")):
        B = A[name].reshape(Lr, 4, 2, 64, 64)
        for q in range(2):
            lw[:, 64 * q:64 * q + 64, n, :, 64 * q:64 * q + 64] = B[:, :, q].transpose(0, 2, 1, 3)
    d["lru_w"] = lw
    d["w_branch"] = A["w_branch"].reshape(Lr, 4, 4, P, 2, 512).transpose(0, 1, 4, 3, 2, 5).reshape(Lr, 8, P, 2048)
    d["w_out"] = A["w_out"].reshape(Lr, KD, P, 4, 256).transpose(0, 3, 2, 1, 4).reshape(Lr, 4, P, 2048)
    d["w_router"] = np.concatenate([A["moe_w_grp"], A["moe_w_rt"]], axis=2).reshape(Lr, KD, P, 36).transpose(0, 2, 1, 3)
    d["b_router"] = np.concatenate([A["moe_b_grp"], A["moe_b_rt"]], axis=1).reshape(Lr, 1, 36)
    GU = np.concatenate([A["moe_w_gate"], A["moe_w_up"]], axis=3)
    d["w_gate_up"] = GU.reshape(Lr, NEXP, KD, P, 2 * HID).transpose(0, 1, 3, 2, 4)
    d["w_down"] = A["moe_w_down"].reshape(Lr, NEXP, 2, P, D).transpose(0, 1, 3, 2, 4)
    for k, v in constants().items():
        d["k_" + k] = v
    return {k: np.ascontiguousarray(v) for k, v in d.items()}, n_pool


def outputs(r):
    y = r["o_y"].transpose(2, 1, 0).reshape(T, D)
    conv = r["o_conv"].transpose(0, 3, 4, 2, 1).reshape(DEPTH, NREQ, 3, 1280)
    ssm = r["o_ssm"].reshape(DEPTH, 2, HD, 4, NREQ, NST).transpose(0, 4, 3, 1, 2, 5).reshape(DEPTH, NREQ, NH, HD, NST)
    hgrn = r["o_hgrn"].transpose(0, 3, 1, 2, 4)
    ckv = r["o_ckv"].transpose(0, 3, 2, 1).reshape(DEPTH, T, 256)
    kr = r["o_krope"].transpose(0, 2, 1)
    lru = r["o_lru"].transpose(0, 3, 2, 1).reshape(DEPTH, NREQ, 512)
    res = [y[:SEQ].reshape(1, SEQ, D), y[SEQ:].reshape(NB, TS, D)]
    for sl, tok, shape in ((slice(0, 1), slice(0, SEQ), (DEPTH, 1, SEQ, -1)), (slice(1, NREQ), slice(SEQ, T), (DEPTH, NB, TS, -1))):
        res += [ckv[:, tok].reshape(shape), kr[:, tok].reshape(shape), ssm[:, sl], conv[:, sl, :, :768], hgrn[:, sl],
                lru[:, sl], conv[:, sl, :, 768:]]
    return tuple(np.ascontiguousarray(a) for a in res)


def kernel(**inputs):
    import concourse.bacc as bacc
    from concourse.bass_utils import run_bass_kernel_spmd

    nc = bacc.Bacc("TRN2", target_bir_lowering=False, num_devices=1)
    arrays, n_pool = lay_out(inputs)
    d = {n: nc.dram_tensor(n, a.shape, mybir.dt.from_np(a.dtype), kind="ExternalInput").ap() for n, a in arrays.items()}
    for n, shape in OUTS.items():
        d[n] = nc.dram_tensor(n, shape, F32, kind="ExternalOutput").ap()
    for n, (shape, dt) in SCRATCH.items():
        d[n] = nc.dram_tensor(n, shape, dt, kind="Internal").ap()
    build(nc, d, n_pool)
    r = run_bass_kernel_spmd(nc, [arrays], core_ids=[0])
    return outputs(r.results[0])
```

```python
from contextlib import ExitStack

import concourse.bass as bass
import numpy as np
from concourse import mybir

ALU = mybir.AluOpType
ACT = mybir.ActivationFunctionType
AX = mybir.AxisListType
F32 = mybir.dt.float32
I32 = mybir.dt.int32
U32 = mybir.dt.uint32

P = 128
DEPTH, D, SEQ, NB, TS = 2, 1024, 256, 8, 8
NSAMP = NB * TS
T = SEQ + NSAMP
KD = D // P
NREQ = 1 + NB
PAST, PAGE = 1024, 128
NPAGE = PAST // PAGE
EPS = 1e-6
NH, HD, NST = 8, 64, 64
HG_LEVELS = (2, 4, 8, 16, 32, 64, 128, 256)
MH, NOPE, ROPE = 8, 64, 32
ATT_SCALE = float((NOPE + ROPE) ** -0.5)
NEXP, HID = 32, 256
CAP, SLOTS = 64, 4
IN_SLOTS = 5
MAX_PASS = -(-T // CAP)
BIG = 1e30

Z0, XBC0, HQ0, HF0, HI0, HG0, QD0, KVD0, LX0, LY0, GL0 = 0, 4, 10, 14, 18, 22, 26, 28, 30, 34, 38
NPROJ = 70
C_N1, C_N2, C_BMOD, C_CW, C_CB, C_SSDN, C_HG0, C_HG1, C_SEL, C_HGN, C_QN, C_KVN, C_BR, C_BI, C_LA, C_DSK, C_DTB, C_ALOG = (
    0, 8, 16, 64, 104, 114, 118, 122, 126, 127, 128, 130, 132, 136, 140, 144, 148, 149)
NCOLS = 150


class Chain:

    def __init__(self, sem):
        self.sem, self.n = sem, 0

    def link(self, eng, ins):
        self.n += 1
        ins.then_inc(self.sem, 1)
        eng.wait_ge(self.sem, self.n)


class Core:
    pass


def root_of_mean(K, out, total, n):
    return K.nc.scalar.activation(out, total, ACT.Sqrt, bias=K.eps[:, 0:1], scale=1.0 / n)


def prompt(ap):
    return ap[:, :, 0:SEQ]


def sample(ap):
    return ap[:, :, SEQ:T].rearrange("p k (b t) -> p k b t", t=TS)


def mod_product(K, pe, bank, silu_c, panel, first, last):
    for q in range(4):
        mm = pe.matmul(K.ps[32 * q:32 * q + NREQ, bank, :], silu_c, panel[:, q * 512:(q + 1) * 512], start=first, stop=last)
    return mm


def spare_panel(wmod):
    return wmod[:, 2, 0:1024].rearrange("p (n c) -> p n c", n=2)


def mod_rows(K, dst, bank, part):
    for q in range(4):
        ins = K.nc.vector.tensor_copy(dst[32 * q:32 * q + NREQ, part, :], K.ps[32 * q:32 * q + NREQ, bank, :])
    return ins


def mod_turn(K, pe, rows, part, bank):
    for m in range(4):
        mm = pe.transpose(K.ps[:, bank, m * P:(m + 1) * P], rows[:, part, m * P:(m + 1) * P], K.ident[:, :])
    return mm


def mod_add_bias(K, bank, i):
    return K.nc.vector.tensor_tensor(
        K.mod[:, 16 * i:16 * i + 16, :].rearrange("p (q m) r -> p q m r", q=4),
        K.ps[:, bank, :].rearrange("p (m q r) -> p q m r", m=4, q=4)[:, :, :, 0:NREQ],
        K.cols[:, C_BMOD + 16 * i:C_BMOD + 16 * i + 16].rearrange("p (q m) -> p q m", q=4).unsqueeze(3
                                                                 ).to_broadcast([P, 4, 4, NREQ]), ALU.add)


def norm_gain(K, n, c):
    return K.nc.vector.scalar_tensor_tensor(out=K.gain[:, n], in0=K.mod[:, 24 * n + 8:24 * n + 16, :], scalar=1.0,
                                            in1=K.cols[:, c:c + 8].unsqueeze(2).to_broadcast([P, 8, NREQ]),
                                            op0=ALU.add, op1=ALU.mult)


def load_in_panel(K, sp, l, n, j, win):
    sp.dma_start(win[:, j], K.d["w_in"][l, n].rearrange("o p k n -> p (o k) n")).then_inc(K.sem(f"in_loaded{j}"), 16)


def load_late_mod(K, sp, l, k, wmod):
    for n in range(2):
        sp.dma_start(wmod[:, n], K.d["w_mod"][l, n + 1, k].rearrange("o p n -> p (o n)")).then_inc(K.sem(f"late_loaded{n}"), 16)


def first_norm_stage(K, l, win, wmod):
    nc, s = K.nc, K.sem
    rows = spare_panel(wmod)
    panels = K.proj[:, :, :].rearrange("p n t -> p (n t)")[:, 0:KD * 2048].rearrange("p (k n) -> p k n", k=KD)
    with nc.sbuf_tensor("n1_rstd_row", [P, T], F32) as rstd, nc.Block(no_gpsimd_drain=True) as block:
        @block.sync
        def _(sp):
            for k in range(KD):
                sp.dma_start(panels[:, k], K.d["w_mod"][l, 0, k]).then_inc(s(f"mod_loaded{k}"), 16)
            for j in range(IN_SLOTS):
                load_in_panel(K, sp, l, slice(j, j + 1), j, win)
            load_late_mod(K, sp, l, slice(0, 1), wmod)

        @block.scalar
        def _(act):
            act.dma_start(K.cols[:, :], K.d["cols"][l]).then_inc(s("cols_loaded"), 16)
            act.wait_ge(s("n1_sum"), 1)
            root_of_mean(K, rstd[:, :], K.ps[:, 0, 0:T], D).then_inc(s("n1_root"), 1)
            act.wait_ge(s("n1_ready"), 1)
            first_gain_and_shift(K, 0)

        @block.tensor
        def _(pe):
            pe.wait_ge(s("n1_squares"), 1)
            sum_over_partitions(K, pe, K.ps[:, 0, 0:T], [K.h[:, k, :] for k in range(KD)]).then_inc(s("n1_sum"), 1)
            for k in range(KD):
                pe.wait_ge(s(f"mod_loaded{k}"), 16)
                mm = mod_product(K, pe, 1, K.silu_c[:, k, :], panels[:, k], k == 0, k == KD - 1)
            mm.then_inc(s("mod_done"), 1)
            pe.wait_ge(s("mod_rows_copied"), 1)
            mod_turn(K, pe, rows, 0, 2).then_inc(s("mod_turned"), 1)

        @block.vector
        def _(dve):
            v, link = nc.vector, lambda ins: K.vc.link(dve, ins)
            v.tensor_tensor(K.h[:, :, :], K.x[:, :, :], K.x[:, :, :], ALU.mult).then_inc(s("n1_squares"), 1)
            link(v.memset(rows[:, 0, :], 0.0))
            dve.wait_ge(s("n1_root"), 1)
            link(v.reciprocal(rstd[:, :], rstd[:, :]))
            link(v.tensor_tensor(K.h[:, :, :], K.x[:, :, :], rstd[:, :].unsqueeze(1).to_broadcast([P, KD, T]), ALU.mult))
            dve.wait_ge(s("mod_done"), 1)
            mod_rows(K, rows, 1, 0).then_inc(s("mod_rows_copied"), 1)
            dve.wait_ge(s("cols_loaded"), 16)
            dve.wait_ge(s("mod_turned"), 1)
            link(mod_add_bias(K, 2, 0))
            link(norm_gain(K, 0, C_N1))
            dve.sem_inc(s("n1_ready"), 1)
            other_gain_and_shift(K, link, 0)


def first_gain_and_shift(K, n):
    for k in range(KD // 2):
        K.nc.scalar.activation(K.h[:, k, 0:SEQ], K.h[:, k, 0:SEQ], ACT.Identity, scale=K.gain[:, n, k, 0:1],
                               bias=K.mod[:, 24 * n + k, 0:1])


def other_gain_and_shift(K, link, n):
    for k in range(KD // 2, KD):
        K.nc.vector.tensor_scalar(K.h[:, k, 0:SEQ], K.h[:, k, 0:SEQ], K.gain[:, n, k, 0:1], K.mod[:, 24 * n + k, 0:1],
                                  ALU.mult, ALU.add)
    for op, a in ((ALU.mult, K.gain[:, n]), (ALU.add, K.mod[:, 24 * n:24 * n + 8, :])):
        link(K.nc.vector.tensor_tensor(sample(K.h), sample(K.h), a[:, :, 1:NREQ].unsqueeze(3).to_broadcast([P, KD, NB, TS]), op))


def sum_over_partitions(K, pe, out, tiles, start=True):
    for n, tile in enumerate(tiles):
        mm = pe.matmul(out, K.ones[:, :], tile, start=(n == 0), stop=(n == len(tiles) - 1))
    return mm


def norm_stage(K, n, tag, loads=None):
    nc, s = K.nc, K.sem
    with nc.sbuf_tensor(tag + "_rstd_row", [P, T], F32) as rstd, nc.Block(no_gpsimd_drain=True) as block:
        if loads:
            block.sync(loads)

        @block.vector
        def _(dve):
            v, link = nc.vector, lambda ins: K.vc.link(dve, ins)
            v.tensor_tensor(K.h[:, :, :], K.x[:, :, :], K.x[:, :, :], ALU.mult).then_inc(s(tag + "_squares"), 1)
            dve.wait_ge(s(tag + "_root"), 1)
            link(v.reciprocal(rstd[:, :], rstd[:, :]))
            if n == 2:
                for k in range(KD):
                    v.scalar_tensor_tensor(out=K.h[:, k, :], in0=K.x[:, k, :], scalar=K.fin[:, k:k + 1], in1=rstd[:, :],
                                           op0=ALU.mult, op1=ALU.mult)
                return
            link(v.tensor_tensor(K.h[:, :, :], K.x[:, :, :], rstd[:, :].unsqueeze(1).to_broadcast([P, KD, T]), ALU.mult))
            dve.sem_inc(s(tag + "_ready"), 1)
            other_gain_and_shift(K, link, n)

        @block.tensor
        def _(pe):
            pe.wait_ge(s(tag + "_squares"), 1)
            sum_over_partitions(K, pe, K.ps[:, 0, 0:T], [K.h[:, k, :] for k in range(KD)]).then_inc(s(tag + "_sum"), 1)

        @block.scalar
        def _(act):
            act.wait_ge(s(tag + "_sum"), 1)
            root_of_mean(K, rstd[:, :], K.ps[:, 0, 0:T], D).then_inc(s(tag + "_root"), 1)
            if n < 2:
                act.wait_ge(s(tag + "_ready"), 1)
                first_gain_and_shift(K, n)


def projection_stage(K, l, G, win, wmod):
    nc, s = K.nc, K.sem
    TRIP, BANKS = 10, 5
    TRIPS, MIXERS = NPROJ // TRIP, -(-GL0 // TRIP)
    MOD, SMALL = 5, 7
    rows, wsm = spare_panel(wmod), wmod[:, 2, 0:KD * (ROPE + NH)].rearrange("p (k c) -> p k c", k=KD)
    dtt = wmod[0:NH, 2, 1024:1024 + 3 * T].rearrange("p (q t) -> p q t", q=3)
    with (nc.sbuf_tensor("conv_in", [P, 10, NB, 3], F32) as cin, nc.sbuf_tensor("conv_out", [P, 10, NREQ, 3], F32) as cout,
          nc.sbuf_tensor("work", [P, 12 * T], F32) as work, nc.sbuf_tensor("hg_lb", [P, 4, 4], F32) as lb,
          nc.sbuf_tensor("silu_c_k", [P, NREQ], F32) as silu_k, nc.Block(no_gpsimd_drain=True) as block):
        xx = work[:, 0:10 * CONV_X].rearrange("p (c x) -> p c x", c=10)
        t = work[:, :].rearrange("p (n h t) -> p n h t", n=3, h=4)

        @block.sync
        def _(sp):
            for m in range(IN_SLOTS, TRIP):
                sp.wait_ge(s("in_evacuated"), m - IN_SLOTS + 1)
                load_in_panel(K, sp, l, slice(m, m + 1), m % IN_SLOTS, win)
            with sp.Fori(1, TRIPS) as i:
                for m in range(TRIP):
                    sp.wait_ge(s("in_evacuated"), i * TRIP + m - IN_SLOTS + 1)
                    load_in_panel(K, sp, l, bass.ds(i * TRIP + m, 1), m % IN_SLOTS, win)
                    if m == 0:
                        sp.wait_ge(s("late_used"), i)
                        load_late_mod(K, sp, l, bass.ds(i, 1), wmod)
            sp.wait_ge(s("late_used"), KD - 1)
            load_late_mod(K, sp, l, slice(KD - 1, KD), wmod)

        @block.tensor
        def _(pe):
            def late_mod(k, first, last):
                pe.wait_ge(s("silu_k_ready"), k + 1)
                for n in range(2):
                    pe.wait_ge(s(f"late_loaded{n}"), k * 16 + 16)
                for n in range(2):
                    mm = mod_product(K, pe, MOD + n, silu_k[:, :], wmod[:, n], first, last)
                mm.then_inc(s("late_used"), 1)

            for i0, i1 in ((0, 1), (1, MIXERS), (MIXERS, TRIPS - 1), (TRIPS - 1, TRIPS)):
                if i0 == MIXERS:
                    pe.wait_ge(s("small_loaded"), 16)
                    for k in range(KD):
                        mm = pe.matmul(K.ps[0:ROPE + NH, SMALL, 0:T], wsm[:, k, :], K.h[:, k, :],
                                       start=(k == 0), stop=(k == KD - 1))
                    mm.then_inc(s("small_done"), 1)
                with pe.Fori(i0, i1) as i:
                    for m in range(TRIP):
                        j = m % IN_SLOTS
                        pe.wait_ge(s(f"in_loaded{j}"), (i * TRIP // IN_SLOTS + m // IN_SLOTS) * 16 + 16)
                        if i0 or m >= BANKS:
                            pe.wait_ge(s("in_evacuated"), i * TRIP + m - BANKS + 1)
                        for k in range(KD):
                            mm = pe.matmul(K.ps[:, m % BANKS, 0:T], win[:, j, k, :], K.h[:, k, :],
                                           start=(k == 0), stop=(k == KD - 1))
                        mm.then_inc(s("in_tile_done"), 1)
                        if m == 3:
                            late_mod(i, i0 == 0, False)
                        if i0 == TRIPS - 1 and m == 7:
                            late_mod(KD - 1, False, True)
            pe.wait_ge(s("late_rows_copied"), 1)
            mod_turn(K, pe, rows, 0, MOD)
            mod_turn(K, pe, rows, 1, MOD + 1).then_inc(s("late_turned"), 1)

        @block.vector
        def _(dve):
            v, link = nc.vector, lambda ins: K.vc.link(dve, ins)
            with dve.Fori(0, MIXERS) as i:
                for m in range(TRIP):
                    dve.wait_ge(s("in_tile_done"), i * TRIP + m + 1)
                    v.tensor_copy(K.proj[:, bass.ds(i * TRIP + m, 1), :], K.ps[:, m % BANKS:m % BANKS + 1, 0:T]
                                  ).then_inc(s("in_evacuated"), 1)
            dve.wait_ge(s("small_done"), 1)
            v.tensor_copy(K.krope[:, :], K.ps[0:ROPE, SMALL, 0:T])
            v.tensor_copy(K.dt[:, :], K.ps[ROPE:ROPE + NH, SMALL, 0:T]).then_inc(s("dt_copied"), 1)
            link(v.memset(rows[:, :, :], 0.0))
            dve.wait_ge(s("in_evacuated"), MIXERS * TRIP)
            conv_on_vector(K, dve, link, xx, cin, cout)
            dt_on_vector(K, dve, link, dtt)
            hgrn_gates_on_vector(K, dve, link, G, t, lb)
            dve.wait_ge(s("late_used"), KD)
            mod_rows(K, rows, MOD, 0)
            mod_rows(K, rows, MOD + 1, 1).then_inc(s("late_rows_copied"), 1)
            dve.wait_ge(s("late_turned"), 1)
            mod_add_bias(K, MOD, 1)
            link(mod_add_bias(K, MOD + 1, 2))
            norm_gain(K, 1, C_N2)

        @block.scalar
        def _(act):
            a, link = nc.scalar, lambda ins: K.ac.link(act, ins)
            act.dma_start(wsm[:, :, :], K.d["w_small"][l]).then_inc(s("small_loaded"), 16)
            act.dma_start(cin[:, :, :, :], K.d["conv_state"][l]).then_inc(s("conv_in_loaded"), 16)

            def silu_c(k):
                a.copy(silu_k[:, :], K.silu_c[:, k, :]).then_inc(s("silu_k_ready"), 1)

            def gate_tiles(i):
                for m in range(TRIP):
                    act.wait_ge(s("in_tile_done"), i * TRIP + m + 1)
                    a.activation(K.proj[:, bass.ds(i * TRIP + m, 1), :], K.ps[:, m % BANKS:m % BANKS + 1, 0:T], ACT.Sigmoid
                                 ).then_inc(s("in_evacuated"), 1)
                    if m == 4:
                        next_silu_c(i + 1)

            def next_silu_c(k):
                act.wait_ge(s("late_used"), k)
                a.copy(silu_k[:, :], K.silu_c[:, bass.ds(k, 1), :].rearrange("p o r -> p (o r)")
                       ).then_inc(s("silu_k_ready"), 1)

            silu_c(0)
            with act.Fori(1, MIXERS + 1) as k:
                next_silu_c(k)
            act.wait_ge(s("in_evacuated"), MIXERS * TRIP)
            dt_on_scalar(K, act, link, dtt)
            with act.Fori(MIXERS, MIXERS + 1) as i:
                gate_tiles(i)
            act.wait_ge(s("conv_done"), 1)
            XBC = K.proj[:, XBC0:XBC0 + 6, :]
            a.activation(XBC, XBC, ACT.Silu)
            act.dma_start(K.d["o_conv"][l], cout[:, :, :, :]).then_inc(s("conv_stored"), 16)
            act.wait_ge(s("wend_arg"), 1)
            a.activation(dtt[:, 1, :], dtt[:, 0, :], ACT.Exp).then_inc(s("wend_exp"), 1)
            hgrn_gates_on_scalar(K, act, link, G, t, lb)
            with act.Fori(MIXERS + 1, TRIPS) as i:
                gate_tiles(i)
            early = K.proj[:, GL0:MIXERS * TRIP, :]
            a.activation(early, early, ACT.Sigmoid)
            act.wait_ge(s("conv_stored"), 16)


TAPS = 4
SEG = TS + TAPS - 1
CONV_S0 = TAPS - 1 + SEQ
CONV_X = CONV_S0 + NB * SEG


def conv_on_vector(K, dve, link, xx, cin, cout):
    v, s, W = K.nc.vector, K.sem, TAPS - 1
    seg = xx[:, :, CONV_S0:CONV_X].rearrange("p c (b t) -> p c b t", t=SEG)
    v.memset(xx[:, :, 0:W], 0.0)
    for c0, n, p0 in ((0, 6, XBC0), (6, 4, LX0)):
        v.tensor_copy(xx[:, c0:c0 + n, W:CONV_S0], prompt(K.proj)[:, p0:p0 + n, :])
        for b in range(NB):
            v.tensor_copy(xx[:, c0:c0 + n, CONV_S0 + b * SEG + W:CONV_S0 + (b + 1) * SEG],
                          K.proj[:, p0:p0 + n, SEQ + b * TS:SEQ + (b + 1) * TS])
    dve.wait_ge(s("conv_in_loaded"), 16)
    link(v.tensor_copy(seg[:, :, :, 0:W], cin[:, :, :, :]))
    v.tensor_copy(cout[:, :, 0, :], xx[:, :, SEQ:CONV_S0])
    v.tensor_copy(cout[:, :, 1:NREQ, :], seg[:, :, :, TS:SEG])
    for w in range(TAPS):
        for c in range(10):
            tile = XBC0 + c if c < 6 else LX0 + c - 6
            tap = K.cols[:, C_CW + 4 * c + w:C_CW + 4 * c + w + 1]
            for y, x in ((K.proj[:, tile, 0:SEQ], xx[:, c, w:w + SEQ]),
                         (K.proj[:, tile, SEQ:T].rearrange("p (b t) -> p b t", t=TS), seg[:, c, :, w:w + TS])):
                if w == 0:
                    ins = v.tensor_scalar(y, x, tap, K.cols[:, C_CB + c:C_CB + c + 1], ALU.mult, ALU.add)
                else:
                    ins = v.scalar_tensor_tensor(out=y, in0=x, scalar=tap, in1=y, op0=ALU.mult, op1=ALU.add)
        link(ins)
    dve.sem_inc(s("conv_done"), 1)


def dt_on_scalar(K, act, link, dtt):
    a, s = K.nc.scalar, K.sem
    act.wait_ge(s("dt_copied"), 1)
    link(a.activation(dtt[:, 0, :], K.dt[:, :], ACT.Identity, bias=K.cols[0:NH, C_DTB:C_DTB + 1]))
    link(a.activation(dtt[:, 1, :], dtt[:, 0, :], ACT.Abs))
    link(a.activation(K.acol[:, :], K.cols[0:NH, C_ALOG:C_ALOG + 1], ACT.Exp))
    link(a.activation(dtt[:, 1, :], dtt[:, 1, :], ACT.Exp, scale=-1.0))
    a.activation(dtt[:, 2, :], dtt[:, 1, :], ACT.Ln, bias=1.0).then_inc(s("dt_ready"), 1)


def dt_on_vector(K, dve, link, dtt):
    v, s = K.nc.vector, K.sem
    dve.wait_ge(s("dt_ready"), 1)
    link(v.scalar_tensor_tensor(out=K.dt[:, :], in0=dtt[:, 0, :], scalar=0.0, in1=dtt[:, 2, :], op0=ALU.max, op1=ALU.add))
    link(v.tensor_scalar(dtt[:, 2, :], K.dt[:, :], K.acol[:, 0:1], -1.0, ALU.mult, ALU.mult))
    link(v.tensor_tensor_scan(K.acs[:, :], K.keep[0:NH, :], dtt[:, 2, :], 0.0, ALU.mult, ALU.add))
    v.tensor_tensor(dtt[:, 0, 0:SEQ], K.acs[:, SEQ - 1:SEQ].to_broadcast([NH, SEQ]), K.acs[:, 0:SEQ], ALU.subtract)
    ac = K.acs[:, SEQ:T].rearrange("p (b t) -> p b t", t=TS)
    v.tensor_tensor(dtt[:, 0, SEQ:T].rearrange("p (b t) -> p b t", t=TS),
                    ac[:, :, TS - 1:TS].to_broadcast([NH, NB, TS]), ac, ALU.subtract).then_inc(s("wend_arg"), 1)
    dve.wait_ge(s("wend_exp"), 1)
    v.tensor_tensor(K.wend[:, :], dtt[:, 1, :], K.dt[:, :], ALU.mult)


def hgrn_gates_on_scalar(K, act, link, G, t, lb):
    a, s, x = K.nc.scalar, K.sem, K.proj[:, HF0:HF0 + 4, :]
    act.wait_ge(s("lb_diff"), 1)
    a.activation(lb[:, 3, :], lb[:, 3, :], ACT.Sigmoid).then_inc(s("lb_sig"), 1)
    a.activation(G.k[:, :, :], x, ACT.Sigmoid, scale=-1.0).then_inc(s("hg_sig"), 1)
    link(a.activation(t[:, 0], x, ACT.Abs))
    a.activation(t[:, 0], t[:, 0], ACT.Exp, scale=-1.0).then_inc(s("hg_eabs"), 1)
    act.wait_ge(s("hg_arg"), 1)
    a.activation(t[:, 1], t[:, 1], ACT.Exp)
    a.activation(t[:, 2], t[:, 2], ACT.Exp).then_inc(s("hg_e"), 1)
    act.wait_ge(s("hg_numer"), 1)
    a.activation(t[:, 1], t[:, 1], ACT.Ln).then_inc(s("hg_ln"), 1)
    act.wait_ge(s("hg_eabs"), 1)
    a.activation(t[:, 0], t[:, 0], ACT.Ln, bias=1.0).then_inc(s("hg_ln"), 1)


def hgrn_gates_on_vector(K, dve, link, G, t, lb):
    v, s, x = K.nc.vector, K.sem, K.proj[:, HF0:HF0 + 4, :]
    bc = lambda c: c.unsqueeze(2).to_broadcast([P, 4, T])
    v.tensor_tensor(lb[:, 3, :], K.cols[:, C_HG1:C_HG1 + 4], K.cols[:, C_HG0:C_HG0 + 4], ALU.subtract
                    ).then_inc(s("lb_diff"), 1)
    v.tensor_scalar(t[:, 1], x, 0.0, None, ALU.min)
    v.tensor_scalar(t[:, 2], x, 0.0, -1.0, ALU.max, ALU.mult).then_inc(s("hg_arg"), 1)
    dve.wait_ge(s("lb_sig"), 1)
    link(v.tensor_scalar(lb[:, 0, :], lb[:, 3, :], K.cols[:, C_SEL:C_SEL + 1], None, ALU.mult))
    v.tensor_scalar(lb[:, 1, :], lb[:, 0, :], -1.0, 1.0, ALU.mult, ALU.add)
    link(v.tensor_scalar(lb[:, 2, :], lb[:, 0, :], 0.0, None, ALU.is_equal))
    dve.wait_ge(s("hg_sig"), 1)
    v.tensor_tensor(G.k[:, :, :], G.k[:, :, :], bc(lb[:, 1, :]), ALU.mult)
    dve.wait_ge(s("hg_e"), 1)
    link(v.tensor_tensor(t[:, 2], t[:, 2], bc(lb[:, 0, :]), ALU.mult))
    link(v.tensor_tensor(t[:, 1], t[:, 1], t[:, 2], ALU.add))
    v.tensor_scalar(t[:, 1], t[:, 1], LN_FLOOR, None, ALU.max).then_inc(s("hg_numer"), 1)
    dve.wait_ge(s("hg_numer"), 1)
    link(v.tensor_scalar(t[:, 2], x, -LOG_LN_FLOOR, 0.0, ALU.add, ALU.min))
    link(v.tensor_tensor(t[:, 2], t[:, 2], bc(lb[:, 2, :]), ALU.mult))
    dve.wait_ge(s("hg_ln"), 2)
    link(v.tensor_tensor(t[:, 1], t[:, 1], t[:, 0], ALU.subtract))
    link(v.tensor_tensor(t[:, 1], t[:, 1], t[:, 2], ALU.add))
    for h in range(4):
        v.tensor_tensor_scan(G.b[:, h, :], K.keep[:, :], t[:, 1, h, :], 0.0, ALU.mult, ALU.add)


def ssd_stage(K, l):
    nc, s = K.nc, K.sem
    REG = ((0, P, 0, SEQ, 0), (P, P, P, P, SEQ), (SEQ, NSAMP, SEQ, NSAMP, SEQ + P))
    SC = SEQ + P + NSAMP
    ACS_BANKS = (0, 1, 5)
    with ExitStack() as e:
        sb = lambda n, sh: e.enter_context(nc.sbuf_tensor("t_" + n, sh, F32))
        xT, bT, rT = sb("ssd_xT", [P, 3, 512]), sb("ssd_bT", [P, 3, P]), sb("ssd_rT", [P, 3, 3, NH])
        xdt, xw = sb("ssd_xdt", [P, 3, 512]), sb("ssd_xw", [P, 3, 512])
        bmask = sb("ssd_bmask", [NSAMP, 2, NB, NST])
        cbm = sb("ssd_cbm", [P, 2, SC])
        E, M = sb("ssd_E", [P, 2, SC]), sb("ssd_M", [P, 2, SC])
        h0T = sb("ssd_h0T", [P, NB, 256])
        h0 = sb("ssd_h0", [P, 4, NB, NST])
        hout = sb("ssd_hout", [P, 4, NREQ, NST])
        ep = sb("ssd_ep", [P, 4, NSAMP])
        carried = sb("ssd_carried", [P, 2, 2, 256])
        zs, rstd = K.h[:, 0:4, :], K.h[:, 4, :]
        c_pad = K.h[:, 6, 0:NB * 32].rearrange("p (b t) -> p b t", b=NB)
        yi = K.h[:, 5, 0:4 * NSAMP].rearrange("p (q t) -> p q t", q=4)
        block = e.enter_context(nc.Block(no_gpsimd_drain=True))
        XB, BB, CB = K.proj[:, XBC0:XBC0 + 4], K.proj[:, XBC0 + 4], K.proj[:, XBC0 + 5]

        @block.sync
        def _(sp):
            sp.dma_start(h0T[:, :, :], K.d["ssm_T"][l]).then_inc(s("h0T_loaded"), 16)
            sp.dma_start(h0[:, :, :, :], K.d["ssm_P"][l]).then_inc(s("h0_loaded"), 16)
            sp.wait_ge(s("ssm_out_ready"), 1)
            sp.dma_start(K.d["o_ssm"][l], hout[:, :, :, :]).then_inc(s("ssm_stored"), 16)
            sp.wait_ge(s("ssm_stored"), 16)

        @block.tensor
        def _(pe):
            for r, (s0, n, _, _, _) in enumerate(REG):
                for c in range(4):
                    mm = pe.transpose(K.ps[0:n, r, c * P:(c + 1) * P], XB[:, c, s0:s0 + n], K.ident[:, :])
                mm = pe.transpose(K.ps[0:n, 3, r * P:(r + 1) * P], BB[:, s0:s0 + n], K.ident[:, :])
                for q, row in enumerate((K.acs, K.dt, K.wend)):
                    mm = pe.transpose(K.ps[0:n, 4, (r * 3 + q) * NH:(r * 3 + q + 1) * NH], row[:, s0:s0 + n],
                                      K.ident[0:NH, 0:NH])
            mm.then_inc(s("ssd_tm"), 1)
            for g in range(2):
                for s0, n, t0, m, c0 in REG:
                    mm = pe.matmul(K.ps[0:n, 5 + g, c0:c0 + m], BB[64 * g:64 * g + 64, s0:s0 + n],
                                   CB[64 * g:64 * g + 64, t0:t0 + m], start=True, stop=True)
            mm.then_inc(s("ssd_cb"), 1)
            for q in range(4):
                mm = pe.matmul(K.ps[:, 7, q * NSAMP:(q + 1) * NSAMP], K.selpair[:, q, :], K.acs[:, SEQ:T],
                               start=True, stop=True)
            mm.then_inc(s("ssd_acspair"), 1)
            pe.wait_ge(s("h0T_loaded"), 16)
            pe.wait_ge(s("ssd_ep"), 1)
            pe.wait_ge(s("ssd_tm_copied"), 1)
            pe.wait_ge(s("ssd_c_pad"), 1)
            for n in range(2):
                for j in range(4):
                    for g in range(2):
                        half = slice(64 * g, 64 * g + 64)
                        mm = pe.matmul(K.ps[32 * j:32 * j + 32, 7 - 3 * g, n * 256:(n + 1) * 256], c_pad[half, 4 * n + j, :],
                                       h0T[half, 4 * n + j, :], start=True, stop=True)
            mm.then_inc(s("ssd_carried"), 1)
            def spread_acs(h):
                if h >= 3:
                    pe.wait_ge(s("ssd_seg"), h - 2)
                pe.matmul(K.ps[:, ACS_BANKS[h % 3], 0:T], K.selhead[:, h, :], K.acs[:, :], start=True, stop=True
                          ).then_inc(s("ssd_acsb"), 1)

            pe.wait_ge(s("ssd_cbm"), 1)
            for h in range(3):
                spread_acs(h)
            pe.wait_ge(s("ssd_carried_copied"), 2)
            for q in range(4):
                for n in range(2):
                    mm = pe.matmul(K.ps[:, 7, q * NSAMP + n * 32:q * NSAMP + (n + 1) * 32],
                                   carried[:, q // 2, n, (q % 2) * P:(q % 2 + 1) * P], K.row_select[:, :], start=True, stop=True)
            mm.then_inc(s("ssd_inter"), 1)
            for h in range(NH):
                ssd_y(K, pe, h, REG, xdt, M)
                if h + 3 < NH:
                    spread_acs(h + 3)
            pe.wait_ge(s("ssd_xw"), 1)
            for q in range(4):
                g = q // 2
                for r in range(2):
                    mm = pe.matmul(K.ps[:, 4, q * NST:(q + 1) * NST], xw[:, r, q * P:(q + 1) * P],
                                   bT[:, r, 64 * g:64 * g + 64], start=(r == 0), stop=(r == 1))
            mm.then_inc(s("ssd_state_p"), 1)
            for q in range(4):
                g = q // 2
                if q >= 2:
                    pe.wait_ge(s("ssd_state_used"), q - 1)
                pe.matmul(K.ps[:, 5 + q % 2, :], xw[0:NSAMP, 2, q * P:(q + 1) * P],
                          bmask[:, g].rearrange("p b n -> p (b n)"), start=True, stop=True).then_inc(s("ssd_state"), 1)
            pe.wait_ge(s("ssd_sq"), 1)
            sum_over_partitions(K, pe, K.ps[:, 7, 0:T], [zs[:, q, :] for q in range(4)]).then_inc(s("ssd_ss"), 1)

        @block.vector
        def _(dve):
            v, link = nc.vector, lambda ins: K.vc.link(dve, ins)
            link(v.memset(c_pad, 0.0))
            v.tensor_copy(c_pad[:, :, 0:TS], CB[:, SEQ:T].rearrange("p (b t) -> p b t", t=TS)).then_inc(s("ssd_c_pad"), 1)
            v.memset(cbm[:, :, :], 0.0)
            v.memset(E[:, :, :], 0.0)
            v.memset(xT[:, 2, :], 0.0)
            link(v.memset(rT[:, 2], 0.0))
            dve.wait_ge(s("ssd_tm"), 1)
            v.tensor_copy(xT[:, 0:2, :], K.ps[:, 0:2, :])
            v.tensor_copy(xT[0:NSAMP, 2, :], K.ps[0:NSAMP, 2, :])
            v.tensor_copy(bT[:, 0:2, :].rearrange("p r n -> p (r n)"), K.ps[:, 3, 0:2 * P])
            v.tensor_copy(bT[0:NSAMP, 2, :], K.ps[0:NSAMP, 3, 2 * P:3 * P])
            v.tensor_copy(rT[:, 0:2].rearrange("p r q h -> p (r q h)"), K.ps[:, 4, 0:6 * NH])
            link(v.tensor_copy(rT[0:NSAMP, 2].rearrange("p q h -> p (q h)"), K.ps[0:NSAMP, 4, 6 * NH:9 * NH]))
            for out, q in ((xdt, 1), (xw, 2)):
                for r in range(3):
                    ins = v.tensor_tensor(out[:, r].rearrange("p (h d) -> p h d", h=NH),
                                          xT[:, r].rearrange("p (h d) -> p h d", h=NH),
                                          rT[:, r, q, :].unsqueeze(2).to_broadcast([P, NH, HD]), ALU.mult)
                if q == 1:
                    ins.then_inc(s("ssd_tm_copied"), 1)
            for g in range(2):
                ins = v.tensor_tensor(bmask[:, g], bT[0:NSAMP, 2, 64 * g:64 * g + 64].unsqueeze(1).to_broadcast([NSAMP, NB, NST]),
                                      K.ownb[:, :].unsqueeze(2).to_broadcast([NSAMP, NB, NST]), ALU.mult)
            ins.then_inc(s("ssd_xw"), 1)
            dve.wait_ge(s("ssd_cb"), 1)
            for g in range(2):
                v.tensor_tensor(cbm[:, g, 0:SEQ + P], K.ps[:, 5 + g, 0:SEQ + P], K.causal[:, 0:SEQ + P], ALU.mult)
                link(v.tensor_tensor(cbm[0:NSAMP, g, SEQ + P:SC], K.ps[0:NSAMP, 5 + g, SEQ + P:SC],
                                     K.causal[0:NSAMP, SEQ + P:SC], ALU.mult))
            dve.sem_inc(s("ssd_cbm"), 1)

            def decayed(h):
                dve.wait_ge(s("ssd_E"), h + 1)
                if h >= 2:
                    dve.wait_ge(s("ssd_y"), h - 1)
                v.tensor_tensor(M[:, h % 2, :], E[:, h % 2, :], cbm[:, h // 4, :], ALU.mult).then_inc(s("ssd_M"), 1)

            def carried_y():
                dve.wait_ge(s("ssd_inter"), 1)
                link(v.tensor_tensor(yi, K.ps[:, 7, 0:4 * NSAMP].rearrange("p (q t) -> p q t", q=4), ep[:, :, :], ALU.mult))

            def pair_y(q):
                dve.wait_ge(s("ssd_y"), 2 * q + 2)
                link(v.scalar_tensor_tensor(out=K.proj[:, Z0 + q, :], in0=XB[:, q, :],
                                            scalar=K.cols[:, C_DSK + q:C_DSK + q + 1], in1=K.ps[:, 2 + q % 2, 0:T],
                                            op0=ALU.mult, op1=ALU.add))
                link(v.tensor_tensor(K.proj[:, Z0 + q, SEQ:T], K.proj[:, Z0 + q, SEQ:T], yi[:, q, :], ALU.add))
                v.tensor_tensor(K.proj[:, Z0 + q, :], K.proj[:, Z0 + q, :], zs[:, q, :], ALU.mult).then_inc(s("ssd_pair"), 1)

            dve.wait_ge(s("ssd_zs"), 1)
            for h in range(NH):
                dve.wait_ge(s("ssd_acsb"), h + 1)
                if h >= 2:
                    dve.wait_ge(s("ssd_M"), h - 1)
                for r, (s0, n, t0, m, c0) in enumerate(REG):
                    ins = v.tensor_scalar(E[0:n, h % 2, c0:c0 + m], K.ps[0:n, ACS_BANKS[h % 3], t0:t0 + m], rT[0:n, r, 0, h:h + 1],
                                          0.0, ALU.subtract, ALU.min)
                ins.then_inc(s("ssd_seg"), 1)
                if h >= 1:
                    decayed(h - 1)
                if h == 2:
                    carried_y()
                if h >= 3 and h % 2:
                    pair_y(h // 2 - 1)
            decayed(NH - 1)
            pair_y(3)
            dve.wait_ge(s("ssd_pair"), 4)
            v.tensor_tensor(zs, K.proj[:, Z0:Z0 + 4, :], K.proj[:, Z0:Z0 + 4, :], ALU.mult).then_inc(s("ssd_sq"), 1)
            dve.wait_ge(s("h0_loaded"), 16)
            dve.wait_ge(s("ssd_state_p"), 1)
            link(v.tensor_copy(hout[:, :, 0, :], K.ps[:, 4, 0:4 * NST].rearrange("p (q n) -> p q n", q=4)))
            for q in range(4):
                end = ep[:, q, :].rearrange("p (b t) -> p b t", t=TS)[:, :, TS - 1:TS].to_broadcast([P, NB, NST])
                link(v.tensor_tensor(hout[:, q, 1:NREQ, :], h0[:, q], end, ALU.mult))
                dve.wait_ge(s("ssd_state"), q + 1)
                v.tensor_tensor(hout[:, q, 1:NREQ, :], hout[:, q, 1:NREQ, :],
                                K.ps[:, 5 + q % 2, :].rearrange("p (b n) -> p b n", b=NB), ALU.add
                                ).then_inc(s("ssd_state_used"), 1)
            dve.wait_ge(s("ssd_root"), 1)
            link(v.reciprocal(rstd, rstd))
            for q in range(4):
                v.scalar_tensor_tensor(out=K.proj[:, Z0 + q, :], in0=K.proj[:, Z0 + q, :],
                                       scalar=K.cols[:, C_SSDN + q:C_SSDN + q + 1], in1=rstd,
                                       op0=ALU.mult, op1=ALU.mult)
            dve.wait_ge(s("ssd_state_used"), 4)
            dve.sem_inc(s("ssm_out_ready"), 1)

        @block.scalar
        def _(act):
            a = nc.scalar
            a.activation(zs, K.proj[:, Z0:Z0 + 4, :], ACT.Silu).then_inc(s("ssd_zs"), 1)
            act.wait_ge(s("ssd_acspair"), 1)
            a.activation(ep[:, :, :].rearrange("p q t -> p (q t)"), K.ps[:, 7, 0:4 * NSAMP], ACT.Exp).then_inc(s("ssd_ep"), 1)
            act.wait_ge(s("ssd_carried"), 1)
            for g in range(2):
                a.copy(carried[:, g].rearrange("p n c -> p (n c)"), K.ps[:, 7 - 3 * g, :]).then_inc(s("ssd_carried_copied"), 1)
            for h in range(NH):
                act.wait_ge(s("ssd_seg"), h + 1)
                a.activation(E[:, h % 2, :], E[:, h % 2, :], ACT.Exp).then_inc(s("ssd_E"), 1)
            act.wait_ge(s("ssd_ss"), 1)
            root_of_mean(K, rstd, K.ps[:, 7, 0:T], 512).then_inc(s("ssd_root"), 1)


def ssd_y(K, pe, h, REG, xdt, M):
    q, s = h // 2, K.sem
    if h % 2 == 0 and q >= 2:
        pe.wait_ge(s("ssd_pair"), q - 1)
    pe.wait_ge(s("ssd_M"), h + 1)
    for r, (s0, n, t0, m, c0) in enumerate(REG):
        mm = pe.matmul(K.ps[64 * (h % 2):64 * (h % 2) + 64, 2 + q % 2, t0:t0 + m], xdt[0:n, r, h * HD:(h + 1) * HD],
                       M[0:n, h % 2, c0:c0 + m], start=(r != 1), stop=(r != 0))
    mm.then_inc(s("ssd_y"), 1)


def hgrn_scores_stage(K, l, G):
    nc, s = K.nc, K.sem
    TILES = ((0, P), (P, P), (SEQ, NSAMP))
    with (nc.sbuf_tensor("u_hg_D", [P, 3, 4, T], F32) as Dk, nc.sbuf_tensor("hg_mask", [P, len(HG_LEVELS) - 1, T], I32) as mask,
          nc.Block(no_gpsimd_drain=True) as block):
        q = K.proj[:, HQ0:HQ0 + 4, :]
        NL = len(HG_LEVELS)

        @block.sync
        def _(sp):
            sp.dma_start(mask[:, :, :], K.d["k_mask"]).then_inc(s("hg_mask_loaded"), 16)

        def halves(ap, L):
            if L <= TS:
                w = ap.rearrange("p h (n c) -> p (h n) c", c=L)
            else:
                w = ap[:, :, 0:SEQ].rearrange("p h (n c) -> p h n c", c=L)
            if L <= TS:
                return w[:, :, 0:L // 2], w[:, :, L // 2:L], w[:, :, L // 2 - 1:L // 2].to_broadcast([P, 4 * T // L, L // 2])
            return (w[:, :, :, 0:L // 2], w[:, :, :, L // 2:L],
                    w[:, :, :, L // 2 - 1:L // 2].to_broadcast([P, 4, SEQ // L, L // 2]))

        def width(L):
            return T if L <= TS else SEQ

        @block.vector
        def _(dve):
            v, link = nc.vector, lambda ins: K.vc.link(dve, ins)
            link(v.memset(G.A[:, :, SEQ:T], 0.0))

            def decays(n):
                L = HG_LEVELS[n]
                b1, b2, ref = halves(G.b, L)
                d1, d2, _ = halves(Dk[:, n % 3], L)
                v.tensor_tensor(d1, ref, b1, ALU.subtract)
                v.tensor_tensor(d2, b2, ref, ALU.subtract).then_inc(s("hg_seg"), 1)

            def weights(n):
                L = HG_LEVELS[n]
                dve.wait_ge(s("hg_D"), n + 1)
                d1, d2, _ = halves(Dk[:, n % 3], L)
                k1, _, _ = halves(G.k, L)
                _, q2, _ = halves(q, L)
                v.tensor_tensor(d1, d1, k1, ALU.mult)
                v.tensor_tensor(d2, d2, q2, ALU.mult).then_inc(s("hg_W"), 1)

            def place(n):
                L, B0 = HG_LEVELS[n], 4 * (n % 2)
                dve.wait_ge(s("hg_gram"), n + 2)
                if L == 256:
                    v.tensor_copy(G.A01[:, :, :], K.ps[:, B0:B0 + 4, 0:P])
                    return
                dve.wait_ge(s("hg_bank_free"), n + 1)
                m = mask[:, n, 0:SEQ].unsqueeze(1).to_broadcast([P, 4, SEQ])
                ins = v.copy_predicated(G.A[:, :, 0:SEQ], m, K.ps[:, B0:B0 + 4, 0:SEQ])
                if L <= TS:
                    m = mask[0:NSAMP, n, SEQ:T].unsqueeze(1).to_broadcast([NSAMP, 4, NSAMP])
                    ins = v.copy_predicated(G.A[0:NSAMP, :, SEQ:T], m, K.ps[0:NSAMP, B0:B0 + 4, SEQ:T])
                ins.then_inc(s("hg_bank_free"), 1)

            decays(0)
            decays(1)
            dve.wait_ge(s("hg_mask_loaded"), 16)
            dve.wait_ge(s("hg_gram"), 1)
            v.tensor_tensor(G.A[:, :, 0:SEQ], K.ps[:, 4:8, 0:SEQ], G.eye[:, 0:SEQ].unsqueeze(1).to_broadcast([P, 4, SEQ]), ALU.mult)
            link(v.tensor_tensor(G.A[0:NSAMP, :, SEQ:T], K.ps[0:NSAMP, 4:8, SEQ:T],
                                 G.eye[0:NSAMP, SEQ:T].unsqueeze(1).to_broadcast([NSAMP, 4, NSAMP]), ALU.mult))
            dve.sem_inc(s("hg_bank_free"), 1)
            for n in range(NL):
                weights(n)
                if n >= 1:
                    place(n - 1)
                if n + 2 < NL:
                    decays(n + 2)
            place(NL - 1)

        @block.scalar
        def _(act):
            for n, L in enumerate(HG_LEVELS):
                act.wait_ge(s("hg_seg"), n + 1)
                w = Dk[:, n % 3, :, 0:width(L)]
                nc.scalar.activation(w, w, ACT.Exp).then_inc(s("hg_D"), 1)

        @block.tensor
        def _(pe):
            for h in range(4):
                for t0, n in TILES:
                    mm = pe.matmul(K.ps[0:n, 4 + h, t0:t0 + n], G.k[:, h, t0:t0 + n], q[:, h, t0:t0 + n], start=True, stop=True)
            mm.then_inc(s("hg_gram"), 1)
            for n, L in enumerate(HG_LEVELS):
                pe.wait_ge(s("hg_W"), n + 1)
                if n >= 1:
                    pe.wait_ge(s("hg_bank_free"), n)
                W = Dk[:, n % 3]
                for h in range(4):
                    if L == 256:
                        mm = pe.matmul(K.ps[:, 4 * (n % 2) + h, 0:P], W[:, h, 0:P], W[:, h, P:SEQ], start=True, stop=True)
                        continue
                    for t0, w in TILES[:3 if L <= TS else 2]:
                        mm = pe.matmul(K.ps[0:w, 4 * (n % 2) + h, t0:t0 + w], W[:, h, t0:t0 + w], W[:, h, t0:t0 + w],
                                       start=True, stop=True)
                mm.then_inc(s("hg_gram"), 1)


def hgrn_output_stage(K, l, G):
    nc, s = K.nc, K.sem
    REG = ((0, P), (P, P), (SEQ, NSAMP))
    with ExitStack() as e:
        sb = lambda n, sh: e.enter_context(nc.sbuf_tensor("t_" + n, sh, F32))
        vT, kwT = sb("hg_vT", [P, 3, 4, P]), sb("hg_kwT", [P, 3, 4, P])
        kw, q_pad = sb("hg_kw", [P, 4, T]), sb("hg_q_pad", [P, 4, NB, 32])
        qe, carried = q_pad[:, :, :, 0:TS], sb("hg_carried", [P, 2, 2, P])
        vm, s0 = sb("hg_vm", [NSAMP, 2, NB, P]), sb("hg_s0", [P, 2, NB, P])
        sout = sb("hg_sout", [P, 2, NREQ, P])
        be, rstd = sb("hg_be", [P, 4, NB]), sb("hg_rstd", [P, 4, T])
        block = e.enter_context(nc.Block(no_gpsimd_drain=True))
        O = K.proj[:, HQ0:HQ0 + 4, :]

        @block.sync
        def _(sp):
            for h in range(4):
                if h >= 2:
                    sp.wait_ge(s("hg_state_ready"), h - 1)
                sp.dma_start(s0[:, h % 2], K.d["hgrn"][l, h]).then_inc(s(f"hg_s0_loaded{h % 2}"), 16)
            for h in range(4):
                sp.wait_ge(s("hg_state_ready"), h + 1)
                sp.dma_start(K.d["o_hgrn"][l, h], sout[:, h % 2]).then_inc(s(f"hg_stored{h % 2}"), 16)
            for j in range(2):
                sp.wait_ge(s(f"hg_stored{j}"), 32)

        @block.vector
        def _(dve):
            v, link = nc.vector, lambda ins: K.vc.link(dve, ins)
            bS = sample(G.b)

            def normalise(h):
                dve.wait_ge(s("hg_root"), h + 1)
                dve.wait_ge(s("hg_silu"), 1)
                link(v.reciprocal(rstd[:, h], rstd[:, h]))
                link(v.scalar_tensor_tensor(out=O[:, h], in0=O[:, h], scalar=K.cols[:, C_HGN:C_HGN + 1], in1=rstd[:, h],
                                            op0=ALU.mult, op1=ALU.mult))
                v.tensor_tensor(O[:, h], O[:, h], K.proj[:, HG0 + h, :], ALU.mult)

            v.memset(q_pad[:, :, :, TS:32], 0.0)
            v.tensor_copy(be[:, :, :], bS[:, :, :, TS - 1])
            v.tensor_tensor(prompt(kw), G.b[:, :, SEQ - 1:SEQ].to_broadcast([P, 4, SEQ]), prompt(G.b), ALU.subtract)
            v.tensor_tensor(sample(kw), bS[:, :, :, TS - 1:TS].to_broadcast([P, 4, NB, TS]), bS, ALU.subtract
                            ).then_inc(s("hg_kw_arg"), 1)
            dve.wait_ge(s("hg_kw_exp"), 1)
            v.tensor_tensor(qe, qe, sample(O), ALU.mult)
            v.tensor_tensor(kw[:, :, :], kw[:, :, :], G.k[:, :, :], ALU.mult).then_inc(s("hg_kw"), 1)
            for n, (dst, sig) in enumerate(((vT, "hg_vT"), (kwT, "hg_kwT"))):
                dve.wait_ge(s("hg_tm"), n + 1)
                v.tensor_copy(dst[:, 0:2].rearrange("p r h c -> p r (h c)"), K.ps[:, 0 + 3 * n:2 + 3 * n, :])
                v.tensor_copy(dst[0:NSAMP, 2].rearrange("p h c -> p (h c)"), K.ps[0:NSAMP, 2 + 3 * n, :]).then_inc(s(sig), 1)
            dve.wait_ge(s("hg_vT"), 1)
            for h in range(4):
                if h >= 2:
                    dve.wait_ge(s("hg_state"), h - 1)
                v.tensor_tensor(vm[:, h % 2], vT[0:NSAMP, 2, h].unsqueeze(1).to_broadcast([NSAMP, NB, P]),
                                K.ownb[:, :].unsqueeze(2).to_broadcast([NSAMP, NB, P]), ALU.mult).then_inc(s("hg_vm"), 1)
                dve.wait_ge(s(f"hg_s0_loaded{h % 2}"), 16 * (h // 2 + 1))
                if h >= 2:
                    dve.wait_ge(s(f"hg_stored{h % 2}"), 16 * (h // 2))
                link(v.tensor_tensor(sout[:, h % 2, 1:NREQ], s0[:, h % 2], be[:, h].unsqueeze(2).to_broadcast([P, NB, P]), ALU.mult))
                dve.wait_ge(s("hg_o"), h + 1)
                B = 4 * (h % 2)
                v.tensor_copy(O[:, h, :], K.ps[:, B, 0:T]).then_inc(s("hg_o_copied"), 1)
                dve.wait_ge(s("hg_state"), h + 1)
                v.tensor_copy(sout[:, h % 2, 0], K.ps[:, B + 1, 0:P])
                so = sout[:, h % 2, 1:NREQ].rearrange("p (a b) n -> p a (b n)", a=2)
                v.tensor_tensor(so, so, K.ps[:, B + 2:B + 4, :], ALU.add).then_inc(s("hg_state_ready"), 1)
                if h >= 1:
                    normalise(h - 1)
            normalise(3)

        @block.scalar
        def _(act):
            a = nc.scalar
            act.wait_ge(s("hg_kw_arg"), 1)
            a.activation(kw[:, :, :], kw[:, :, :], ACT.Exp)
            a.activation(qe, sample(G.b), ACT.Exp)
            a.activation(be[:, :, :], be[:, :, :], ACT.Exp).then_inc(s("hg_kw_exp"), 1)
            a.activation(K.proj[:, HG0:HG0 + 4, :], K.proj[:, HG0:HG0 + 4, :], ACT.Silu).then_inc(s("hg_silu"), 1)

            def root(h):
                act.wait_ge(s("hg_ss"), h + 1)
                root_of_mean(K, rstd[:, h], K.ps[:, 4 * (h % 2) + 1, P:P + T], P).then_inc(s("hg_root"), 1)

            for h in range(4):
                act.wait_ge(s("hg_carried"), h + 1)
                a.copy(carried[:, h % 2].rearrange("p n c -> p (n c)"), K.ps[:, 4 * (h % 2) + 1, P:3 * P]
                       ).then_inc(s("hg_carried_copied"), 1)
                act.wait_ge(s("hg_o_copied"), h + 1)
                a.activation(kw[:, h], O[:, h], ACT.Square).then_inc(s("hg_sq"), 1)
                if h >= 1:
                    root(h - 1)
            root(3)

        @block.tensor
        def _(pe):
            for h in range(4):
                for r, (t0, n) in enumerate(REG):
                    mm = pe.transpose(K.ps[0:n, r, h * P:(h + 1) * P], K.proj[:, HI0 + h, t0:t0 + n], K.ident[:, :])
            mm.then_inc(s("hg_tm"), 1)
            pe.wait_ge(s("hg_kw"), 1)
            for h in range(4):
                for r, (t0, n) in enumerate(REG):
                    mm = pe.transpose(K.ps[0:n, 3 + r, h * P:(h + 1) * P], kw[:, h, t0:t0 + n], K.ident[:, :])
            mm.then_inc(s("hg_tm"), 1)
            pe.wait_ge(s("hg_kwT"), 1)
            def sum_of_squares(h):
                pe.wait_ge(s("hg_sq"), h + 1)
                pe.wait_ge(s("hg_state_ready"), h + 1)
                pe.matmul(K.ps[:, 4 * (h % 2) + 1, P:P + T], K.ones[:, :], kw[:, h, :], start=True, stop=True
                          ).then_inc(s("hg_ss"), 1)

            for h in range(4):
                B = 4 * (h % 2)
                if h >= 2:
                    pe.wait_ge(s("hg_o_copied"), h - 1)
                    pe.wait_ge(s("hg_root"), h - 1)
                pe.wait_ge(s(f"hg_s0_loaded{h % 2}"), 16 * (h // 2 + 1))
                for b in range(NB):
                    r0, c0 = 32 * (b % 4), P * (1 + b // 4)
                    mm = pe.matmul(K.ps[r0:r0 + 32, B + 1, c0:c0 + P], q_pad[:, h, b, :], s0[:, h % 2, b], start=True, stop=True)
                mm.then_inc(s("hg_carried"), 1)
                o = K.ps[:, B, :]
                pe.matmul(o[:, 0:P], vT[:, 0, h], G.A[:, h, 0:P], start=True, stop=True)
                pe.matmul(o[:, P:SEQ], vT[:, 0, h], G.A01[:, h], start=True, stop=False)
                pe.matmul(o[:, P:SEQ], vT[:, 1, h], G.A[:, h, P:SEQ], start=False, stop=True)
                pe.matmul(o[:, SEQ:T], vT[0:NSAMP, 2, h], G.A[0:NSAMP, h, SEQ:T], start=True, stop=False)
                pe.wait_ge(s("hg_carried_copied"), h + 1)
                for n in range(2):
                    mm = pe.matmul(o[:, SEQ + n * 32:SEQ + (n + 1) * 32], carried[:, h % 2, n], K.row_select[:, :],
                                   start=False, stop=(n == 1))
                mm.then_inc(s("hg_o"), 1)
                pe.matmul(K.ps[:, B + 1, 0:P], kwT[:, 0, h], vT[:, 0, h], start=True, stop=False)
                pe.matmul(K.ps[:, B + 1, 0:P], kwT[:, 1, h], vT[:, 1, h], start=False, stop=True)
                pe.wait_ge(s("hg_vm"), h + 1)
                for j in range(2):
                    mm = pe.matmul(K.ps[:, B + 2 + j, :], kwT[0:NSAMP, 2, h],
                                   vm[:, h % 2, 4 * j:4 * j + 4].rearrange("p b n -> p (b n)"), start=True, stop=True)
                mm.then_inc(s("hg_state"), 1)
                if h >= 1:
                    sum_of_squares(h - 1)
            sum_of_squares(3)


LN_FLOOR = 1e-18
LOG_LN_FLOOR = -41.44653167389282


def lru_gates_on_scalar(K, act, link, U):
    a, s = K.nc.scalar, K.sem
    link(a.activation(U.soft[:, 0], K.cols[:, C_LA:C_LA + 4], ACT.Abs))
    link(a.activation(U.soft[:, 0], U.soft[:, 0], ACT.Exp, scale=-1.0))
    a.activation(U.soft[:, 1], U.soft[:, 0], ACT.Ln, bias=1.0).then_inc(s("lru_ln"), 1)
    for n in range(8):
        dst, c0, c = (U.r, C_BR, n) if n < 4 else (U.i, C_BI, n - 4)
        act.wait_ge(s("lru_gates"), n + 1)
        a.activation(dst[:, c], K.ps[:, 6 + n % 2, 0:T], ACT.Sigmoid, bias=K.cols[:, c0 + c:c0 + c + 1]
                     ).then_inc(s("lru_gate_read"), 1)


def lru_decay_on_scalar(K, act, U):
    a, s = K.nc.scalar, K.sem
    act.wait_ge(s("lru_loga"), 1)
    a.activation(U.t[:, :, :], U.r, ACT.Tanh).then_inc(s("lru_tanh"), 1)
    act.wait_ge(s("lru_tanh"), 1)
    a.activation(U.r, U.r, ACT.Exp).then_inc(s("lru_a"), 1)


def lru_output_gate_on_scalar(K, act, U):
    a, s = K.nc.scalar, K.sem
    act.wait_ge(s("lru_m2"), 1)
    a.activation(U.t[:, :, :], U.t[:, :, :], ACT.Sqrt).then_inc(s("lru_mult"), 1)
    a.activation(U.Y, U.Y, ACT.Gelu_apprx_tanh).then_inc(s("lru_gelu"), 1)


def lru_log_decay(K, dve, link, U):
    v, s = K.nc.vector, K.sem
    link(v.tensor_scalar(U.soft[:, 2], K.cols[:, C_LA:C_LA + 4], -1.0, 0.0, ALU.mult, ALU.max))
    dve.wait_ge(s("lru_ln"), 1)
    link(v.tensor_tensor(U.soft[:, 2], U.soft[:, 2], U.soft[:, 1], ALU.add))
    link(v.tensor_scalar(U.soft[:, 3], U.soft[:, 2], -8.0, None, ALU.mult))
    dve.wait_ge(s("lru_gate_read"), 8)
    v.tensor_tensor(U.r, U.r, U.soft[:, 3].unsqueeze(2).to_broadcast([P, 4, T]), ALU.mult).then_inc(s("lru_loga"), 1)
    link(v.tensor_tensor(U.i, U.i, U.X, ALU.mult))


def lru_one_plus_square(K, dve, link, U):
    v, s = K.nc.vector, K.sem
    dve.wait_ge(s("lru_a"), 1)
    link(v.tensor_tensor(U.X, U.r, U.r, ALU.mult))
    link(v.tensor_scalar(U.X, U.X, 1.0, -1.0, ALU.add, ALU.mult))


def lru_multiplier(K, dve, link, U):
    v, s = K.nc.vector, K.sem
    link(v.tensor_tensor(U.t[:, :, :], U.t[:, :, :], U.X, ALU.mult))
    v.tensor_scalar(U.t[:, :, :], U.t[:, :, :], 1e-30, None, ALU.max).then_inc(s("lru_m2"), 1)


def lru_input(K, dve, link, U):
    v, s = K.nc.vector, K.sem
    dve.wait_ge(s("lru_mult"), 1)
    link(v.memset(U.t[:, :, 0:1], 1.0))
    link(v.tensor_tensor(U.t[:, :, :], U.t[:, :, :], U.i, ALU.mult))


def lru_carry_in(K, dve, link, U):
    v, s = K.nc.vector, K.sem
    dve.wait_ge(s("lru_h0_loaded"), 16)
    link(v.tensor_tensor(U.h0[:, :, :], U.h0[:, :, :], sample(U.r)[:, :, :, 0], ALU.mult))
    link(v.tensor_tensor(sample(U.t)[:, :, :, 0], sample(U.t)[:, :, :, 0], U.h0[:, :, :], ALU.add))
    link(v.tensor_tensor(U.r, U.r, K.keep[:, :].unsqueeze(1).to_broadcast([P, 4, T]), ALU.mult))


def lru_scan(K, dve, link, U):
    v, s = K.nc.vector, K.sem
    row = lambda ap: ap.rearrange("p c t -> p (c t)")
    link(v.tensor_tensor_scan(row(U.X), row(U.r), row(U.t[:, :, :]), 0.0, ALU.mult, ALU.add))
    v.tensor_copy(U.out[:, :, 0:1], U.X[:, :, SEQ - 1:SEQ])
    v.tensor_copy(U.out[:, :, 1:NREQ], sample(U.X)[:, :, :, TS - 1]).then_inc(s("lru_out_ready"), 1)


def lru_output(K, dve, link, U):
    v, s = K.nc.vector, K.sem
    dve.wait_ge(s("lru_gelu"), 1)
    v.tensor_tensor(U.Y, U.X, U.Y, ALU.mult)


def mla_project_stage(K, l, A):
    nc, s = K.nc, K.sem
    with ExitStack() as e:
        sb = lambda n, sh: e.enter_context(nc.sbuf_tensor("t_" + n, sh, F32))
        wuq, wuk = sb("w_uq", [P, 2, MH * P]), sb("w_uk", [NOPE, MH, 256])
        sq, rstd = sb("mla_sq", [P, 4, T]), sb("mla_rstd", [P, 2, T])
        qn, rot = sb("mla_qn", [NOPE, 2, T]), sb("mla_rot", [ROPE, 2, T])
        U = Core()
        U.w, U.t = sb("lru_w", [P, 2, 4, P]), sb("lru_t", [P, 4, T])
        U.soft, U.h0, U.out = sb("lru_soft", [P, 4, 4]), sb("lru_h0", [P, 4, NB]), sb("lru_out", [P, 4, NREQ])
        U.r, U.i = K.h[:, 0:4, :], K.h[:, 4:8, :]
        U.X, U.Y = K.proj[:, LX0:LX0 + 4, :], K.proj[:, LY0:LY0 + 4, :]
        block = e.enter_context(nc.Block(no_gpsimd_drain=True))
        C = K.proj[:, QD0:QD0 + 4, :]

        @block.sync
        def _(sp):
            sp.dma_start(wuq[:, :, :], K.d["w_uq"][l]).then_inc(s("uq_loaded"), 16)
            sp.dma_start(wuk[:, :, :], K.d["w_uk"][l]).then_inc(s("uk_loaded"), 16)
            sp.wait_ge(s("mla_normed"), 1)
            sp.dma_start(K.d["o_ckv"][l], K.proj[:, KVD0:KVD0 + 2, :]).then_inc(s("ckv_stored"), 16)
            sp.wait_ge(s("krope_ready"), 1)
            sp.dma_start(K.d["o_krope"][l], K.krope[:, :]).then_inc(s("krope_stored"), 16)
            sp.wait_ge(s("ckv_stored"), 16)
            sp.wait_ge(s("krope_stored"), 16)

        @block.vector
        def _(dve):
            v, link = nc.vector, lambda ins: K.vc.link(dve, ins)
            v.tensor_tensor(sq[:, :, :], C, C, ALU.mult).then_inc(s("mla_sq"), 1)
            dve.wait_ge(s("mla_root"), 1)
            link(v.reciprocal(rstd[:, :, :], rstd[:, :, :]))
            for c in range(4):
                ins = v.scalar_tensor_tensor(out=C[:, c], in0=C[:, c], scalar=K.cols[:, C_QN + c:C_QN + c + 1],
                                             in1=rstd[:, c // 2, :], op0=ALU.mult, op1=ALU.mult)
            ins.then_inc(s("mla_normed"), 1)
            dve.wait_ge(s("krope_turned"), 1)
            link(v.tensor_tensor(rot[:, 0], K.ps[0:ROPE, 2, 0:T], K.sin[:, :], ALU.mult))
            link(v.tensor_tensor(K.krope[:, :], K.krope[:, :], K.cos[:, :], ALU.mult))
            v.tensor_tensor(K.krope[:, :], K.krope[:, :], rot[:, 0], ALU.add).then_inc(s("krope_ready"), 1)
            dve.wait_ge(s("ckv_tm"), 1)
            for r, n in enumerate((P, P, NSAMP)):
                v.tensor_copy(A.ckv[0:n, r, :], K.ps[0:n, 3 + r, 0:256])
            dve.sem_inc(s("ckv_tm_copied"), 1)
            dve.wait_ge(s("krope_ready"), 1)
            for h in range(MH):
                if h >= 2:
                    dve.wait_ge(s("q_abs_done"), h - 1)
                dve.wait_ge(s("q_head_done"), h + 1)
                head = K.ps[:, h % 2, 0:T]
                v.tensor_copy(qn[:, h % 2], head[0:NOPE]).then_inc(s("q_nope_copied"), 1)
                v.tensor_tensor(A.qr[:, h], head[NOPE:NOPE + ROPE], K.cos[:, :], ALU.mult)
                ins = v.tensor_tensor(rot[:, h % 2], head[NOPE + ROPE:P], K.sin_turned[:, :], ALU.mult)
                ins.then_inc(s("q_rope_read"), 1)
                dve.wait_ge(s("q_rope_read"), h + 1)
                v.tensor_tensor(A.qr[:, h], A.qr[:, h], rot[:, h % 2], ALU.add)
                if h == 0:
                    lru_log_decay(K, dve, link, U)
                if h == 2:
                    lru_one_plus_square(K, dve, link, U)
                if h == 3:
                    lru_multiplier(K, dve, link, U)
                if h == 4:
                    lru_input(K, dve, link, U)
                if h == 5:
                    lru_carry_in(K, dve, link, U)
                if h == 6:
                    lru_scan(K, dve, link, U)
                if h == 7:
                    lru_output(K, dve, link, U)

        @block.scalar
        def _(act):
            a, link = nc.scalar, lambda ins: K.ac.link(act, ins)
            act.dma_start(U.w[:, :, :, :], K.d["lru_w"][l]).then_inc(s("lru_w_loaded"), 16)
            act.dma_start(U.h0[:, :, :], K.d["lru_state"][l]).then_inc(s("lru_h0_loaded"), 16)
            act.wait_ge(s("mla_ss"), 1)
            root_of_mean(K, rstd[:, :, :], K.ps[:, 0:2, 0:T], 256).then_inc(s("mla_root"), 1)

            def copy_absorbed(heads):
                for h in heads:
                    act.wait_ge(s("q_abs_done"), h + 1)
                    a.copy(A.qa[:, :, h, :], K.ps[:, 3 + 2 * (h % 2):5 + 2 * (h % 2), 0:T]).then_inc(s("q_abs_copied"), 1)

            lru_gates_on_scalar(K, act, link, U)
            copy_absorbed(range(0, 2))
            lru_decay_on_scalar(K, act, U)
            copy_absorbed(range(2, 4))
            lru_output_gate_on_scalar(K, act, U)
            copy_absorbed(range(4, MH))
            act.wait_ge(s("lru_out_ready"), 1)
            act.dma_start(K.d["o_lru"][l], U.out[:, :, :]).then_inc(s("lru_stored"), 16)
            act.wait_ge(s("lru_stored"), 16)

        @block.tensor
        def _(pe):
            pe.matmul(K.ps[0:ROPE, 2, 0:T], K.turn[:, :], K.krope[:, :], start=True, stop=True).then_inc(s("krope_turned"), 1)
            pe.wait_ge(s("mla_sq"), 1)
            sum_over_partitions(K, pe, K.ps[:, 0, 0:T], [sq[:, 0], sq[:, 1]])
            sum_over_partitions(K, pe, K.ps[:, 1, 0:T], [sq[:, 2], sq[:, 3]]).then_inc(s("mla_ss"), 1)
            pe.wait_ge(s("lru_w_loaded"), 16)
            for n in range(8):
                if n >= 2:
                    pe.wait_ge(s("lru_gate_read"), n - 1)
                pe.matmul(K.ps[:, 6 + n % 2, 0:T], U.w[:, n // 4, n % 4, :], U.X[:, n % 4], start=True, stop=True
                          ).then_inc(s("lru_gates"), 1)
            pe.wait_ge(s("mla_normed"), 1)
            for r, (t0, n) in enumerate(((0, P), (P, P), (SEQ, NSAMP))):
                for c in range(2):
                    mm = pe.transpose(K.ps[0:n, 3 + r, c * P:(c + 1) * P], C[:, 2 + c, t0:t0 + n], K.ident[:, :])
            mm.then_inc(s("ckv_tm"), 1)
            pe.wait_ge(s("uq_loaded"), 16)

            def head(h):
                if h >= 2:
                    pe.wait_ge(s("q_nope_copied"), h - 1)
                    pe.wait_ge(s("q_rope_read"), h - 1)
                for k in range(2):
                    mm = pe.matmul(K.ps[:, h % 2, 0:T], wuq[:, k, h * P:(h + 1) * P], C[:, k], start=(k == 0), stop=(k == 1))
                mm.then_inc(s("q_head_done"), 1)

            head(0)
            for h in range(MH):
                if h + 1 < MH:
                    head(h + 1)
                pe.wait_ge(s("q_nope_copied"), h + 1)
                if h == 0:
                    pe.wait_ge(s("uk_loaded"), 16)
                    pe.wait_ge(s("ckv_tm_copied"), 1)
                if h == 1:
                    pe.wait_ge(s("lru_gate_read"), 8)
                if h >= 2:
                    pe.wait_ge(s("q_abs_copied"), h - 1)
                for c in range(2):
                    mm = pe.matmul(K.ps[:, 3 + 2 * (h % 2) + c, 0:T], wuk[:, h, c * P:(c + 1) * P], qn[:, h % 2],
                                   start=True, stop=True)
                mm.then_inc(s("q_abs_done"), 1)


def mla_prompt_stage(K, l, A):
    nc, s = K.nc, K.sem
    spare = K.h[:, :, :].rearrange("p k t -> p (k t)")[:, 0:2 * MH * P]
    pT = spare.rearrange("p (j h q) -> p j h q", j=2, h=MH)
    with (nc.sbuf_tensor("u_pr_p", [P, MH, SEQ], F32) as p_all, nc.sbuf_tensor("pr_stat", [P, 4, 4, 4], F32) as st,
          nc.Block(no_gpsimd_drain=True) as block):
        p = (pT[:, 1], p_all)
        TURNS = ((0, 0, 0), (0, 1, 0), (1, 0, 0), (1, 0, 1), (1, 1, 0), (1, 1, 1))
        heads = lambda g: slice(4 * g, 4 * g + 4)

        def scores(n, g, j):
            return K.ps[:, 6 + g if n == 0 else 2 * j + g, :].rearrange("p (h k) -> p h k", h=4)

        @block.sync
        def _(sp):
            for g in range(2):
                pages = page_numbers(K, sp, 0, g)
                load_keys(K, sp, l, g, pages, A.keys)
                load_values(K, sp, l, g, pages, A.values)

        @block.tensor
        def _(pe):
            def score(n, g):
                q0 = n * P
                for j in range(n + 1):
                    for h in range(4 * g, 4 * g + 4):
                        out = scores(n, g, j)[:, h % 4]
                        for c in range(2):
                            pe.matmul(out, A.qa[:, c, h, q0:q0 + P], K.proj[:, KVD0 + c, j * P:(j + 1) * P],
                                      start=(c == 0), stop=False)
                        mm = pe.matmul(out, A.qr[:, h, q0:q0 + P], K.krope[:, j * P:(j + 1) * P], start=False, stop=True)
                mm.then_inc(s("pr_scores"), 1)

            def turn(u):
                n, g, j = TURNS[u]
                pe.wait_ge(s("pr_p"), 2 * n + g + 1)
                if u >= 2:
                    pe.wait_ge(s("pr_pT_copied"), u - 1)
                for h in range(4):
                    mm = pe.transpose(K.ps[:, 4 + u % 2, h * P:(h + 1) * P], p[n][:, 4 * g + h, j * P:(j + 1) * P], K.ident[:, :])
                mm.then_inc(s("pr_pT"), 1)

            def value(n, g, last_turn):
                pe.wait_ge(s("pr_pT_copied"), last_turn + 1)
                if n + g == 0:
                    pe.wait_ge(s("pr_arg"), 2)
                else:
                    pe.wait_ge(s("pr_o_copied"), 2 * n + g)
                for c in range(2):
                    for j in range(n + 1):
                        mm = pe.matmul(K.ps[:, 6 + c, :], A.ckv[:, j, c * P:(c + 1) * P],
                                       pT[:, j, heads(g)].rearrange("p h q -> p (h q)"), start=(j == 0), stop=(j == n))
                mm.then_inc(s("pr_o"), 1)

            score(0, 0)
            score(0, 1)
            score(1, 0)
            turn(0)
            turn(1)
            score(1, 1)
            value(0, 0, 0)
            value(0, 1, 1)
            turn(2)
            turn(3)
            value(1, 0, 3)
            turn(4)
            turn(5)
            value(1, 1, 5)

        @block.vector
        def _(dve):
            v, link = nc.vector, lambda ins: K.vc.link(dve, ins)

            def less_maximum(n, g):
                q = 2 * n + g
                dve.wait_ge(s("pr_scores"), q + 1)
                own = scores(n, g, n)
                link(v.tensor_tensor(own, own, K.later[:, :].unsqueeze(1).to_broadcast([P, 4, P]), ALU.add))
                for j in range(n + 1):
                    ins = v.tensor_reduce(st[:, q, j, :], scores(n, g, j), AX.X, ALU.max)
                link(ins)
                if n:
                    link(v.tensor_tensor(st[:, q, 0, :], st[:, q, 0, :], st[:, q, 1, :], ALU.max))
                for j in range(n + 1):
                    ins = v.tensor_tensor(p[n][:, heads(g), j * P:(j + 1) * P], scores(n, g, j),
                                          st[:, q, 0, :].unsqueeze(2).to_broadcast([P, 4, P]), ALU.subtract)
                ins.then_inc(s("pr_arg"), 1)

            def divide(n, g):
                q, w = 2 * n + g, p[n][:, heads(g), :]
                dve.wait_ge(s("pr_exp"), q + 1)
                link(v.tensor_reduce(st[:, q, 2, :], w, AX.X, ALU.add))
                link(v.reciprocal(st[:, q, 3, :], st[:, q, 2, :]))
                v.tensor_tensor(w, w, st[:, q, 3, :].unsqueeze(2).to_broadcast([P, 4, (n + 1) * P]), ALU.mult
                                ).then_inc(s("pr_p"), 1)

            for n in range(2):
                less_maximum(n, 0)
                less_maximum(n, 1)
                divide(n, 0)
                divide(n, 1)

        @block.scalar
        def _(act):
            def exp(n, g):
                act.wait_ge(s("pr_arg"), 2 * n + g + 1)
                w = p[n][:, heads(g), :]
                nc.scalar.activation(w, w, ACT.Exp, scale=ATT_SCALE).then_inc(s("pr_exp"), 1)

            def copy_turned(u):
                n, g, j = TURNS[u]
                act.wait_ge(s("pr_pT"), u + 1)
                nc.scalar.copy(pT[:, j, heads(g)].rearrange("p h q -> p (h q)"), K.ps[:, 4 + u % 2, :]
                               ).then_inc(s("pr_pT_copied"), 1)

            def copy_output(n, g):
                act.wait_ge(s("pr_o"), 2 * n + g + 1)
                nc.scalar.copy(A.qa[:, :, heads(g), n * P:(n + 1) * P], K.ps[:, 6:8, :].rearrange("p c (h q) -> p c h q", h=4)
                               ).then_inc(s("pr_o_copied"), 1)

            exp(0, 0)
            exp(0, 1)
            copy_turned(0)
            copy_turned(1)
            exp(1, 0)
            copy_output(0, 0)
            exp(1, 1)
            copy_output(0, 1)
            copy_turned(2)
            copy_turned(3)
            copy_output(1, 0)
            copy_turned(4)
            copy_turned(5)
            copy_output(1, 1)


def page_numbers(K, eng, n, g):
    return [(r, j, eng.value_load(K.table[0:1, (2 * n + r) * NPAGE + j:(2 * n + r) * NPAGE + j + 1],
                                  min_val=0, max_val=K.n_pool - 1))
            for j in range(g * NPAGE // 2, (g + 1) * NPAGE // 2) for r in range(2)]


def load_keys(K, eng, l, g, pages, dst):
    for r, j, page in pages:
        eng.dma_start(dst[:, r, j, :], K.d["pages_k"][l, bass.ds(page, 1)].rearrange("o p c -> p (o c)")
                      ).then_inc(K.sem(f"keys_loaded{g}"), 16)


def load_values(K, eng, l, g, pages, dst):
    for r, j, page in pages:
        eng.dma_start(dst[:, r, j, :], K.d["pages_v"][l, bass.ds(page, 1)].rearrange("o p c -> p (o c)")
                      ).then_inc(K.sem(f"values_loaded{g}"), 16)


def mla_sample_stage(K, l, A):
    nc, s = K.nc, K.sem
    NK, PAIRS, HALF = PAST + NSAMP, NB // 2, NPAGE // 2
    PER_HALF = 16 * 2 * HALF
    with ExitStack() as e:
        sb = lambda n, sh: e.enter_context(nc.sbuf_tensor("t_" + n, sh, F32))
        p, o, st = sb("sa_p", [P, NK]), sb("sa_o", [P, 256]), sb("sa_stat", [P, 4])
        spare = K.h[:, :, :].rearrange("p k t -> p (k t)")
        cut = (NPAGE + 1) * P
        pT = spare[:, 0:cut].rearrange("p (j q) -> p j q", j=NPAGE + 1)
        qa_b = spare[:, cut:cut + 2 * NB * NSAMP].rearrange("p (c b q) -> p c b q", c=2, b=NB)
        qr_b = K.proj[0:ROPE, XBC0:XBC0 + 2, 0:NB * NSAMP // 2].rearrange("p c (b q) -> p c b q", b=NB // 2)
        block = e.enter_context(nc.Block(no_gpsimd_drain=True))
        rows = lambda r: slice(r * NSAMP, (r + 1) * NSAMP)

        @block.sync
        def _(sp):
            sp.dma_start(A.w_uv, K.d["w_uv"][l]).then_inc(s("uv_loaded"), 16)
            for n in range(1, PAIRS):
                for g in range(2):
                    pages = page_numbers(K, sp, n, g)
                    sp.wait_ge(s("keys_used"), 2 * n - 1 + g)
                    load_keys(K, sp, l, g, pages, A.keys)

        def turn_o(pe, n):
            pe.wait_ge(s("sa_o_scaled"), n + 1)
            if n:
                pe.wait_ge(s("sa_o_copied"), n)
            for c in range(2):
                mm = pe.transpose(K.ps[:, 7, c * P:(c + 1) * P], o[:, c * P:(c + 1) * P], K.ident[:, :])
            mm.then_inc(s("sa_o_turned"), 1)

        @block.tensor
        def _(pe):
            def query(b, c):
                return qa_b[:, c, b] if c < 2 else qr_b[:, b // 4, b % 4]

            pe.wait_ge(s("sa_q"), 1)
            for n in range(PAIRS):
                if n:
                    pe.wait_ge(s("sa_exp"), n)
                for g in range(2):
                    pe.wait_ge(s(f"keys_loaded{g}"), PER_HALF * (n + 1))
                    for c in range(3):
                        for r in range(2):
                            keys = A.keys[0:P if c < 2 else ROPE, r, HALF * g:HALF * (g + 1), c * P:(c + 1) * P]
                            mm = pe.matmul(K.ps[rows(r), g, :], query(2 * n + r, c), keys, start=(c == 0), stop=(c == 2))
                    mm.then_inc(s("keys_used"), 1)
                for c in range(3):
                    own = K.proj[:, KVD0 + c, SEQ:T] if c < 2 else K.krope[:, SEQ:T]
                    for r in range(2):
                        mm = pe.matmul(K.ps[rows(r), 2, 0:NSAMP], query(2 * n + r, c), own, start=(c == 0), stop=(c == 2))
                mm.then_inc(s("sa_scores"), 1)
                if n:
                    turn_o(pe, n - 1)
                pe.wait_ge(s("sa_exp"), n + 1)
                pe.transpose(K.ps[0:NSAMP, 3, 0:P], p[:, PAST:NK], K.ident[:, :])
                for g in range(2):
                    for j in range(HALF):
                        mm = pe.transpose(K.ps[:, 4 + g, j * P:(j + 1) * P], p[:, (HALF * g + j) * P:(HALF * g + j + 1) * P],
                                          K.ident[:, :])
                    mm.then_inc(s("sa_pT"), 1)
                for g in range(2):
                    pe.wait_ge(s(f"sa_pT_copied{g}"), n + 1)
                    pe.wait_ge(s(f"values_loaded{g}"), PER_HALF * (n + 1))
                    if g == 0:
                        for r in range(2):
                            pe.matmul(K.ps[rows(r), 6, 0:256], pT[0:NSAMP, NPAGE, rows(r)], A.ckv[0:NSAMP, 2, :],
                                      start=True, stop=False)
                    for j in range(HALF * g, HALF * (g + 1)):
                        for r in range(2):
                            mm = pe.matmul(K.ps[rows(r), 6, 0:256], pT[:, j, rows(r)], A.values[:, r, j, :],
                                           start=False, stop=(j == NPAGE - 1))
                    mm.then_inc(s("values_used"), 1)
            turn_o(pe, PAIRS - 1)

        @block.vector
        def _(dve):
            v, link = nc.vector, lambda ins: K.vc.link(dve, ins)

            def store_o(n):
                dve.wait_ge(s("sa_o_turned"), n + 1)
                for r in range(2):
                    t0 = SEQ + (2 * n + r) * TS
                    ins = v.tensor_copy(A.qa[:, :, :, t0:t0 + TS], K.ps[:, 7, 0:2 * P].rearrange(
                        "p (c r h t) -> p c r h t", c=2, r=2, h=MH)[:, :, r])
                ins.then_inc(s("sa_o_copied"), 1)

            for b in range(NB):
                for c in range(2):
                    v.tensor_copy(qa_b[:, c, b].rearrange("p (h t) -> p h t", t=TS), A.qa[:, c, :, SEQ + b * TS:SEQ + (b + 1) * TS])
                ins = v.tensor_copy(qr_b[:, b // 4, b % 4].rearrange("p (h t) -> p h t", t=TS), A.qr[:, :, SEQ + b * TS:SEQ + (b + 1) * TS])
            link(ins)
            dve.sem_inc(s("sa_q"), 1)
            for n in range(PAIRS):
                S = K.ps[:, 0:3, :].rearrange("p b c -> p (b c)")[:, 0:NK]
                dve.wait_ge(s("sa_scores"), n + 1)
                link(v.tensor_tensor(K.ps[:, 2, 0:NSAMP], K.ps[:, 2, 0:NSAMP], K.own[:, n, :], ALU.add))
                link(v.tensor_reduce(st[:, 0:1], S, AX.X, ALU.max))
                v.tensor_scalar(st[:, 1:2], st[:, 0:1], -ATT_SCALE, None, ALU.mult).then_inc(s("sa_max"), 1)
                if n:
                    store_o(n - 1)
                dve.wait_ge(s("sa_exp"), n + 1)
                link(v.reciprocal(st[:, 3:4], st[:, 2:3]))
                dve.wait_ge(s("sa_pT"), 2 * n + 1)
                v.tensor_copy(pT[0:NSAMP, NPAGE], K.ps[0:NSAMP, 3, 0:P])
                v.tensor_copy(pT[:, 0:HALF].rearrange("p j q -> p (j q)"), K.ps[:, 4, :]).then_inc(s("sa_pT_copied0"), 1)
                dve.wait_ge(s("sa_pT"), 2 * n + 2)
                v.tensor_copy(pT[:, HALF:NPAGE].rearrange("p j q -> p (j q)"), K.ps[:, 5, :]).then_inc(s("sa_pT_copied1"), 1)
                dve.wait_ge(s("values_used"), 2 * n + 2)
                v.tensor_scalar(o[:, :], K.ps[:, 6, 0:256], st[:, 3:4], None, ALU.mult).then_inc(s("sa_o_scaled"), 1)
            store_o(PAIRS - 1)

        @block.scalar
        def _(act):
            for n in range(PAIRS):
                if n:
                    act.wait_ge(s("values_used"), 2 * n - 1)
                    load_values(K, act, l, 0, pages0, A.values)
                act.wait_ge(s("sa_max"), n + 1)
                nc.scalar.activation(p[:, :], K.ps[:, 0:3, :].rearrange("p b c -> p (b c)")[:, 0:NK], ACT.Exp,
                                     bias=st[:, 1:2], scale=ATT_SCALE, accum_out=st[:, 2:3]).then_inc(s("sa_exp"), 1)
                if n:
                    act.wait_ge(s("values_used"), 2 * n)
                    load_values(K, act, l, 1, pages1, A.values)
                if n + 1 < PAIRS:
                    pages0, pages1 = (page_numbers(K, act, n + 1, g) for g in range(2))


def mla_value_stage(K, l, A, wb):
    nc, s, wuv = K.nc, K.sem, A.w_uv
    with nc.Block(no_gpsimd_drain=True) as block:
        @block.sync
        def _(sp):
            for n in range(MERGE_SLOTS):
                load_merge_panel(K, sp, l, n, wb)

        @block.tensor
        def _(pe):
            pe.wait_ge(s("uv_loaded"), 16)
            for h in range(MH):
                for k in range(2):
                    mm = pe.matmul(K.ps[64 * (h % 2):64 * (h % 2) + 64, h // 2, 0:T], wuv[:, k, h, :], A.qa[:, k, h, :],
                                   start=(k == 0), stop=(k == 1))
            mm.then_inc(s("yc_done"), 1)

        @block.vector
        def _(dve):
            dve.wait_ge(s("yc_done"), 1)
            nc.vector.tensor_copy(K.proj[:, HF0:HF0 + 4, :], K.ps[:, 0:4, 0:T])


MERGE_SLOTS = 4


def load_merge_panel(K, sp, l, n, wb):
    src = K.d["w_branch"][l, n] if n < 8 else K.d["w_out"][l, n - 8]
    sp.dma_start(wb[:, n % MERGE_SLOTS].rearrange("p a b -> p (a b)"), src).then_inc(K.sem(f"mg_loaded{n % MERGE_SLOTS}"), 16)


def merge_stage(K, l, wb):
    nc, s = K.nc, K.sem
    SL = MERGE_SLOTS
    SRC = (Z0, HQ0, HF0, LY0)
    with nc.sbuf_tensor("mg_tmp", [P, 2, T], F32) as tmp, nc.Block(no_gpsimd_drain=True) as block:
        @block.sync
        def _(sp):
            for n in range(SL, 12):
                sp.wait_ge(s("mg_tile"), 4 * (n - SL + 1))
                load_merge_panel(K, sp, l, n, wb)

        @block.tensor
        def _(pe):
            for n in range(12):
                pe.wait_ge(s(f"mg_loaded{n % SL}"), 16 * (n // SL + 1))
                if n == 8:
                    pe.wait_ge(s("mg_merged"), 1)
                for m in range(4 if n < 8 else 2):
                    t = 4 * n + m if n < 8 else 32 + 2 * (n - 8) + m
                    if t >= 8:
                        pe.wait_ge(s("mg_read"), t - 7)
                    if n < 8:
                        for k in range(4):
                            mm = pe.matmul(K.ps[:, t % 8, 0:T], wb[:, n % SL, k, m * P:(m + 1) * P],
                                           K.proj[:, SRC[n // 2] + k, :], start=(k == 0), stop=(k == 3))
                    else:
                        w = wb[:, n % SL].rearrange("p a b -> p (a b)").rearrange("p (k c) -> p k c", k=KD)
                        for k in range(KD):
                            mm = pe.matmul(K.ps[:, t % 8, 0:T], w[:, k, m * P:(m + 1) * P], K.h[:, k, :],
                                           start=(k == 0), stop=(k == KD - 1))
                    mm.then_inc(s("mg_tile"), 1)

        @block.vector
        def _(dve):
            v, link = nc.vector, lambda ins: K.vc.link(dve, ins)
            for t in range(32):
                n, m = t // 8, t % 8
                dve.wait_ge(s("mg_tile"), t + 1)
                if n == 0:
                    v.tensor_tensor(K.h[:, m, :], K.ps[:, t % 8, 0:T], K.proj[:, GL0 + t, :], ALU.mult).then_inc(s("mg_read"), 1)
                else:
                    v.tensor_tensor(tmp[:, t % 2], K.ps[:, t % 8, 0:T], K.proj[:, GL0 + t, :], ALU.mult).then_inc(s("mg_read"), 1)
                    dve.wait_ge(s("mg_read"), t + 1)
                    link(v.tensor_tensor(K.h[:, m, :], K.h[:, m, :], tmp[:, t % 2], ALU.add))
            dve.sem_inc(s("mg_merged"), 1)
            for m in range(KD):
                t = 32 + m
                dve.wait_ge(s("mg_tile"), t + 1)
                residual(K, dve, K.ps[:, t % 8, 0:T], tmp[:, t % 2], 16 + m, m, s("mg_read"), t + 1)


def residual(K, dve, src, tmp, g, m, read, count):
    v = K.nc.vector
    v.scalar_tensor_tensor(out=K.x[:, m, 0:SEQ], in0=src[:, 0:SEQ], scalar=K.mod[:, g, 0:1], in1=K.x[:, m, 0:SEQ],
                           op0=ALU.mult, op1=ALU.add)
    v.tensor_tensor(tmp[:, SEQ:T].rearrange("p (b t) -> p b t", t=TS), src[:, SEQ:T].rearrange("p (b t) -> p b t", t=TS),
                    K.mod[:, g, 1:NREQ].unsqueeze(2).to_broadcast([P, NB, TS]), ALU.mult).then_inc(read, 1)
    dve.wait_ge(read, count)
    v.tensor_tensor(K.x[:, m, SEQ:T], K.x[:, m, SEQ:T], tmp[:, SEQ:T], ALU.add)


def router_stage(K, l, R):
    nc, s = K.nc, K.sem
    with ExitStack() as e:
        sb = lambda n, sh: e.enter_context(nc.sbuf_tensor("t_" + n, sh, F32))
        w, bias = R.w_router, R.b_router
        L, g = sb("rt_L", [P, 3, 36]), sb("rt_g", [P, 4, 3, 4])
        ee, st, gate = sb("rt_e", [P, 5, 3, 8]), sb("rt_st", [P, 10, 3]), sb("rt_gate", [P, 3, 4, 8])
        sel, tmp32 = sb("rt_sel", [P, 3, 3, NEXP]), sb("rt_tmp32", [P, 3, NEXP])
        total = sb("rt_total", [1, 2 + MAX_PASS])
        block = e.enter_context(nc.Block(no_gpsimd_drain=True))
        REG = ((0, P), (P, P), (SEQ, NSAMP))

        @block.tensor
        def _(pe):
            pe.wait_ge(s("rt_w_loaded"), 16)
            pe.wait_ge(s("rt_b_loaded"), 16)
            for r, (t0, n) in enumerate(REG):
                for k in range(KD):
                    pe.matmul(K.ps[0:n, 0, r * 36:(r + 1) * 36], K.h[:, k, t0:t0 + n], w[:, k, :], start=(k == 0), stop=False)
                mm = pe.matmul(K.ps[0:n, 0, r * 36:(r + 1) * 36], K.ones[0:1, 0:n], bias[:, :], start=False, stop=True)
            mm.then_inc(s("rt_logits"), 1)
            for r, (t0, n) in enumerate(REG):
                if r == 2:
                    pe.wait_ge(s("h_tm_copied"), 1)
                for k in range(KD):
                    mm = pe.transpose(K.ps[0:n, 4 + 2 * (r % 2) + k // 4, (k % 4) * P:(k % 4 + 1) * P],
                                      K.h[:, k, t0:t0 + n], K.ident[:, :])
                mm.then_inc(s("h_tm"), 1)
            pe.wait_ge(s("rt_sel"), 1)
            for r, (t0, n) in enumerate(REG):
                for q in range(r):
                    pe.matmul(K.ps[0:n, 2, r * NEXP:(r + 1) * NEXP], K.ones[:, 0:n], sel[:, 2, q, :], start=(q == 0), stop=False)
                pe.matmul(K.ps[0:n, 2, r * NEXP:(r + 1) * NEXP], K.causal[0:n, 0:n], sel[0:n, 2, r, :], start=(r == 0), stop=True)
            for r, (t0, n) in enumerate(REG):
                mm = pe.matmul(K.ps[0:32, 3, 0:NEXP], K.ones[0:n, 0:32], sel[0:n, 2, r, :], start=(r == 0), stop=(r == 2))
            mm.then_inc(s("rt_counts"), 1)

        @block.vector
        def _(dve):
            v, link = nc.vector, lambda ins: K.vc.link(dve, ins)

            def first_max(x, mx, onehot, tmp, n):
                bc = lambda a: a.unsqueeze(2).to_broadcast([P, 3, n])
                io = K.iota[:, 0:n].unsqueeze(1).to_broadcast([P, 3, n])
                link(v.tensor_reduce(mx, x, AX.X, ALU.max))
                link(v.tensor_tensor(tmp, x, bc(mx), ALU.is_equal))
                link(v.tensor_scalar(tmp, tmp, -100.0, 100.0, ALU.mult, ALU.add))
                link(v.tensor_tensor(tmp, tmp, io, ALU.add))
                link(v.tensor_reduce(st[:, 9], tmp, AX.X, ALU.min))
                link(v.tensor_tensor(onehot, io, bc(st[:, 9]), ALU.is_equal))

            link(v.memset(L[:, 2, :], 0.0))
            dve.wait_ge(s("rt_logits"), 1)
            v.tensor_copy(L[:, 0:2].rearrange("p r c -> p (r c)"), K.ps[:, 0, 0:72])
            link(v.tensor_copy(L[0:NSAMP, 2], K.ps[0:NSAMP, 0, 72:108]))
            G, E = L[:, :, 0:4], L[:, :, 4:36].rearrange("p r (g e) -> p r g e", g=4)
            first_max(G, st[:, 0], g[:, 0], g[:, 1], 4)
            v.tensor_tensor(g[:, 2], G, st[:, 0].unsqueeze(2).to_broadcast([P, 3, 4]), ALU.subtract).then_inc(s("rt_garg"), 1)
            link(v.tensor_tensor(gate[:, :, :, :], E, g[:, 0].unsqueeze(3).to_broadcast([P, 3, 4, 8]), ALU.mult))
            link(v.tensor_tensor(ee[:, 0], gate[:, :, 0, :], gate[:, :, 1, :], ALU.add))
            link(v.tensor_tensor(ee[:, 1], gate[:, :, 2, :], gate[:, :, 3, :], ALU.add))
            link(v.tensor_tensor(ee[:, 0], ee[:, 0], ee[:, 1], ALU.add))
            first_max(ee[:, 0], st[:, 1], ee[:, 1], ee[:, 2], 8)
            link(v.scalar_tensor_tensor(out=ee[:, 2], in0=ee[:, 1], scalar=-BIG, in1=ee[:, 0], op0=ALU.mult, op1=ALU.add))
            first_max(ee[:, 2], st[:, 2], ee[:, 3], ee[:, 4], 8)
            v.tensor_tensor(st[:, 3], st[:, 2], st[:, 1], ALU.subtract).then_inc(s("rt_darg"), 1)
            for n in range(2):
                link(v.tensor_tensor(sel[:, n].rearrange("p r (g e) -> p r g e", g=4),
                                     ee[:, 1 + 2 * n].unsqueeze(2).to_broadcast([P, 3, 4, 8]),
                                     g[:, 0].unsqueeze(3).to_broadcast([P, 3, 4, 8]), ALU.mult))
            v.tensor_tensor(sel[:, 2], sel[:, 0], sel[:, 1], ALU.add).then_inc(s("rt_sel"), 1)
            dve.wait_ge(s("rt_exp"), 1)
            link(v.tensor_reduce(st[:, 5], g[:, 3], AX.X, ALU.add))
            link(v.tensor_scalar(st[:, 6], st[:, 4], 1.0, None, ALU.add))
            link(v.tensor_tensor(st[:, 6], st[:, 6], st[:, 5], ALU.mult))
            link(v.reciprocal(st[:, 7], st[:, 6]))
            link(v.tensor_tensor(st[:, 8], st[:, 7], st[:, 4], ALU.mult))
            v.tensor_copy(R.w[:, 0], st[:, 7])
            v.tensor_copy(R.w[:, 1], st[:, 8])
            dve.wait_ge(s("rt_counts"), 1)
            link(v.memset(R.pos[:, :, :], -1.0))
            v.tensor_tensor(tmp32[:, 0:2, :], sel[:, 2, 0:2], K.ps[:, 2, 0:2 * NEXP].rearrange("p (r e) -> p r e", r=2), ALU.mult)
            link(v.tensor_tensor(tmp32[0:NSAMP, 2, :], sel[0:NSAMP, 2, 2], K.ps[0:NSAMP, 2, 2 * NEXP:3 * NEXP], ALU.mult))
            v.tensor_scalar(R.pos[:, 0:2, 0:NEXP], tmp32[:, 0:2], -1.0, None, ALU.add)
            link(v.tensor_scalar(R.pos[0:NSAMP, 2, 0:NEXP], tmp32[0:NSAMP, 2], -1.0, None, ALU.add))
            for n in range(2):
                for q, of_expert in enumerate((R.pos[:, :, 0:NEXP], K.first_slot[:, :].unsqueeze(1).to_broadcast([P, 3, NEXP]))):
                    link(v.tensor_tensor(tmp32[:, :, :], of_expert, sel[:, n], ALU.mult))
                    link(v.tensor_reduce(R.place[:, q, n], tmp32[:, :, :], AX.X, ALU.add))
            link(v.tensor_reduce(total[:, 0:1], K.ps[0:1, 3, 0:NEXP], AX.X, ALU.max))
            link(v.tensor_scalar(total[:, 2:2 + MAX_PASS], K.first_slot[0:1, 0:MAX_PASS], total[:, 0:1], None, ALU.is_lt))
            link(v.tensor_reduce(total[:, 1:2], total[:, 2:2 + MAX_PASS], AX.X, ALU.add))
            v.tensor_copy(R.passes[:, :], total[:, 1:2])
        @block.scalar
        def _(act):
            for r, (t0, n) in enumerate(REG):
                act.wait_ge(s("h_tm"), r + 1)
                nc.scalar.copy(R.hT[0:n, r, :], K.ps[0:n, 4 + 2 * (r % 2):6 + 2 * (r % 2), :].rearrange("p b c -> p (b c)")
                               ).then_inc(s("h_tm_copied"), 1)
            act.wait_ge(s("rt_garg"), 1)
            nc.scalar.activation(g[:, 3], g[:, 2], ACT.Exp)
            act.wait_ge(s("rt_darg"), 1)
            nc.scalar.activation(st[:, 4], st[:, 3], ACT.Exp).then_inc(s("rt_exp"), 1)


def load_expert(K, sp, l, e, j):
    s = K.sem
    sp.dma_start(K.gate_up[:, j], K.d["w_gate_up"][l, e].rearrange("o p k n -> p (o k) n")).then_inc(s(f"gu_loaded{j}"), 16)


def load_down(K, sp, l, e, j, wd):
    sp.dma_start(wd[:, j], K.d["w_down"][l, e].rearrange("o p k n -> p (o k) n")).then_inc(K.sem(f"down_loaded{j}"), 16)


def experts_stage(K, l, R, turn):
    nc, s = K.nc, K.sem
    TILES = ((0, P), (1, P), (2, NSAMP))
    PAIRS = NEXP // 2
    NI = PAIRS // 2
    LOOPS = ((0, 1), (1, NI - 1), (NI - 1, NI))
    G0, X0, GU, HT, DN = 0, 2, 4, 5, 6
    with ExitStack() as e_:
        sb = lambda n, sh: e_.enter_context(nc.sbuf_tensor("t_" + n, sh, F32))
        wd = R.w_down
        pick, xt, xf = sb("ex_pick", [P, 2, 3, 2, CAP]), sb("ex_xt", [P, D]), sb("ex_xf", [P, 2, KD, P])
        hid, hf, y = sb("ex_hid", [P, 2, HID]), sb("ex_hf", [P, 2, 2, P]), sb("ex_y", [P, 2, D])
        block = e_.enter_context(nc.Block(no_gpsimd_drain=True))

        def pairs(eng):
            for i0, i1 in LOOPS:
                with eng.Fori(i0, i1) as i:
                    for b in range(2):
                        yield i, b, i * 2 + b, i0 == 0, i1 == NI

        @block.sync
        def _(sp):
            with sp.If(turn > 0):
                for j in range(SLOTS):
                    load_expert(K, sp, l, slice(j, j + 1), j)
                    load_down(K, sp, l, slice(j, j + 1), j, wd)
            with sp.Fori(1, NI) as i:
                for b in range(2):
                    sp.wait_ge(s("gu_done"), (i - 1) * 2 + b + 1)
                    for j in (2 * b, 2 * b + 1):
                        load_expert(K, sp, l, bass.ds(i * SLOTS + j, 1), j)
                    sp.wait_ge(s("down_done"), (i - 1) * 2 + b + 1)
                    for j in (2 * b, 2 * b + 1):
                        load_down(K, sp, l, bass.ds(i * SLOTS + j, 1), j, wd)

        @block.tensor
        def _(pe):
            def gather(q, b, first):
                pe.wait_ge(s("pick_ready"), q + 1)
                if not first:
                    pe.wait_ge(s("xt_ready"), q)
                for half in range(2):
                    for r, n in TILES:
                        mm = pe.matmul(K.ps[:, G0 + half, :], pick[0:n, b, r].rearrange("p e c -> p (e c)"),
                                       R.hT[0:n, r, half * 512:(half + 1) * 512], start=(r == 0), stop=(r == 2))
                mm.then_inc(s("gathered"), 1)

            def turn_x(q, first):
                pe.wait_ge(s("xt_ready"), q + 1)
                if not first:
                    pe.wait_ge(s("xf_ready"), q)
                for k in range(KD):
                    mm = pe.transpose(K.ps[:, X0 + k // 4, (k % 4) * P:(k % 4 + 1) * P], xt[:, k * P:(k + 1) * P], K.ident[:, :])
                mm.then_inc(s("x_turned"), 1)

            gather(0, 0, True)
            turn_x(0, True)
            gather(1, 1, False)
            for i, b, p, head, tail in pairs(pe):
                first = head and b == 0
                pe.wait_ge(s("xf_ready"), p + 1)
                for j in (2 * b, 2 * b + 1):
                    pe.wait_ge(s(f"gu_loaded{j}"), i * 16 + 16)
                if not first:
                    pe.wait_ge(s("hid_ready"), p)
                for k in range(KD):
                    for q in range(2):
                        rows = slice(q * CAP, (q + 1) * CAP)
                        mm = pe.matmul(K.ps[rows, GU, :], xf[:, b, k, rows], K.gate_up[:, 2 * b + q, k, :],
                                       start=(k == 0), stop=(k == KD - 1))
                mm.then_inc(s("gu_done"), 1)
                if not (tail and b == 1):
                    turn_x(p + 1, False)
                pe.wait_ge(s("hid_ready"), p + 1)
                if not first:
                    pe.wait_ge(s("hf_ready"), p)
                for f in range(2):
                    mm = pe.transpose(K.ps[:, HT, f * P:(f + 1) * P], hid[:, b, f * P:(f + 1) * P], K.ident[:, :])
                mm.then_inc(s("hid_turned"), 1)
                if not tail:
                    gather(p + 2, b, False)
                pe.wait_ge(s("hf_ready"), p + 1)
                for j in (2 * b, 2 * b + 1):
                    pe.wait_ge(s(f"down_loaded{j}"), i * 16 + 16)
                if not first:
                    pe.wait_ge(s("y_low"), p)
                    pe.wait_ge(s("y_high"), p)
                for half in range(2):
                    for f in range(2):
                        for q in range(2):
                            rows = slice(q * CAP, (q + 1) * CAP)
                            mm = pe.matmul(K.ps[rows, DN + half, :], hf[:, b, f, rows],
                                           wd[:, 2 * b + q, f, half * 512:(half + 1) * 512], start=(f == 0), stop=(f == 1))
                mm.then_inc(s("down_done"), 1)

        @block.vector
        def _(dve):
            v = nc.vector

            def choose(experts, b):
                v.tensor_tensor(pick[:, b], R.pos[:, :, experts].unsqueeze(3).to_broadcast([P, 3, 2, CAP]),
                                K.slot[:, :].unsqueeze(1).unsqueeze(1).to_broadcast([P, 3, 2, CAP]), ALU.is_equal
                                ).then_inc(s("pick_ready"), 1)

            def copy_x(q, b):
                dve.wait_ge(s("x_turned"), q + 1)
                v.tensor_copy(xf[:, b].rearrange("p k c -> p (k c)"), K.ps[:, X0:X0 + 2, :].rearrange("p a c -> p (a c)")
                              ).then_inc(s("xf_ready"), 1)

            choose(slice(0, 2), 0)
            choose(slice(2, 4), 1)
            copy_x(0, 0)
            for i, b, p, head, tail in pairs(dve):
                if not tail:
                    dve.wait_ge(s("gathered"), p + 1)
                    choose(bass.ds((i + 1) * SLOTS + 2 * b, 2), b)
                dve.wait_ge(s("gate_ready"), p + 1)
                v.tensor_tensor(hid[:, b], hid[:, b], K.ps[:, GU, HID:2 * HID], ALU.mult).then_inc(s("hid_ready"), 1)
                if not (tail and b == 1):
                    copy_x(p + 1, 1 - b)
                dve.wait_ge(s("hid_turned"), p + 1)
                v.tensor_copy(hf[:, b].rearrange("p f c -> p (f c)"), K.ps[:, HT, 0:2 * P]).then_inc(s("hf_ready"), 1)
                dve.wait_ge(s("down_done"), p + 1)
                if not head:
                    dve.wait_ge(s(f"y_stored{b}"), i * 16)
                v.tensor_copy(y[:, b, 0:512], K.ps[:, DN, :]).then_inc(s("y_low"), 1)

        @block.scalar
        def _(act):
            a = nc.scalar

            def copy_gathered(q):
                act.wait_ge(s("gathered"), q + 1)
                a.copy(xt[:, :], K.ps[:, G0:G0 + 2, :].rearrange("p a c -> p (a c)")).then_inc(s("xt_ready"), 1)

            copy_gathered(0)
            act.wait_ge(s("x_turned"), 1)
            copy_gathered(1)
            for i, b, p, head, tail in pairs(act):
                act.wait_ge(s("gu_done"), p + 1)
                if not head:
                    act.wait_ge(s("hid_turned"), p - 1)
                a.activation(hid[:, b], K.ps[:, GU, 0:HID], ACT.Silu).then_inc(s("gate_ready"), 1)
                if not tail:
                    act.wait_ge(s("x_turned"), p + 2)
                    copy_gathered(p + 2)
                act.wait_ge(s("down_done"), p + 1)
                if not head:
                    act.wait_ge(s(f"y_stored{b}"), i * 16)
                a.copy(y[:, b, 512:D], K.ps[:, DN + 1, :]).then_inc(s("y_high"), 1)
                act.wait_ge(s("y_low"), p + 1)
                act.wait_ge(s("y_high"), p + 1)
                act.dma_start(K.d["rows"][bass.ds(p * P, P), :], y[:, b, :]).then_inc(s(f"y_stored{b}"), 16)
            for b in range(2):
                act.wait_ge(s(f"y_stored{b}"), NI * 16)


def combine_stage(K, l, R):
    nc, s = K.nc, K.sem
    flat = K.proj[:, :, :].rearrange("p n t -> p (n t)")
    yr = flat[:, 0:6 * D].rearrange("p (n r c) -> p n r c", n=2, r=3)
    with (nc.sbuf_tensor("u_cb_tmp", [P, KD, NSAMP], F32) as tmp, nc.sbuf_tensor("cb_w", [P, 5, 6], F32) as w,
          nc.sbuf_tensor("cb_row", [P, 2, 3], U32) as row, nc.Block(no_gpsimd_drain=True) as block):
        place, first = (R.place[:, q].rearrange("p n r -> p (n r)") for q in range(2))

        @block.gpsimd
        def _(pool):
            pool.wait_ge(s("rows_known"), 1)
            for r, n in ((0, P), (1, P), (2, NSAMP)):
                for q in range(2):
                    pool.indirect_dma_start(out=yr[0:n, q, r, :], out_offset=None, in_=K.d["rows"],
                                            in_offset=bass.IndirectOffsetOnAxis(ap=row[0:n, q, r:r + 1], axis=0)
                                            ).then_inc(K.rows_loaded[r], 16)

        @block.vector
        def _(dve):
            v, link = nc.vector, lambda ins: K.vc.link(dve, ins)
            v.tensor_scalar(w[:, 0], place, 0.0, None, ALU.is_ge)
            v.tensor_scalar(w[:, 1], place, CAP - 0.5, None, ALU.is_lt)
            link(v.tensor_scalar(w[:, 2], place, 0.0, CAP - 1.0, ALU.max, ALU.min))
            link(v.tensor_tensor(w[:, 2], w[:, 2], first, ALU.add))
            v.tensor_copy(row[:, :, :].rearrange("p n r -> p (n r)"), w[:, 2]).then_inc(s("rows_known"), 1)
            link(v.tensor_tensor(w[:, 3], w[:, 0], w[:, 1], ALU.mult))
            link(v.tensor_tensor(w[:, 4], w[:, 3], R.w[:, :, :].rearrange("p n r -> p (n r)"), ALU.mult))
            v.tensor_scalar(place, place, -float(CAP), None, ALU.add)
            v.tensor_scalar(R.pos[:, :, :], R.pos[:, :, :], -float(CAP), None, ALU.add)
            for r, n in ((0, P), (1, P), (2, NSAMP)):
                dve.wait_ge(K.rows_loaded[r], 32)
                link(v.tensor_scalar(yr[0:n, 0, r], yr[0:n, 0, r], w[0:n, 4, r:r + 1], None, ALU.mult))
                v.scalar_tensor_tensor(out=yr[0:n, 0, r], in0=yr[0:n, 1, r], scalar=w[0:n, 4, 3 + r:4 + r], in1=yr[0:n, 0, r],
                                       op0=ALU.mult, op1=ALU.add).then_inc(s("rows_summed"), 1)
            for m in range(KD):
                dve.wait_ge(s("moe_fm"), m + 1)
                v.scalar_tensor_tensor(out=K.x[:, m, 0:SEQ], in0=K.ps[:, m, 0:SEQ], scalar=K.mod[:, 40 + m, 0:1],
                                       in1=K.x[:, m, 0:SEQ], op0=ALU.mult, op1=ALU.add)
            link(v.tensor_tensor(tmp[:, :, :].rearrange("p k (b t) -> p k b t", t=TS),
                                 K.ps[:, :, SEQ:T].rearrange("p k (b t) -> p k b t", t=TS),
                                 K.mod[:, 40:48, 1:NREQ].unsqueeze(3).to_broadcast([P, KD, NB, TS]), ALU.mult))
            v.tensor_tensor(K.x[:, :, SEQ:T], K.x[:, :, SEQ:T], tmp[:, :, :], ALU.add)

        @block.tensor
        def _(pe):
            for r, (t0, n) in enumerate(((0, P), (P, P), (SEQ, NSAMP))):
                pe.wait_ge(s("rows_summed"), r + 1)
                for k in range(KD):
                    mm = pe.transpose(K.ps[:, k, t0:t0 + n], yr[0:n, 0, r, k * P:(k + 1) * P], K.ident[0:n, 0:n])
                    if r == 2:
                        mm.then_inc(s("moe_fm"), 1)




def build(nc, d, n_pool):
    K = Core()
    K.nc, K.d, K.n_pool = nc, d, n_pool
    with ExitStack() as ctx:
        def sb(name, shape, dt=F32):
            return ctx.enter_context(nc.sbuf_tensor("s_" + name, shape, dt))

        once = {n: ctx.enter_context(nc.semaphore(n)) for n in ("consts_loaded", "silu_c_ready")}
        K.rows_loaded = [ctx.enter_context(nc.semaphore(f"rows_loaded{r}")) for r in range(3)]
        phase_sems, phase = {}, [ExitStack()]

        def sem(name):
            if name not in phase_sems:
                phase_sems[name] = phase[0].enter_context(nc.semaphore(name))
            return phase_sems[name]

        def end_phase():
            with nc.Block(no_gpsimd_drain=True) as block:
                @block.sync
                def _(sp):
                    for semaphore in (*phase_sems.values(), *K.rows_loaded):
                        sp.sem_clear(semaphore)
            phase_sems.clear()
            phase[0].close()
            phase[0] = ExitStack()
            K.vc, K.ac = Chain(sem("dve_step")), Chain(sem("act_step"))

        K.sem = sem
        K.ps = ctx.enter_context(nc.psum_tensor("ps", [P, 8, 512], F32))
        K.x, K.h, K.proj = sb("x", [P, KD, T]), sb("h", [P, KD, T]), sb("proj", [P, NPROJ, T])
        K.dt, K.acs, K.wend, K.krope = sb("dt", [NH, T]), sb("acs", [NH, T]), sb("wend", [NH, T]), sb("krope", [ROPE, T])
        K.acol = sb("acol", [NH, 1])
        K.cols, K.mod, K.gain = sb("cols", [P, NCOLS]), sb("mod", [P, 48, NREQ]), sb("gain", [P, 2, 8, NREQ])
        K.silu_c, K.fin, K.table = sb("silu_c", [P, KD, NREQ]), sb("fin", [P, KD]), sb("table", [1, NB * NPAGE], I32)
        consts = {}
        for name, arr in constants().items():
            if name == "mask":
                continue
            consts[name] = sb("k_" + name, list(arr.shape))
        K.ident, K.ones, K.causal, K.keep = (consts[n] for n in ("ident", "ones", "causal", "keep"))
        K.selhead, K.selpair, K.ownb, K.own = (consts[n] for n in ("selhead", "selpair", "ownb", "own"))
        K.cos, K.sin, K.sin_turned, K.turn, K.eye = (consts[n] for n in ("cos", "sin", "sin_turned", "turn", "eye"))
        K.row_select, K.eps, K.later, K.iota, K.slot, K.first_slot = (consts[n] for n in ("row_select", "eps", "later", "iota", "slot", "first_slot"))
        with nc.Block(no_gpsimd_drain=True) as block:
            @block.sync
            def _(sp):
                for dst, name in ((K.x, "x"), (K.silu_c, "c"), (K.fin, "fin"), (K.table, "table")):
                    sp.dma_start(whole(dst), d[name]).then_inc(once["consts_loaded"], 16)
                for name in list(consts)[::2]:
                    sp.dma_start(whole(consts[name]), d["k_" + name]).then_inc(once["consts_loaded"], 16)
                sp.wait_ge(once["consts_loaded"], 16 * (4 + len(consts)))

            @block.scalar
            def _(act):
                for name in list(consts)[1::2]:
                    act.dma_start(whole(consts[name]), d["k_" + name]).then_inc(once["consts_loaded"], 16)
                act.wait_ge(once["consts_loaded"], 16 * (4 + len(consts)))
                nc.scalar.activation(K.silu_c[:, :, :], K.silu_c[:, :, :], ACT.Silu).then_inc(once["silu_c_ready"], 1)
                act.wait_ge(once["silu_c_ready"], 1)
        with nc.Fori(0, DEPTH) as l:
            K.vc, K.ac = Chain(sem("dve_step")), Chain(sem("act_step"))
            with ExitStack() as e:
                G = Core()
                G.b, G.k = (e.enter_context(nc.sbuf_tensor(n, [P, 4, T], F32)) for n in ("hg_b", "hg_k"))
                with (nc.sbuf_tensor("w_in_tiles", [P, IN_SLOTS, KD, P], F32) as win,
                      nc.sbuf_tensor("w_mod_panels", [P, 3, 2048], F32) as wmod):
                    first_norm_stage(K, l, win, wmod)
                    projection_stage(K, l, G, win, wmod)
                ssd_stage(K, l)
                G.A = e.enter_context(nc.sbuf_tensor("hg_A", [P, 4, T], F32))
                G.A01 = e.enter_context(nc.sbuf_tensor("u_hg_A01", [P, 4, P], F32))
                G.eye = K.eye
                hgrn_scores_stage(K, l, G)
                hgrn_output_stage(K, l, G)
            end_phase()
            with ExitStack() as e:
                A = Core()
                A.qa = e.enter_context(nc.sbuf_tensor("u_mla_qa", [P, 2, MH, T], F32))
                A.ckv = e.enter_context(nc.sbuf_tensor("u_mla_ckv", [P, 3, 256], F32))
                A.w_uv = K.proj[:, HF0:HF0 + 4, :].rearrange("p n t -> p (n t)")[:, 0:2 * MH * 64].rearrange(
                    "p (k h v) -> p k h v", k=2, h=MH)
                A.qr = K.proj[0:ROPE, HI0:HI0 + MH, :]
                mla_project_stage(K, l, A)
                with (nc.sbuf_tensor("page_keys", [P, 2, NPAGE, 384], F32) as keys,
                      nc.sbuf_tensor("page_values", [P, 2, NPAGE, 256], F32) as values):
                    A.keys, A.values = keys, values
                    mla_prompt_stage(K, l, A)
                    mla_sample_stage(K, l, A)
                with nc.sbuf_tensor("w_merge", [P, MERGE_SLOTS, 4, 512], F32) as wb:
                    mla_value_stage(K, l, A, wb)
                    merge_stage(K, l, wb)
            K.gate_up = K.proj[:, :, :].rearrange("p n t -> p (n t)")[:, 0:SLOTS * KD * 2 * HID].rearrange(
                "p (j k n) -> p j k n", j=SLOTS, k=KD)
            with ExitStack() as e:
                R = Core()
                R.w_down = e.enter_context(nc.sbuf_tensor("w_down_slots", [P, SLOTS, 2, D], F32))

                R.w_router = e.enter_context(nc.sbuf_tensor("w_router_", [P, KD, 36], F32))
                R.b_router = e.enter_context(nc.sbuf_tensor("b_router_", [1, 36], F32))

                def router_and_first_experts(sp):
                    sp.dma_start(R.w_router[:, :, :], K.d["w_router"][l]).then_inc(sem("rt_w_loaded"), 16)
                    sp.dma_start(R.b_router[:, :], K.d["b_router"][l]).then_inc(sem("rt_b_loaded"), 16)
                    for j in range(SLOTS):
                        load_expert(K, sp, l, slice(j, j + 1), j)
                        load_down(K, sp, l, slice(j, j + 1), j, R.w_down)

                norm_stage(K, 1, "n2", router_and_first_experts)
                R.hT = e.enter_context(nc.sbuf_tensor("h_tm_", [P, 3, D], F32))
                R.pos = e.enter_context(nc.sbuf_tensor("rt_pos", [P, 3, NEXP + 1], F32))
                R.w = e.enter_context(nc.sbuf_tensor("rt_w", [P, 2, 3], F32))
                R.place = e.enter_context(nc.sbuf_tensor("rt_place", [P, 2, 2, 3], F32))
                R.passes = e.enter_context(nc.sbuf_tensor("rt_passes", [1, 1], I32))
                router_stage(K, l, R)
                passes = nc.values_load(R.passes[0:1, 0:1], min_val=1, max_val=MAX_PASS)
                K.vc = Chain(sem("pass_dve_step"))
                with nc.Fori(0, passes) as turn:
                    experts_stage(K, l, R, turn)
                    combine_stage(K, l, R)
                    end_phase()
        norm_stage(K, 2, "nf")
        with nc.Block(no_gpsimd_drain=True) as block:
            @block.sync
            def _(sp):
                sp.dma_start(d["o_y"], K.h[:, :, :]).then_inc(sem("y_stored"), 16)
                sp.wait_ge(sem("y_stored"), 16)


def whole(t):
    return t[tuple(slice(None) for _ in t.shape)]


def constants():
    f = np.float32
    i, j = np.arange(P)[:, None], np.arange(P)[None, :]
    row_select = np.zeros((P, 4 * TS), f)
    for r in range(4 * TS):
        row_select[32 * (r // TS) + r % TS, r] = 1
    own64 = (i[:64] // TS == j[:, :64] // TS)
    causal = np.zeros((P, SEQ + P + NSAMP), f)
    causal[:, 0:P] = j >= i
    causal[:, P:SEQ] = 1
    causal[:, SEQ:SEQ + P] = j >= i
    causal[:64, SEQ + P:] = own64 & (j[:, :64] >= i[:64])
    selhead = np.zeros((NH, NH, P), f)
    selpair = np.zeros((NH, 4, P), f)
    for h in range(NH):
        selhead[h, h, :] = 1
        selpair[h, h // 2, 64 * (h % 2):64 * (h % 2) + 64] = 1
    keep = np.ones((P, T), f)
    keep[:, 0] = 0
    keep[:, SEQ::TS] = 0
    ownb = (np.arange(NSAMP)[:, None] // TS == np.arange(NB)[None, :]).astype(f)
    pos = np.concatenate([np.arange(SEQ), PAST + np.arange(NSAMP) % TS]).astype(f)
    half = ROPE // 2
    inv = (f(10000.0) ** (-np.arange(half, dtype=f) * f(2.0) / f(ROPE))).astype(f)
    ang = (pos[None, :] * inv[:, None]).astype(f)
    cos, sin = (np.concatenate([g(ang), g(ang)]).astype(f) for g in (np.cos, np.sin))
    sin_turned = np.concatenate([-sin[:half], sin[half:]])
    turn = np.zeros((ROPE, ROPE), f)
    for n in range(half):
        turn[n + half, n] = -1
        turn[n, n + half] = 1
    eye = np.zeros((P, T), f)
    mask = np.zeros((P, len(HG_LEVELS) - 1, T), np.int32)
    for t0, n in ((0, P), (P, P), (SEQ, NSAMP)):
        a, b = i[:n], j[:, :n]
        eye[:n, t0:t0 + n] = a == b
        for q, L in enumerate(HG_LEVELS[:-1]):
            mask[:n, q, t0:t0 + n] = (a // L == b // L) & (a % L < L // 2) & (b % L >= L // 2)
    later = np.where(j > i, f(-BIG), f(0)).astype(f)
    own = np.full((P, NB // 2, NSAMP), -BIG, f)
    for b in range(NB):
        for h in range(MH):
            for t in range(TS):
                own[(b % 2) * NSAMP + h * TS + t, b // 2, b * TS:b * TS + t + 1] = 0
    iota = np.tile(np.arange(8, dtype=f), (P, 1))
    slot = np.tile(np.arange(CAP, dtype=f), (P, 1))
    first_slot = np.tile(np.arange(NEXP, dtype=f) * CAP, (P, 1))
    return dict(row_select=row_select, eps=np.full((P, 1), EPS, f), ident=np.eye(P, dtype=f), ones=np.ones((P, P), f), causal=causal, selhead=selhead, selpair=selpair,
                keep=keep, ownb=ownb, cos=cos, sin=sin, sin_turned=sin_turned, turn=turn, eye=eye, mask=mask, later=later, own=own, iota=iota, slot=slot,
                first_slot=first_slot)


OUTS = {"o_y": (P, KD, T), "o_conv": (DEPTH, P, 10, NREQ, 3), "o_ssm": (DEPTH, P, 4, NREQ, NST),
        "o_hgrn": (DEPTH, 4, P, NREQ, P), "o_ckv": (DEPTH, P, 2, T), "o_krope": (DEPTH, ROPE, T),
        "o_lru": (DEPTH, P, 4, NREQ)}


SCRATCH = {"rows": ((NEXP * CAP, D), F32)}


def lay_out(w):
    A = {k: np.asarray(v) for k, v in w.items()}
    Lr = DEPTH
    fm = lambda a: np.moveaxis(a.reshape(*a.shape[:-1], a.shape[-1] // P, P), (-1, -2), (0, 1))
    d = {}
    d["x"] = fm(np.concatenate([A["x_prompt"].reshape(SEQ, D), A["x_sample"].reshape(NSAMP, D)]))
    d["c"] = fm(np.concatenate([A["c_prompt"], A["c_sample"]]))
    d["fin"] = A["final_norm_g"].reshape(KD, P).T
    d["table"] = A["page_table"].reshape(1, NB * NPAGE)
    rows = lambda a: a.reshape(Lr, -1, P).transpose(0, 2, 1)
    first = np.zeros((Lr, P, 1), np.float32)
    first[1:] = 1
    taps = np.concatenate([A["ssd_conv_w"], A["lru_conv_w"]], axis=2).reshape(Lr, 4, 10, P).transpose(0, 3, 2, 1).reshape(Lr, P, 40)
    head = np.zeros((Lr, P, 2), np.float32)
    head[:, :NH, 0] = A["ssd_dt_bias"]
    head[:, :NH, 1] = A["ssd_a_log"]
    hg = rows(A["hg_lb_raw"])
    hg0, hg1 = np.stack([hg[0]] * Lr), np.stack([hg[1]] * Lr)
    dsk = np.broadcast_to(A["ssd_d"].reshape(Lr, 4, 2, 1), (Lr, 4, 2, 64)).reshape(Lr, 4, P).transpose(0, 2, 1)
    d["cols"] = np.concatenate([
        rows(A["norm1_g"]), rows(A["norm2_g"]), rows(A["b_mod"]), taps,
        rows(np.concatenate([A["ssd_conv_b"], A["lru_conv_b"]], axis=1)), rows(A["ssd_norm_g"]), hg0, hg1, first,
        rows(A["hg_norm_g"]), rows(A["mla_q_norm_g"]), rows(A["mla_kv_norm_g"]), rows(A["lru_b_r"]), rows(A["lru_b_i"]),
        rows(A["lru_a"]), dsk, head], axis=2)
    panels = lambda a, n: a.reshape(Lr, a.shape[1] // P, P, a.shape[2] // n, n).transpose(0, 3, 2, 1, 4)
    d["w_mod"] = A["w_mod"].reshape(Lr, KD, P, 3, 2048).transpose(0, 3, 1, 2, 4)
    W = A["w_in"]
    d["w_in"] = panels(np.concatenate([W[:, :, 0:1280], W[:, :, 1288:3848], W[:, :, 3880:]], axis=2), P)
    d["w_small"] = np.concatenate([W[:, :, 3848:3880], W[:, :, 1280:1288]], axis=2).reshape(Lr, KD, P, 40).transpose(0, 2, 1, 3)
    st = np.concatenate([A["state_ssm_conv"], A["state_lru_conv"]], axis=3)
    d["conv_state"] = st.reshape(Lr, NB, 3, 10, P).transpose(0, 4, 3, 1, 2)
    S = A["state_ssm"]
    d["ssm_T"] = S.reshape(Lr, NB, 2, 4, HD, NST).transpose(0, 2, 5, 1, 3, 4).reshape(Lr, P, NB, 256)
    d["ssm_P"] = S.reshape(Lr, NB, 4, 2, HD, NST).transpose(0, 3, 4, 2, 1, 5).reshape(Lr, P, 4, NB, NST)
    d["hgrn"] = A["state_hgrn"].transpose(0, 2, 3, 1, 4)
    d["lru_state"] = A["state_lru"].reshape(Lr, NB, 4, P).transpose(0, 3, 2, 1)
    C, R = A["cache_kv_latent"], A["cache_k_rope"]
    n_pool = C.shape[1]
    keys = np.zeros((Lr, n_pool, P, 384), np.float32)
    keys[..., 0:256] = C.reshape(Lr, n_pool, P, 2, P).transpose(0, 1, 4, 3, 2).reshape(Lr, n_pool, P, 256)
    keys[:, :, 0:ROPE, 256:384] = R.transpose(0, 1, 3, 2)
    d["pages_k"], d["pages_v"] = keys, C
    uq, half = A["mla_w_uq"].reshape(Lr, 2, P, MH, NOPE + ROPE), ROPE // 2
    uq = np.concatenate([uq, uq[..., NOPE + half:], uq[..., NOPE:NOPE + half]], axis=4)
    d["w_uq"] = uq.reshape(Lr, 2, P, MH * P).transpose(0, 2, 1, 3)
    U = A["mla_w_ukv"].reshape(Lr, 256, MH, 128)
    d["w_uk"] = U[..., :64].transpose(0, 3, 2, 1)
    d["w_uv"] = U[..., 64:].reshape(Lr, 2, P, MH, 64).transpose(0, 2, 1, 3, 4)
    lw = np.zeros((Lr, P, 2, 4, P), np.float32)
    for n, name in enumerate(("lru_w_r", "lru_w_i")):
        B = A[name].reshape(Lr, 4, 2, 64, 64)
        for q in range(2):
            lw[:, 64 * q:64 * q + 64, n, :, 64 * q:64 * q + 64] = B[:, :, q].transpose(0, 2, 1, 3)
    d["lru_w"] = lw
    d["w_branch"] = A["w_branch"].reshape(Lr, 4, 4, P, 2, 512).transpose(0, 1, 4, 3, 2, 5).reshape(Lr, 8, P, 2048)
    d["w_out"] = A["w_out"].reshape(Lr, KD, P, 4, 256).transpose(0, 3, 2, 1, 4).reshape(Lr, 4, P, 2048)
    d["w_router"] = np.concatenate([A["moe_w_grp"], A["moe_w_rt"]], axis=2).reshape(Lr, KD, P, 36).transpose(0, 2, 1, 3)
    d["b_router"] = np.concatenate([A["moe_b_grp"], A["moe_b_rt"]], axis=1).reshape(Lr, 1, 36)
    GU = np.concatenate([A["moe_w_gate"], A["moe_w_up"]], axis=3)
    d["w_gate_up"] = GU.reshape(Lr, NEXP, KD, P, 2 * HID).transpose(0, 1, 3, 2, 4)
    d["w_down"] = A["moe_w_down"].reshape(Lr, NEXP, 2, P, D).transpose(0, 1, 3, 2, 4)
    for k, v in constants().items():
        d["k_" + k] = v
    return {k: np.ascontiguousarray(v) for k, v in d.items()}, n_pool


def outputs(r):
    y = r["o_y"].transpose(2, 1, 0).reshape(T, D)
    conv = r["o_conv"].transpose(0, 3, 4, 2, 1).reshape(DEPTH, NREQ, 3, 1280)
    ssm = r["o_ssm"].reshape(DEPTH, 2, HD, 4, NREQ, NST).transpose(0, 4, 3, 1, 2, 5).reshape(DEPTH, NREQ, NH, HD, NST)
    hgrn = r["o_hgrn"].transpose(0, 3, 1, 2, 4)
    ckv = r["o_ckv"].transpose(0, 3, 2, 1).reshape(DEPTH, T, 256)
    kr = r["o_krope"].transpose(0, 2, 1)
    lru = r["o_lru"].transpose(0, 3, 2, 1).reshape(DEPTH, NREQ, 512)
    res = [y[:SEQ].reshape(1, SEQ, D), y[SEQ:].reshape(NB, TS, D)]
    for sl, tok, shape in ((slice(0, 1), slice(0, SEQ), (DEPTH, 1, SEQ, -1)), (slice(1, NREQ), slice(SEQ, T), (DEPTH, NB, TS, -1))):
        res += [ckv[:, tok].reshape(shape), kr[:, tok].reshape(shape), ssm[:, sl], conv[:, sl, :, :768], hgrn[:, sl],
                lru[:, sl], conv[:, sl, :, 768:]]
    return tuple(np.ascontiguousarray(a) for a in res)


def kernel(**inputs):
    import concourse.bacc as bacc
    from concourse.bass_utils import run_bass_kernel_spmd

    nc = bacc.Bacc("TRN2", target_bir_lowering=False, num_devices=1)
    arrays, n_pool = lay_out(inputs)
    d = {n: nc.dram_tensor(n, a.shape, mybir.dt.from_np(a.dtype), kind="ExternalInput").ap() for n, a in arrays.items()}
    for n, shape in OUTS.items():
        d[n] = nc.dram_tensor(n, shape, F32, kind="ExternalOutput").ap()
    for n, (shape, dt) in SCRATCH.items():
        d[n] = nc.dram_tensor(n, shape, dt, kind="Internal").ap()
    build(nc, d, n_pool)
    r = run_bass_kernel_spmd(nc, [arrays], core_ids=[0])
    return outputs(r.results[0])
```
